# Optimizing a Trainium2 kernel written in Bass

```python
import jax, jax.numpy as jnp
from jax import lax
import numpy as np

D_MODEL = 1024
BATCH = 1
SEQ = 256
DEPTH = 1
DEC_BATCH = 8
DEC_SEQ = 1
PAST_LEN = 1024
PAGE_SIZE = 128

POOL_WINDOWS = (2, 4, 8, 16)
POOL_GROUPS = len(POOL_WINDOWS)
POOL_GDIM = D_MODEL // 16
POOL_W = POOL_GROUPS * POOL_GDIM
POOL_BUF = max(POOL_WINDOWS) - 1
HEAD_DIM = 64
ATT_HEADS = D_MODEL // 128
ATT_W = ATT_HEADS * HEAD_DIM
MOBA_BLOCK = 256
MOBA_TOPK = 3
MOBA_QCHUNK = 32
DN_HEADS = D_MODEL // 256
DN_DK = 64
DN_DV = 64
DN_W = DN_HEADS * DN_DV
DN_CHUNK = 64
CONV_W = 4
MIX_W = POOL_W + ATT_W + DN_W
D_FF = -(-8 * D_MODEL // (3 * 256)) * 256
N_MOD = 6
IN_SPLITS = (POOL_W, ATT_W, ATT_W, ATT_W, DN_W, DN_W, DN_W, DN_W, DN_HEADS, DN_HEADS)
IN_COLS = sum(IN_SPLITS)
NORM_EPS = 1e-6

kernel_name = 'hybrid_pool_moba_gdn_decode_step'

def rms_norm(x, w):
    xf = x.astype(jnp.float32)
    y = xf * lax.rsqrt(jnp.mean(xf * xf, axis=-1, keepdims=True) + NORM_EPS)
    return (y * w.astype(jnp.float32)).astype(x.dtype)

def l2_norm(x):
    return x * lax.rsqrt(jnp.sum(x * x, axis=-1, keepdims=True) + NORM_EPS)

def pool_mixer(u, buf, pos0, pool_w, pool_scale):
    B, L, _ = u.shape
    ext = jnp.concatenate([buf.astype(u.dtype), u], axis=1)
    cs = jnp.pad(jnp.cumsum(ext.astype(jnp.float32), axis=1), ((0, 0), (1, 0), (0, 0)))
    pos = pos0 + jnp.arange(L)
    top = cs[:, POOL_BUF + 1:POOL_BUF + 1 + L]
    uf = u.astype(jnp.float32)
    diffs = []
    for g, w in enumerate(POOL_WINDOWS):
        sl = slice(g * POOL_GDIM, (g + 1) * POOL_GDIM)
        wsum = top[..., sl] - cs[:, POOL_BUF + 1 - w:POOL_BUF + 1 - w + L, sl]
        cnt = jnp.minimum(w, pos + 1).astype(jnp.float32)[None, :, None]
        diffs.append(wsum / cnt - uf[..., sl])
    d = jnp.stack(diffs, axis=2)
    y = jnp.einsum('blgc,gcd->blgd', d, pool_w.astype(jnp.float32)).reshape(B, L, POOL_W)
    y = y * pool_scale.astype(jnp.float32)
    return y.astype(u.dtype), ext[:, ext.shape[1] - POOL_BUF:]

def moba_attention(q, k_all, v_all, q_start):
    B, Lq, H, hd = q.shape
    T = k_all.shape[1]
    nbk = -(-T // MOBA_BLOCK)
    padw = ((0, 0), (0, nbk * MOBA_BLOCK - T), (0, 0), (0, 0))
    kb = jnp.pad(k_all, padw).reshape(B, nbk, MOBA_BLOCK, H, hd).transpose(0, 3, 1, 2, 4)
    vb = jnp.pad(v_all, padw).reshape(B, nbk, MOBA_BLOCK, H, hd).transpose(0, 3, 1, 2, 4)
    kmean = jnp.mean(kb.astype(jnp.float32), axis=3)
    qh = q.transpose(0, 2, 1, 3)
    qpos = q_start + jnp.arange(Lq)
    qblk = qpos // MOBA_BLOCK
    gate = jnp.einsum('bhqd,bhnd->bhqn', qh.astype(jnp.float32), kmean)
    is_past = jnp.arange(nbk)[None, :] < qblk[:, None]
    gate = jnp.where(is_past, gate, -jnp.inf)
    n_top = min(MOBA_TOPK, nbk)
    _, sel = lax.top_k(gate, n_top)
    sel_ok = sel < qblk[:, None]
    own = jnp.broadcast_to(qblk[:, None], (B, H, Lq, 1)).astype(sel.dtype)
    blk_idx = jnp.concatenate([sel, own], axis=-1)
    blk_ok = jnp.concatenate([sel_ok, jnp.ones((B, H, Lq, 1), bool)], axis=-1)
    nsel = n_top + 1
    qc = MOBA_QCHUNK if Lq % MOBA_QCHUNK == 0 else Lq
    nc = Lq // qc

    def chunks(a):
        return jnp.moveaxis(a.reshape(B, H, nc, qc, *a.shape[3:]), 2, 0)

    bi = jnp.arange(B)[:, None, None, None]
    hi = jnp.arange(H)[None, :, None, None]
    offs = jnp.arange(MOBA_BLOCK)
    scale = hd ** -0.5

    def attend(args):
        q_c, idx_c, ok_c, pos_c = args
        kg = kb[bi, hi, idx_c]
        vg = vb[bi, hi, idx_c]
        kpos = idx_c[..., None] * MOBA_BLOCK + offs
        mask = ok_c[..., None] & (kpos <= pos_c[:, None, None])
        s = jnp.einsum('bhqd,bhqnkd->bhqnk', q_c, kg, preferred_element_type=jnp.float32) * scale
        s = jnp.where(mask, s, -jnp.inf).reshape(B, H, qc, nsel * MOBA_BLOCK)
        p = jax.nn.softmax(s, axis=-1).reshape(B, H, qc, nsel, MOBA_BLOCK)
        o = jnp.einsum('bhqnk,bhqnkd->bhqd', p, vg.astype(jnp.float32))
        return o.astype(q.dtype)

    o = lax.map(attend, (chunks(qh), chunks(blk_idx), chunks(blk_ok), qpos.reshape(nc, qc)))
    o = jnp.moveaxis(o, 0, 2).reshape(B, H, Lq, hd).transpose(0, 2, 1, 3)
    return o

def short_conv(x, buf, w):
    ext = jnp.concatenate([buf.astype(x.dtype), x], axis=1)
    y = lax.conv_general_dilated(ext, w.astype(x.dtype)[:, None, :], window_strides=(1,),
                                 padding='VALID', dimension_numbers=('NWC', 'WIO', 'NWC'),
                                 feature_group_count=x.shape[-1])
    return jax.nn.silu(y), ext[:, ext.shape[1] - (CONV_W - 1):]

def gated_delta_rule(q, k, v, g, beta, S0):
    B, L, H, dk = q.shape
    dv = v.shape[-1]
    C = DN_CHUNK
    pad = (-L) % C
    N = (L + pad) // C

    def prep(a):
        a = jnp.pad(a, ((0, 0), (0, pad)) + ((0, 0),) * (a.ndim - 2))
        a = jnp.moveaxis(a, 2, 1)
        return a.reshape(B, H, N, C, *a.shape[3:])

    q, k, v, g, beta = prep(q), prep(k), prep(v), prep(g), prep(beta)
    gcum = jnp.cumsum(g, axis=-1)
    incl = jnp.tril(jnp.ones((C, C), bool))
    strict = jnp.tril(jnp.ones((C, C), bool), -1)
    diff = gcum[..., :, None] - gcum[..., None, :]
    decay = jnp.where(incl, jnp.exp(jnp.where(incl, diff, 0.0)), 0.0)
    kbeta = k * beta[..., None]
    M = jnp.where(strict, jnp.einsum('bhnid,bhnjd->bhnij', kbeta, k) * decay, 0.0)
    A = M + jnp.eye(C, dtype=M.dtype)
    rhs = jnp.concatenate([v * beta[..., None], kbeta * jnp.exp(gcum)[..., None]], axis=-1)
    sol = lax.linalg.triangular_solve(A, rhs, left_side=True, lower=True, unit_diagonal=True)
    u_base, kcum = sol[..., :dv], sol[..., dv:]
    attn = jnp.einsum('bhnid,bhnjd->bhnij', q, k) * decay
    q_dec = q * jnp.exp(gcum)[..., None]
    k_dec = k * jnp.exp(gcum[..., -1:] - gcum)[..., None]
    g_tot = jnp.exp(gcum[..., -1])
    xs = tuple(jnp.moveaxis(a, 2, 0) for a in (u_base, kcum, attn, q_dec, k_dec, g_tot))

    def step(S, xc):
        u_c, kc_c, at_c, qd_c, kd_c, gt_c = xc
        v_new = u_c - jnp.einsum('bhck,bhkv->bhcv', kc_c, S)
        o = jnp.einsum('bhck,bhkv->bhcv', qd_c, S) + jnp.einsum('bhij,bhjv->bhiv', at_c, v_new)
        S = S * gt_c[..., None, None] + jnp.einsum('bhck,bhcv->bhkv', kd_c, v_new)
        return S, o

    S, o = lax.scan(step, S0, xs)
    o = jnp.moveaxis(o, 0, 2).reshape(B, H, N * C, dv)[:, :, :L].transpose(0, 2, 1, 3)
    return o, S

def decoder_layer(x, c, past_k, past_v, pool_buf, conv_buf, S0, lw):
    (norm1_w, ada_w, ada_b, w_in, pool_w, pool_scale, q_norm_w, k_norm_w, conv_w,
     a_log, dt_bias, dn_norm_w, w_out, norm2_w, w_gate, w_up, w_down) = lw
    B, L, _ = x.shape
    dt = x.dtype
    pos0 = past_k.shape[1]
    mod = (jax.nn.silu(c) @ ada_w + ada_b)[:, None, :]
    sh1, sc1, g1, sh2, sc2, g2 = jnp.split(mod, N_MOD, axis=-1)
    h = rms_norm(x, norm1_w) * (1 + sc1) + sh1
    proj = h @ w_in
    u_pool, q_a, k_a, v_a, q_d, k_d, v_d, z, b_raw, a_raw = jnp.split(
        proj, np.cumsum(IN_SPLITS)[:-1], axis=-1)
    y_pool, pool_new = pool_mixer(u_pool, pool_buf, pos0, pool_w, pool_scale)
    q_a = rms_norm(q_a.reshape(B, L, ATT_HEADS, HEAD_DIM), q_norm_w)
    k_a = rms_norm(k_a.reshape(B, L, ATT_HEADS, HEAD_DIM), k_norm_w)
    v_a = v_a.reshape(B, L, ATT_HEADS, HEAD_DIM)
    k_all = jnp.concatenate([past_k.astype(dt), k_a], axis=1)
    v_all = jnp.concatenate([past_v.astype(dt), v_a], axis=1)
    y_att = moba_attention(q_a, k_all, v_all, pos0).reshape(B, L, ATT_W)
    qkv, conv_new = short_conv(jnp.concatenate([q_d, k_d, v_d], axis=-1), conv_buf, conv_w)
    qkv = qkv.astype(jnp.float32)
    q_c = l2_norm(qkv[..., :DN_W].reshape(B, L, DN_HEADS, DN_DK)) * (DN_DK ** -0.5)
    k_c = l2_norm(qkv[..., DN_W:2 * DN_W].reshape(B, L, DN_HEADS, DN_DK))
    v_c = qkv[..., 2 * DN_W:].reshape(B, L, DN_HEADS, DN_DV)
    beta = jax.nn.sigmoid(b_raw.astype(jnp.float32))
    g = -jnp.exp(a_log.astype(jnp.float32)) * jax.nn.softplus(
        a_raw.astype(jnp.float32) + dt_bias.astype(jnp.float32))
    o_c, S_new = gated_delta_rule(q_c, k_c, v_c, g, beta, S0.astype(jnp.float32))
    y_dn = rms_norm(o_c, dn_norm_w) * jax.nn.silu(z.astype(jnp.float32)).reshape(B, L, DN_HEADS, DN_DV)
    y_dn = y_dn.reshape(B, L, DN_W).astype(dt)
    mix = jnp.concatenate([y_pool, y_att, y_dn], axis=-1)
    x = x + g1 * (mix @ w_out)
    h2 = rms_norm(x, norm2_w) * (1 + sc2) + sh2
    x = x + g2 * ((jax.nn.silu(h2 @ w_gate) * (h2 @ w_up)) @ w_down)
    return x, k_a, v_a, pool_new, conv_new, S_new

def setup_inputs(seed: int = 0) -> dict:
    key = jax.random.key(seed)
    ks = jax.random.split(key, 32)
    f32 = jnp.float32

    def nrm(k, shape, s=1.0):
        return jax.random.normal(k, shape, f32) * s

    n_pages = PAST_LEN // PAGE_SIZE
    n_used = DEC_BATCH * n_pages
    n_phys = n_used + n_used // 4
    page_table = jax.random.permutation(ks[0], n_phys)[:n_used].reshape(DEC_BATCH, n_pages).astype(jnp.int32)
    return {
        'x_prompt': nrm(ks[1], (BATCH, SEQ, D_MODEL)),
        'x_sample': nrm(ks[2], (DEC_BATCH, DEC_SEQ, D_MODEL)),
        'cache_k': nrm(ks[3], (DEPTH, n_phys, PAGE_SIZE, ATT_HEADS, HEAD_DIM)),
        'cache_v': nrm(ks[4], (DEPTH, n_phys, PAGE_SIZE, ATT_HEADS, HEAD_DIM)),
        'state_pool': nrm(ks[5], (DEPTH, DEC_BATCH, POOL_BUF, POOL_W)),
        'state_conv': nrm(ks[6], (DEPTH, DEC_BATCH, CONV_W - 1, 3 * DN_W)),
        'state_delta': nrm(ks[7], (DEPTH, DEC_BATCH, DN_HEADS, DN_DK, DN_DV), DN_DK ** -0.5),
        'page_table': page_table,
        'c_prompt': nrm(ks[8], (BATCH, D_MODEL)),
        'c_sample': nrm(ks[9], (DEC_BATCH, D_MODEL)),
        'norm1_w': 1.0 + nrm(ks[10], (DEPTH, D_MODEL), 0.02),
        'ada_w': nrm(ks[11], (DEPTH, D_MODEL, N_MOD * D_MODEL), 0.5 * D_MODEL ** -0.5),
        'ada_b': nrm(ks[12], (DEPTH, N_MOD * D_MODEL), 0.02),
        'w_in': nrm(ks[13], (DEPTH, D_MODEL, IN_COLS), D_MODEL ** -0.5),
        'pool_w': nrm(ks[14], (DEPTH, POOL_GROUPS, POOL_GDIM, POOL_GDIM), POOL_GDIM ** -0.5),
        'pool_scale': 1.0 + nrm(ks[15], (DEPTH, POOL_W), 0.1),
        'q_norm_w': 1.0 + nrm(ks[16], (DEPTH, HEAD_DIM), 0.02),
        'k_norm_w': 1.0 + nrm(ks[17], (DEPTH, HEAD_DIM), 0.02),
        'conv_w': nrm(ks[18], (DEPTH, CONV_W, 3 * DN_W), CONV_W ** -0.5),
        'a_log': jnp.log(jax.random.uniform(ks[19], (DEPTH, DN_HEADS), f32, 1.0, 16.0)),
        'dt_bias': nrm(ks[20], (DEPTH, DN_HEADS), 0.1),
        'dn_norm_w': 1.0 + nrm(ks[21], (DEPTH, DN_DV), 0.02),
        'w_out': nrm(ks[22], (DEPTH, MIX_W, D_MODEL), MIX_W ** -0.5),
        'norm2_w': 1.0 + nrm(ks[23], (DEPTH, D_MODEL), 0.02),
        'w_gate': nrm(ks[24], (DEPTH, D_MODEL, D_FF), D_MODEL ** -0.5),
        'w_up': nrm(ks[25], (DEPTH, D_MODEL, D_FF), D_MODEL ** -0.5),
        'w_down': nrm(ks[26], (DEPTH, D_FF, D_MODEL), D_FF ** -0.5),
    }

def reference(x_prompt, x_sample, cache_k, cache_v, state_pool, state_conv, state_delta, page_table,
              c_prompt, c_sample, norm1_w, ada_w, ada_b, w_in, pool_w, pool_scale, q_norm_w, k_norm_w,
              conv_w, a_log, dt_bias, dn_norm_w, w_out, norm2_w, w_gate, w_up, w_down):
    B = x_prompt.shape[0]
    DB = x_sample.shape[0]
    n_pages = page_table.shape[1]
    dt = x_prompt.dtype
    yp, ys = x_prompt, x_sample
    kp_l, vp_l, ks_l, vs_l = [], [], [], []
    pp_l, ps_l, cp_l, cs_l, sp_l, ss_l = [], [], [], [], [], []
    for l in range(DEPTH):
        lw = (norm1_w[l], ada_w[l], ada_b[l], w_in[l], pool_w[l], pool_scale[l], q_norm_w[l], k_norm_w[l],
              conv_w[l], a_log[l], dt_bias[l], dn_norm_w[l], w_out[l], norm2_w[l], w_gate[l], w_up[l], w_down[l])
        yp, kp, vp, pp, cp, sp = decoder_layer(
            yp, c_prompt,
            jnp.zeros((B, 0, ATT_HEADS, HEAD_DIM), dt), jnp.zeros((B, 0, ATT_HEADS, HEAD_DIM), dt),
            jnp.zeros((B, POOL_BUF, POOL_W), dt), jnp.zeros((B, CONV_W - 1, 3 * DN_W), dt),
            jnp.zeros((B, DN_HEADS, DN_DK, DN_DV), jnp.float32), lw)
        past_k = cache_k[l][page_table].reshape(DB, n_pages * PAGE_SIZE, ATT_HEADS, HEAD_DIM)
        past_v = cache_v[l][page_table].reshape(DB, n_pages * PAGE_SIZE, ATT_HEADS, HEAD_DIM)
        ys, ks_, vs_, ps, cs, ss = decoder_layer(
            ys, c_sample, past_k, past_v, state_pool[l], state_conv[l], state_delta[l], lw)
        kp_l.append(kp); vp_l.append(vp); ks_l.append(ks_); vs_l.append(vs_)
        pp_l.append(pp); ps_l.append(ps); cp_l.append(cp); cs_l.append(cs)
        sp_l.append(sp.astype(state_delta.dtype)); ss_l.append(ss.astype(state_delta.dtype))
    return (yp, ys,
            jnp.stack(kp_l), jnp.stack(vp_l), jnp.stack(ks_l), jnp.stack(vs_l),
            jnp.stack(pp_l), jnp.stack(ps_l), jnp.stack(cp_l), jnp.stack(cs_l),
            jnp.stack(sp_l), jnp.stack(ss_l))


_drawn_inputs = setup_inputs


def setup_inputs(seed=0):
    import zlib

    import numpy as np

    out = dict(_drawn_inputs(seed))
    spreads = {}
    factors = {'cache_k': 5.432,
     'cache_v': 4.584,
     'pool_scale': 4.444,
     'q_norm_w': 8.0,
     'k_norm_w': 2.857,
     'dt_bias': 6.055,
     'dn_norm_w': 8.0,
     'norm2_w': 8.0}
    for name, (base, spread) in spreads.items():
        noise = np.random.default_rng([zlib.crc32(name.encode()), seed]).standard_normal(out[name].shape)
        drawn = base * np.exp(spread * noise) if base else spread * noise
        out[name] = __import__('jax').numpy.asarray(drawn.astype(out[name].dtype))
    for name, factor in factors.items():
        out[name] = (out[name] * factor).astype(out[name].dtype)
    return out
```

```python
from contextlib import ExitStack

import concourse.bass as bass
from concourse import mybir

F32 = mybir.dt.float32
I32 = mybir.dt.int32
ALU = mybir.AluOpType
ACT = mybir.ActivationFunctionType
AX = mybir.AxisListType.X
P = 128
EPS = 1e-6
FAR = 1.0e30
MOBA_BLOCK = 256
TOPK = 3
WINDOWS = (2, 4, 8, 16)
RING = 6
SLOT = 2048


def build(nc, x_prompt, x_sample, cache_k, cache_v, state_pool, state_conv, state_delta, page_table,
          c_prompt, c_sample, norm1_w, ada_w, ada_b, w_in, pool_w, pool_scale, q_norm_w, k_norm_w,
          conv_w, a_log, dt_bias, dn_norm_w, w_out, norm2_w, w_gate, w_up, w_down,
          y_prompt, y_sample, k_prompt, v_prompt, k_sample, v_sample, pool_prompt, pool_sample,
          conv_prompt, conv_sample, delta_prompt, delta_sample):
    _, T, D = x_prompt.shape
    NS = x_sample.shape[0]
    NPHYS, PAGE, H, HD = cache_k.shape[1:]
    NPG = page_table.shape[1]
    POOLW = state_pool.shape[3]
    NBUF = state_pool.shape[2]
    CW3 = state_conv.shape[3]
    NCV = state_conv.shape[2]
    GH, DK, DV = state_delta.shape[2:]
    DFF = w_gate.shape[2]
    NT = T + NS
    NC = 1 + NS
    DC = D // P
    TT = T // P
    AW = H * HD
    AC = AW // P
    PCH = POOLW // P
    GC = GH * DV // P
    QC0, KC0, VC0 = PCH, PCH + AC, PCH + 2 * AC
    CV0 = PCH + 3 * AC
    CVN = CW3 // P
    Z0 = CV0 + CVN
    PJ = Z0 + GC
    FC = DFF // P
    NB = NPG * PAGE // MOBA_BLOCK
    PPB = MOBA_BLOCK // PAGE
    SCALE = float(HD) ** -0.5
    assert T == 2 * P and T <= MOBA_BLOCK and PAGE == P and D == DC * P and HD == DK == DV == 64
    assert PJ * P + 2 * GH == w_in.shape[2] and PJ == FC and NS * NPG * H == 512 and AW == 512

    IW = SLOT // DC
    PGI = SLOT // AW
    HALVES = NPG // PGI
    stream = [("ada", i) for i in range(2 * D // IW)]
    win_order = [1, 2, 3, 4, 5, 6, 0, 7, 8, 9, 10]
    kv = [(b, hf) for b in range(NS) for hf in range(HALVES)]
    kq = list(kv)
    for n, i in enumerate(win_order):
        stream.append(("win", i))
        if n >= 2 and kq:
            stream.append(("k", kq.pop(0)))
            if n >= 5 and kq:
                stream.append(("k", kq.pop(0)))
    stream += [("k", b) for b in kq]
    stream += [("ada", i) for i in range(2 * D // IW, 6 * D // IW)]
    stream += [("v", b) for b in kv]
    stream += [("wout", i) for i in range(D // IW)]
    for i in range(DFF // IW):
        stream += [("gate", i), ("up", i)]
    DKT = [(a, min(a + DC, FC)) for a in range(0, FC, DC)]
    stream += [("down", (i, j)) for i in range(D // IW) for j in range(len(DKT))]
    place = {it: (n % RING, n // RING) for n, it in enumerate(stream)}

    ctx = ExitStack()
    with ctx:
        sb = lambda name, shape, dt=F32: ctx.enter_context(nc.sbuf_tensor(name, shape, dt))
        sems = {}

        def sem(name):
            if name not in sems:
                sems[name] = ctx.enter_context(nc.semaphore(name))
            return sems[name]

        ring = sb("ring", [P, RING, SLOT])
        x_nat = sb("x_nat", [P, TT + 1, D])
        c_nat = x_nat[32:32 + NC, TT, :]
        rows = sb("rows", [P, P])
        R_ADAB, R_N1, R_N2 = 0, 6 * DC, 7 * DC
        R_PS = 8 * DC
        R_CW = R_PS + PCH
        R_Q = R_CW + (NCV + 1) * CVN
        NR = R_Q + 3
        xT = sb("xT", [P, DC, NT])
        hT = sb("hT", [P, DC, NT])
        mixT = sb("mixT", [P, DC, NT])
        proj = sb("proj", [P, PJ, NT])
        hid = proj
        cv = sb("cv", [P, CVN, NT])
        modT = sb("modT", [P, 6 * DC, NC])
        scA = sb("scA", [P, DC, NC])
        cT = sb("cT", [P, DC, 32])
        adaS = sb("adaS", [P, 2, IW])
        constT = sb("constT", [P, 96])
        rbc = sb("rbc", [P, 4, NT])
        ident = sb("ident", [P, P])
        ones = sb("ones", [P, P])
        blk = sb("blk", [P, P])
        i64 = sb("i64", [P, HD])
        triu = sb("triu", [P, P])
        lvl = sb("lvl", [P, 7, P])
        cmask = sb("cmask", [P, 3, P])
        selh = sb("selh", [GH, GC, P])
        selc = sb("selc", [P, NS, 32])
        dm8 = sb("dm8", [P, H])
        vn = sb("vn", [P, TT, GH * DV])
        rcnt = vn
        wba = sb("wba", [P, DC, 2 * GH])
        poolw = sb("poolw", [P, PCH, 64])
        gcol = sb("gcol", [GH, 4])
        nat8 = sb("nat8", [NS, 3, AW])
        stg = sb("stg", [P, 2, AW])
        vnat = sb("vnat", [P, TT, AW])
        qb = sb("qb", [P, 2, AW])
        prod = sb("prod", [P, SLOT])
        s_all = sb("s_all", [P, 512])
        pP = prod[:, :].rearrange("p (a m) -> p a m", m=32)
        sq4 = prod[:, 0:AC * NT].rearrange("p (c t) -> p c t", c=AC)
        w_ab = sb("w_ab", [P, 1024])
        w_a, w_b = w_ab[:, 0:512], w_ab[:, 512:1024]
        eps = sb("eps", [P, 2])
        gate4 = sb("gate4", [P, NS, NB, H])
        cnt4 = sb("cnt4", [P, NS, NB, H])
        cmp1 = sb("cmp1", [P, NS, H])
        sm64 = sb("sm64", [P, 6, NS, H])
        own8 = sb("own8", [NS, 2, 64])
        tokmax = sb("tokmax", [P, 4])
        smpT = sb("smpT", [P, 2, 2, 3 * P])
        sm, pT = smpT[:, 0, :, :], smpT[:, 1, :, :]
        st4 = sb("st4", [P, 2, 8])
        table = sb("table", [1, NS * NPG], I32)
        ab = smpT[0:GH, :, :, :].rearrange("p a b c -> p (a b c)")[:, 0:5 * NT].rearrange("p (a t) -> p a t", a=5)
        gn = sb("gn", [P, TT, 2, GH])
        gs = sb("gs", [P, 8, TT * GH])
        vb = sb("vb", [P, TT, GH * DV])
        kbkd = sb("kbkd", [P, 2, TT, GH * DK])
        kbg, kd = kbkd[:, 0, :, :], kbkd[:, 1, :, :]
        kbT = w_b.rearrange("p (c t) -> p c t", c=GC)
        qdT = sb("qdT", [P, GC, P])
        mats = sb("mats", [P, 4, TT, GH, P])
        DT, MT, Tn, Tt = (mats[:, n, :, :, :] for n in range(4))
        AT = DT
        hflat = hT[:, :, :].rearrange("p c t -> p (c t)")
        BT, P1 = (hflat[:, n * 1024:(n + 1) * 1024].rearrange("p (n h i) -> p n h i", n=TT, h=GH) for n in range(2))
        kcT = sb("kcT", [P, GC, P])
        S1 = sb("S1", [P, GC, DV])
        S2 = sb("S2", [P, GC, DV])
        Ss = x_nat[:, 0, :].rearrange("p (b c v) -> p b c v", b=NS, c=GC)
        Sx = x_nat[:, 1, :].rearrange("p (b c v) -> p b c v", b=NS, c=GC)
        cst = kbkd[0:NS * NCV, :, :, :].rearrange("p a n d -> p (a n d)")[:, 0:CW3]
        cext = sb("cext", [P, CVN, NS * NCV])
        pbuf = mats[0:NS, :, :, :, :].rearrange("p a n h i -> p (a n h i)")[:, 0:NBUF * POOLW]
        pd8 = vb[0:NS, :, :]
        pw1, pw2 = x_nat[:, TT, 0:T], x_nat[:, TT, T:2 * T]
        pdT = sb("pdT", [P, PCH, NT])
        tail, utail = w_ab[0:32, 0:CW3], w_ab[0:32, CW3:CW3 + POOLW]
        ynat = x_nat
        bgs = sb("bgs", [P, 2, GC, NS])
        sv = sb("sv", [P, 3, GC, NS])
        bank = [ctx.enter_context(nc.psum_tensor(f"bank{i}", [P, 512], F32)) for i in range(8)]

        slot_full = [sem(f"slot_full{i}") for i in range(RING)]
        bank_full = [sem(f"bank_full{i}") for i in range(8)]
        bank_free = [sem(f"bank_free{i}") for i in range(8)]
        filled, freed_by, fills, frees = {}, {}, [0] * 8, [0] * 8

        counts, running = {}, [0] * RING
        for it in stream:
            s, _ = place[it]
            running[s] += 16 * (PGI if it[0] in "kv" else 1)
            counts[it] = running[s]

        def full_count(item):
            return counts[item]

        def arrived(eng, item):
            eng.wait_ge(slot_full[place[item][0]], full_count(item))
            return ring[:, place[item][0], :]

        released, singles = {}, {"pe_read": 0, "keys_read": 0}

        def used_up(ins, item, name):
            singles[name] += 1
            ins.then_inc(sem(name), 1)
            released[item] = (sem(name), singles[name])

        def read_by(name, item):
            b, n = filled[name]
            released[item] = (bank_full[b], n)

        def full(eng, name):
            b, n = filled[name]
            eng.wait_ge(bank_full[b], n)
            return bank[b]

        def freed(ins, name):
            ins.then_inc(bank_free[filled[name][0]], 1)

        def frees_at(name):
            return freed_by[name]

        def order(eng, name):
            n = [0]
            s = sem(name)

            def chain(ins):
                n[0] += 1
                ins.then_inc(s, 1)
                eng.wait_ge(s, n[0])
            return chain

        block = ctx.enter_context(nc.Block())

        @block.tensor
        def _(pe):
            def opened(name, b, readers=1):
                if frees[b]:
                    pe.wait_ge(bank_free[b], frees[b])
                fills[b] += 1
                frees[b] += readers
                assert name not in filled, name
                filled[name] = (b, fills[b])
                freed_by[name] = frees[b]
                return bank[b]

            def closed(ins, name):
                ins.then_inc(bank_full[filled[name][0]], 1)

            def mm(out, lhsT, rhs, start=True, stop=True):
                return pe.matmul(out, lhsT, rhs, start=start, stop=stop, skip_group_check=True)

            pe.wait_ge(sem("ident_made"), 1)
            pe.wait_ge(sem("rows_in"), 16 * 11)
            b = opened("rowsT", 2)
            closed(pe.transpose(b[:, 0:NR], rows[0:NR, :], ident[0:NR, 0:NR]), "rowsT")
            pe.wait_ge(sem("c_silu"), 1)
            b = opened("cT", 3)
            for c in range(DC):
                last = pe.transpose(b[:, c * NC:(c + 1) * NC], c_nat[:, c * P:(c + 1) * P], ident[32:32 + NC, 32:32 + NC])
            closed(last, "cT")
            pe.wait_ge(sem("x_in"), 16 * (TT + 1))
            for c in range(DC):
                b = opened(f"xT{c}", 4 + c % 4)
                for r in range(TT):
                    pe.transpose(b[:, r * P:(r + 1) * P], x_nat[:, r, c * P:(c + 1) * P], ident[:, :])
                closed(pe.transpose(b[:, T:NT], x_nat[0:NS, TT, c * P:(c + 1) * P], ident[0:NS, 0:NS]), f"xT{c}")

            def ada(i):
                slot = arrived(pe, ("ada", i)).rearrange("p (k n) -> p k n", k=DC)
                b = opened(f"ada{i}", 2 + i % 2)
                for kk in range(2):
                    for g in range(4):
                        k = 2 * g + kk
                        last = mm(b[32 * g:32 * g + 32, 0:IW], cT[:, k, :], slot[:, k, :], kk == 0, kk == 1)
                closed(last, f"ada{i}")
                read_by(f"ada{i}", ("ada", i))

            def ada_turn(i):
                pe.wait_ge(sem("ada_rows"), i + 1)
                if i % 2 == 0:
                    opened(f"adaT{i // 2}", 4 + i // 2 % 2)
                b = bank[filled[f"adaT{i // 2}"][0]]
                for n in range(2):
                    o = (2 * (i % 2) + n) * P
                    last = pe.transpose(b[:, o:o + P], adaS[:, i % 2, n * P:(n + 1) * P], ident[:, :])
                if i % 2:
                    closed(last, f"adaT{i // 2}")
                else:
                    last.then_inc(sem("ada_turned"), 1)

            pe.wait_ge(sem("cT_made"), 1)
            pe.wait_ge(sem("masks_made"), 1)

            def ada_run(a, z):
                for i in range(a, z):
                    ada(i)
                    if i > a:
                        ada_turn(i - 1)
                ada_turn(z - 1)

            ada_run(0, 2 * D // IW)

            def square_sums(name, ready, src):
                pe.wait_ge(sem(ready), 1)
                b = opened(name, 0)
                for c in range(DC):
                    last = mm(b[:, 0:NT], ones[:, :], src[:, c, :], c == 0, c == DC - 1)
                closed(last, name)

            square_sums("ss1", "sq1", hT)
            pe.wait_ge(sem("h1"), 1)

            def project(item):
                slot = arrived(pe, ("win", item)).rearrange("p (k n) -> p k n", k=DC)
                for n in range(2):
                    j = 2 * item + n
                    b = opened(f"proj{j}", n)
                    for k in range(DC):
                        last = mm(b[:, 0:NT], slot[:, k, n * P:(n + 1) * P], hT[:, k, :], k == 0, k == DC - 1)
                    closed(last, f"proj{j}")
                read_by(f"proj{j}", ("win", item))

            def head_sums(name, ready, src, n=4, base=4):
                pe.wait_ge(sem(ready), 1)
                for c in range(n):
                    b = opened(f"{name}{c}", base + c)
                    closed(mm(b[:, 0:NT], blk[:, :], src(c)), f"{name}{c}")

            def to_rows8(name, ready, c0, b_, n=1):
                pe.wait_ge(sem(ready), n)
                b = opened(name, b_)
                for c in range(AC):
                    last = pe.transpose(b[0:NS, c * P:(c + 1) * P], proj[:, c0 + c, T:NT], ident[:, :])
                closed(last, name)

            def q_spread(b_):
                pe.wait_ge(sem("q_rows8"), 1)
                b = opened(f"qb{b_}", 2 + b_ % 2)
                closed(mm(b[:, :], ident[0:NS, b_:b_ + 1].to_broadcast([NS, P]), nat8[:, 0, :]), f"qb{b_}")

            def kv_rows(name, c0, ready, n):
                pe.wait_ge(sem(ready), n)
                for r in range(TT):
                    b = opened(f"{name}{r}", 4 + r)
                    for c in range(AC):
                        last = pe.transpose(b[:, c * P:(c + 1) * P], proj[:, c0 + c, r * P:(r + 1) * P], ident[:, :])
                    closed(last, f"{name}{r}")

            for n, item in enumerate(win_order):
                project(item)
                if n == 2:
                    head_sums("qss", "q_sq", lambda c: mixT[:, c, :])
                if n == 3:
                    to_rows8("q8", "q_done", QC0, 2)
                if n == 4:
                    head_sums("kss", "k_sq", lambda c: mixT[:, AC + c, :])
                if n >= 4:
                    q_spread(n - 4)
                if n == 5:
                    to_rows8("k8", "k_done", KC0, 4)
                    kv_rows("krow", KC0, "k_done", 1)
                if n == 6:
                    to_rows8("v8", "proj_out", VC0, 6, 12)
                    kv_rows("vrow", VC0, "proj_out", 12)
            pe.wait_ge(sem("wba_in"), 16)
            b = opened("ba", 0)
            for k in range(DC):
                mm(b[0:GH, 0:NT], wba[:, k, 0:GH], hT[:, k, :], k == 0, k == DC - 1)
                last = mm(b[32:32 + GH, 0:NT], wba[:, k, GH:2 * GH], hT[:, k, :], k == 0, k == DC - 1)
            closed(last, "ba")
            q_spread(NS - 1)

            pe.wait_ge(sem("proj_out"), PJ)
            b = opened("utail", 7)
            for c in range(PCH):
                last = pe.transpose(b[0:NBUF + NS, c * P:(c + 1) * P], proj[:, c, T - NBUF:NT], ident[:, :])
            closed(last, "utail")
            for hlf in range(2):
                b = opened(f"ctail{hlf}", 6 + hlf)
                for c in range(3):
                    last = pe.transpose(b[0:NCV + NS, c * P:(c + 1) * P],
                                        proj[:, CV0 + 3 * hlf + c, T - NCV:NT], ident[:, :])
                closed(last, f"ctail{hlf}")
            pe.wait_ge(sem("cst_in"), 16)
            b = opened("cext", 6)
            for c in range(CVN):
                last = pe.transpose(b[:, c * NS * NCV:(c + 1) * NS * NCV], cst[:, c * P:(c + 1) * P],
                                    ident[0:NS * NCV, 0:NS * NCV])
            closed(last, "cext")

            def att_scores(h):
                c, r = h // 2, 64 * (h % 2)
                b = opened(f"S{h}", 4 + h % 2)
                mm(b[:, 0:P], proj[r:r + 64, QC0 + c, 0:P], proj[r:r + 64, KC0 + c, 0:P])
                closed(mm(b[:, P:3 * P], proj[r:r + 64, QC0 + c, P:T], proj[r:r + 64, KC0 + c, 0:T]), f"S{h}")

            def att_turn(h):
                pe.wait_ge(sem("probs"), h + 1)
                b = opened(f"PT{h}", 6)
                for n in range(3):
                    last = pe.transpose(b[:, n * P:(n + 1) * P], sm[:, h % 2, n * P:(n + 1) * P], ident[:, :])
                closed(last, f"PT{h}")

            def att_out(h):
                pe.wait_ge(sem("probsT"), h + 1)
                c, r = h // 2, 64 * (h % 2)
                if h % 2 == 0:
                    opened(f"O{c}", 7)
                b = bank[7]
                mm(b[r:r + 64, 0:T], vnat[:, 0, h * HD:(h + 1) * HD], pT[:, h % 2, 0:2 * P], True, False)
                last = mm(b[r:r + 64, P:T], vnat[:, 1, h * HD:(h + 1) * HD], pT[:, h % 2, 2 * P:3 * P], False, True)
                if h % 2:
                    closed(last, f"O{c}")
                else:
                    last.then_inc(sem("att_even"), 1)

            pe.wait_ge(sem("v_rows"), 2)
            att_scores(0)
            for h in range(H):
                if h + 1 < H:
                    att_scores(h + 1)
                att_turn(h)
                if h >= 1:
                    att_out(h - 1)
            att_out(H - 1)

            pe.wait_ge(sem("pool_rows"), 1)
            b = opened("pdT8", 6)
            for c in range(PCH):
                last = pe.transpose(b[:, c * NS:(c + 1) * NS], pd8[:, 0, c * P:(c + 1) * P], ident[0:NS, 0:NS])
            closed(last, "pdT8")
            pe.wait_ge(sem("pool_diff"), 1)
            pe.wait_ge(sem("poolw_in"), 16 * 2 * PCH)
            for c in range(PCH):
                b = opened(f"pool{c}", 6 + c)
                for g in range(2):
                    r = 64 * g
                    last = mm(b[r:r + 64, 0:NT], poolw[r:r + 64, c, :], pdT[r:r + 64, c, :])
                closed(last, f"pool{c}")

            ada_run(2 * D // IW, 6 * D // IW)

            head_sums("dss", "d_sq", lambda c: sq4[:, c, :])
            pe.wait_ge(sem("ab_done"), 1)
            b = opened("gn", 2)
            for n in range(TT):
                for w in range(2):
                    o = (2 * n + w) * GH
                    last = pe.transpose(b[:, o:o + GH], ab[:, w, n * P:(n + 1) * P], ident[0:GH, 0:GH])
            closed(last, "gn")
            for c in range(GC):
                b = opened(f"bbc{c}", c)
                mm(b[:, 0:NT], selh[:, c, :], ab[:, 0, :])
                closed(mm(b[:, NT:NT + NS], selh[:, c, :], ab[:, 2, T:NT]), f"bbc{c}")
            pe.wait_ge(sem("gn_out"), 1)
            b = opened("gcum", 3)
            for n in range(TT):
                mm(b[:, n * GH:(n + 1) * GH], triu[:, :], gn[:, n, 1, :])
                last = mm(b[:, (TT + n) * GH:(TT + n + 1) * GH], ones[:, :], gn[:, n, 1, :])
            closed(last, "gcum")
            pe.wait_ge(sem("ug"), 1)
            for n in range(TT):
                b = opened(f"gbc{n}", 4 + n, 2 if n else 1)
                closed(mm(b[:, :], ones[:, :], P1[:, n, :, :].rearrange("p h i -> p (h i)")), f"gbc{n}")
            pe.wait_ge(sem("qk_d"), 1)
            for w in range(2):
                b = opened(f"dn_rows{w}", 6 + w)
                for n in range(TT):
                    for c in range(GC):
                        o = (n * GC + c) * P
                        last = pe.transpose(b[:, o:o + P], cv[:, (1 + w) * GC + c, n * P:(n + 1) * P], ident[:, :])
                closed(last, f"dn_rows{w}")
            pe.wait_ge(sem("kbT"), 1)
            for h2 in range(2):
                r = slice(64 * h2, 64 * h2 + 64)
                for w, right in enumerate((kbT, cv)):
                    b = opened(f"kk{w}{h2}", 2 * w + h2)
                    for n in range(TT):
                        for c in range(GC):
                            o = (n * GC + c) * P
                            last = mm(b[:, o:o + P], cv[r, GC + c, n * P:(n + 1) * P], right[r, c, n * P:(n + 1) * P])
                    closed(last, f"kk{w}{h2}")
            for n in range(TT):
                pe.wait_ge(sem("Tt"), n + 1)
                b = opened(f"T0{n}", n)
                for h in range(GH):
                    last = pe.transpose(b[:, h * P:(h + 1) * P], Tt[:, n, h, :], ident[:, :])
                closed(last, f"T0{n}")
            for s in range(1, 7):
                for n in range(TT):
                    pe.wait_ge(sem("BT"), TT * (s - 1) + n + 1)
                    pe.wait_ge(sem("Tn"), TT * (s - 1) + n + 1)
                    b = opened(f"P1{s}{n}", 2 + n)
                    for h in range(GH):
                        last = mm(b[:, h * P:(h + 1) * P], BT[:, n, h, :], Tn[:, n, h, :])
                    closed(last, f"P1{s}{n}")
                for n in range(TT):
                    pe.wait_ge(sem("P1"), TT * (s - 1) + n + 1)
                    pe.wait_ge(sem("Tt"), TT * (s - 1) + n + 1)
                    b = opened(f"Pt{s}{n}", 4 + n)
                    for h in range(GH):
                        last = mm(b[:, h * P:(h + 1) * P], P1[:, n, h, :], Tt[:, n, h, :])
                    closed(last, f"Pt{s}{n}")
                    if s < 6:
                        b = opened(f"Pn{s}{n}", 6 + n)
                        for h in range(GH):
                            last = mm(b[:, h * P:(h + 1) * P], Tt[:, n, h, :], P1[:, n, h, :])
                        closed(last, f"Pn{s}{n}")
            pe.wait_ge(sem("Tt"), TT * 7)
            pe.wait_ge(sem("dn_scaled"), 1)
            for n in range(TT):
                b = opened(f"u{n}", 2 + n)
                for h in range(GH):
                    last = mm(b[:, h * DV:(h + 1) * DV], Tt[:, n, h, :], vb[:, n, h * DV:(h + 1) * DV])
                closed(last, f"u{n}")
            b = opened("kc", 4)
            for h in range(GH):
                c, r = h // 2, 64 * (h % 2)
                last = mm(b[r:r + 64, c * P:(c + 1) * P], kbg[:, 1, h * DK:(h + 1) * DK], Tt[:, 1, h, :])
            closed(last, "kc")

            def state(name, n, b_, ready, cnt):
                pe.wait_ge(sem(ready), cnt)
                b = opened(name, b_)
                for h in range(GH):
                    c, r = h // 2, 64 * (h % 2)
                    last = mm(b[r:r + 64, c * DV:(c + 1) * DV], kd[:, n, h * DK:(h + 1) * DK],
                              vn[:, n, h * DV:(h + 1) * DV])
                closed(last, name)

            state("state1", 0, 5, "vn", 1)
            pe.wait_ge(sem("S1"), 1)
            pe.wait_ge(sem("kcT"), 1)
            for h2 in range(2):
                r = slice(64 * h2, 64 * h2 + 64)
                b = opened(f"kcS{h2}", 6 - 2 * h2)
                for c in range(GC):
                    last = mm(b[:, c * DV:(c + 1) * DV], kcT[r, c, :], S1[r, c, :])
                closed(last, f"kcS{h2}")
            state("state2", 1, 7, "vn", 2)
            pe.wait_ge(sem("qdT"), 1)
            b = opened("oT", 0)
            for h in range(GH):
                c, r = h // 2, 64 * (h % 2)
                mm(b[r:r + 64, c * T:c * T + P], vn[:, 0, h * DV:(h + 1) * DV], AT[:, 0, h, :])
            for h in range(GH):
                c, r = h // 2, 64 * (h % 2)
                mm(b[r:r + 64, c * T + P:(c + 1) * T], vn[:, 1, h * DV:(h + 1) * DV], AT[:, 1, h, :], True, False)
                last = mm(b[r:r + 64, c * T + P:(c + 1) * T], S1[r:r + 64, c, :], qdT[r:r + 64, c, :], False, True)
            closed(last, "oT")

            def state_product(name, b_, src, col):
                b = opened(name, b_)
                for c in range(GC):
                    for h2 in range(2):
                        r = 64 * h2
                        for q in range(NS):
                            last = mm(b[r:r + 64, c * NS + q:c * NS + q + 1], src[r:r + 64, q, c, :],
                                      cv[r:r + 64, col + c, T + q:T + q + 1])
                closed(last, name)

            pe.wait_ge(sem("S_in"), 16 * 4)
            state_product("kS", 1, Ss, GC)
            pe.wait_ge(sem("vdiag"), 1)
            vd = P1[:, :, :, :].rearrange("p n h i -> p (n h i)")
            for n in range(2):
                b = opened(f"vbc{n}", 2 + n)
                closed(mm(b[:, :], blk[:, :], vd[:, 512 * n:512 * n + 512]), f"vbc{n}")
            pe.wait_ge(sem("Snew"), 1)
            state_product("qS", 4, Ss, 0)
            pe.wait_ge(sem("o_sq"), 1)
            for c in range(GC):
                b = opened(f"oss{c}", 5 + c)
                closed(mm(b[:, 0:NT], blk[:, :], sq4[:, c, :]), f"oss{c}")

            pe.wait_ge(sem("own_diag"), 1)
            b = opened("own", 7)
            closed(mm(b[:, 0:NS * H], ones[0:NS, :], own8[:, 1, :]), "own")
            pe.wait_ge(sem("k_scores"), 1)
            b = opened("gsum", 0)
            closed(mm(b[:, :], ones[:, :], s_all[:, :]), "gsum")
            b = opened("sT", 1)
            for n in range(4):
                last = pe.transpose(b[:, n * P:(n + 1) * P], s_all[:, n * P:(n + 1) * P], ident[:, :])
            closed(last, "sT")
            pe.wait_ge(sem("max_diag"), 1)
            b = opened("pmax", 2)
            closed(mm(b[:, :], ones[:, :], w_a[:, :]), "pmax")
            pe.wait_ge(sem("exps"), 1)
            b = opened("den", 3)
            closed(mm(b[:, :], ones[:, :], w_b[:, :]), "den")
            pe.wait_ge(sem("p_ready"), 1)

            def fold(q):
                pe.wait_ge(sem("pv_masked"), q + 1)
                if q == 0:
                    opened("y8", 6)
                g = 32 * (q % 4)
                last = mm(bank[6][g:g + 32, :], selc[:, q, :], stg[:, q % 2, :], q < 4, q >= 4)
                if q < NS - 1:
                    last.then_inc(sem("folded"), 1)
                return last

            for q in range(NS):
                b = opened(f"pv{q}", 4 + q % 2)
                for hf in range(HALVES):
                    slot = arrived(pe, ("v", (q, hf))).rearrange("p (k n) -> p k n", k=PGI)
                    for k in range(PGI):
                        last = mm(b[32 * k:32 * k + 32, :], pP[:, q * NPG + hf * PGI + k, :], slot[:, k, :],
                                  hf == 0, hf == HALVES - 1)
                    if hf < HALVES - 1:
                        used_up(last, ("v", (q, hf)), "pe_read")
                closed(last, f"pv{q}")
                read_by(f"pv{q}", ("v", (q, HALVES - 1)))
                if q:
                    fold(q - 1)
            closed(fold(NS - 1), "y8")
            pe.wait_ge(sem("y8_out"), 1)
            b = opened("yT8", 7)
            for c in range(AC):
                last = pe.transpose(b[:, c * P:(c + 1) * P], w_a[:, c * P:(c + 1) * P], ident[:, :])
            closed(last, "yT8")

            pe.wait_ge(sem("mix"), 1)
            for i in range(D // IW):
                slot = arrived(pe, ("wout", i)).rearrange("p (k n) -> p k n", k=DC)
                for n in range(2):
                    j = 2 * i + n
                    b = opened(f"out{j}", n)
                    for k in range(DC):
                        last = mm(b[:, 0:NT], slot[:, k, n * P:(n + 1) * P], mixT[:, k, :], k == 0, k == DC - 1)
                    closed(last, f"out{j}")
                read_by(f"out{j}", ("wout", i))
            square_sums("ss2", "sq2", hT)
            pe.wait_ge(sem("h2"), 1)

            for i in range(DFF // IW):
                for w, kind in enumerate(("gate", "up")):
                    slot = arrived(pe, (kind, i)).rearrange("p (k n) -> p k n", k=DC)
                    for n in range(2):
                        name = f"{kind}{2 * i + n}"
                        b = opened(name, 2 * w + n)
                        for k in range(DC):
                            last = mm(b[:, 0:NT], slot[:, k, n * P:(n + 1) * P], hT[:, k, :], k == 0, k == DC - 1)
                        closed(last, name)
                    read_by(name, (kind, i))
            pe.wait_ge(sem("hidden"), FC)
            for i in range(D // IW):
                for n in range(2):
                    opened(f"down{2 * i + n}", 4 + 2 * (i % 2) + n)
                for m, (k0, k1) in enumerate(DKT):
                    slot = arrived(pe, ("down", (i, m))).rearrange("p (k n) -> p k n", k=DC)
                    for n in range(2):
                        for k in range(k0, k1):
                            last = mm(bank[4 + 2 * (i % 2) + n][:, 0:NT], slot[:, k - k0, n * P:(n + 1) * P],
                                      hid[:, k, :], k == 0, k == FC - 1)
                        if m == len(DKT) - 1:
                            closed(last, f"down{2 * i + n}")
                    if m < len(DKT) - 1:
                        used_up(last, ("down", (i, m)), "pe_read")
                    else:
                        read_by(f"down{2 * i + 1}", ("down", (i, m)))
            pe.wait_ge(sem("x2"), DC)
            for r in range(TT + 1):
                m = P if r < TT else NS
                for hlf in range(2):
                    b = opened(f"y{r}{hlf}", 2 * (r % 2) + hlf)
                    for c in range(4):
                        last = pe.transpose(b[0:m, c * P:(c + 1) * P], xT[:, 4 * hlf + c, r * P:r * P + m], ident[:, :])
                    closed(last, f"y{r}{hlf}")

        @block.vector
        def _(v):
            step = order(v, "dve_step")

            def tt(out, a, b_, op):
                return v.tensor_tensor(out, a, b_, op)

            def bc(ap, shape):
                return ap.to_broadcast(shape)

            def inc(ins, name):
                ins.then_inc(sem(name), 1)

            step(v.memset(cT[:, :, :], 0.0))
            v.memset(eps[:, 0:1], EPS)
            step(v.memset(eps[:, 1:2], 1.0))
            step(v.memset(st4[:, :, :], 0.0))
            b = full(v, "rowsT")
            step(v.tensor_copy(constT[:, 0:NR], b[:, 0:NR]))
            v.sem_inc(bank_free[2], 1)
            b = full(v, "cT")
            freed(v.tensor_copy(cT[:, :, 0:NC], b[:, 0:DC * NC].rearrange("p (c r) -> p c r", c=DC)), "cT")
            v.wait_ge(bank_free[3], frees_at("cT"))
            v.sem_inc(sem("cT_made"), 1)
            for c in range(0, DC, 2):
                b = full(v, f"xT{c}")
                freed(v.tensor_copy(xT[:, c, :], b[:, 0:NT]), f"xT{c}")
            v.wait_ge(sem("iota_made"), 1)
            for c in range(PCH):
                for g in range(2):
                    r = slice(64 * g, 64 * g + 64)
                    v.tensor_scalar(rcnt[r, c, :], rcnt[r, c, :], float(WINDOWS[2 * c + g]), None, ALU.min)
            step(v.tensor_scalar(eps[:, 0:1], eps[:, 0:1], 1.0, None, ALU.mult))
            v.reciprocal(rcnt[:, :, :], rcnt[:, :, :]).then_inc(sem("rcnt_made"), 1)

            def mod_reduce(j):
                b = full(v, f"adaT{j}")
                seen = b[:, :].rearrange("p (t g r) -> p t r g", t=4, g=4)[:, :, 0:NC, :]
                dst = modT[:, 4 * j:4 * j + 4, :]
                freed(v.tensor_reduce(dst, seen, AX, ALU.add), f"adaT{j}")
                v.wait_ge(bank_free[filled[f"adaT{j}"][0]], frees_at(f"adaT{j}"))
                step(tt(dst, dst, bc(constT[:, 4 * j:4 * j + 4].unsqueeze(2), [P, 4, NC]), ALU.add))

            def modulation(sc, wrow):
                step(v.scalar_tensor_tensor(out=scA[:, :, :], in0=modT[:, sc * DC:(sc + 1) * DC, :], scalar=1.0,
                                            in1=bc(constT[:, wrow:wrow + DC].unsqueeze(2), [P, DC, NC]),
                                            op0=ALU.add, op1=ALU.mult))

            def norm_apply(root, sh, done):
                v.wait_ge(sem(root), 1)
                step(v.reciprocal(rbc[:, 0, :], rbc[:, 0, :]))
                step(tt(hT[:, :, :], xT[:, :, :], bc(rbc[:, 0:1, :], [P, DC, NT]), ALU.mult))
                for c in range(DC):
                    v.tensor_scalar(hT[:, c, 0:T], hT[:, c, 0:T], scA[:, c, 0:1],
                                    modT[:, sh * DC + c, 0:1], ALU.mult, ALU.add)
                step(tt(hT[:, :, T:NT], hT[:, :, T:NT], scA[:, :, 1:NC], ALU.mult))
                inc(tt(hT[:, :, T:NT], hT[:, :, T:NT], modT[:, sh * DC:(sh + 1) * DC, 1:NC], ALU.add), done)

            for j in range(2 * DC // 4):
                mod_reduce(j)
            modulation(1, R_N1)
            norm_apply("root1", 0, "h1")

            def head_norm(root, c0, row, done):
                v.wait_ge(sem(root), 4)
                step(v.reciprocal(rbc[:, :, :], rbc[:, :, :]))
                inc(v.scalar_tensor_tensor(out=proj[:, c0:c0 + AC, :].rearrange("p c t -> p (c t)"),
                                           in0=proj[:, c0:c0 + AC, :].rearrange("p c t -> p (c t)"),
                                           scalar=constT[:, row:row + 1],
                                           in1=rbc[:, :, :].rearrange("p c t -> p (c t)"),
                                           op0=ALU.mult, op1=ALU.mult), done)

            def rows8(name, n, done):
                b = full(v, name)
                freed(v.tensor_copy(nat8[:, n, :], b[0:NS, :]), name)
                v.wait_ge(bank_free[filled[name][0]], frees_at(name))
                v.sem_inc(sem(done), 1)

            def k_item(q, hf):
                slot = arrived(v, ("k", (q, hf)))
                v.wait_ge(sem("qb"), q + 1)
                ins = tt(prod[:, :].rearrange("p (k n) -> p k n", k=PGI), slot.rearrange("p (k n) -> p k n", k=PGI),
                         bc(qb[:, q % 2:q % 2 + 1, :], [P, PGI, AW]), ALU.mult)
                used_up(ins, ("k", (q, hf)), "keys_read")
                v.wait_ge(*released[("k", (q, hf))])
                o = (q * NPG + hf * PGI) * H
                ins = v.tensor_reduce(s_all[:, o:o + PGI * H], prod[:, :].rearrange("p (g d) -> p g d", d=HD), AX, ALU.add)
                if hf == HALVES - 1:
                    ins.then_inc(sem("k_scored"), 1)
                    v.wait_ge(sem("k_scored"), q + 1)
                else:
                    step(ins)

            head_norm("rootq", QC0, R_Q, "q_done")
            rows8("q8", 0, "q_rows8")
            head_norm("rootk", KC0, R_Q + 1, "k_done")
            for q in range(NS):
                for hf in range(HALVES):
                    k_item(q, hf)
                if q == 0:
                    rows8("k8", 1, "k_rows8")
                if q == 1:
                    rows8("v8", 2, "v_rows8")
            v.sem_inc(sem("k_scores"), 1)

            def att_mask(h):
                b = full(v, f"S{h}")
                freed(tt(sm[:, h % 2, :], b[:, 0:3 * P], cmask[:, :, :].rearrange("p a k -> p (a k)"), ALU.add), f"S{h}")
                v.wait_ge(bank_free[filled[f"S{h}"][0]], frees_at(f"S{h}"))
                v.tensor_reduce(st4[:, h % 2, 0:1], sm[:, h % 2, 0:P], AX, ALU.max)
                step(v.tensor_reduce(st4[:, h % 2, 1:2], sm[:, h % 2, P:3 * P], AX, ALU.max))
                inc(v.tensor_scalar(st4[:, h % 2, 2:4], st4[:, h % 2, 0:2], -SCALE, None, ALU.mult), "masked")

            def att_norm(h):
                v.wait_ge(sem("exped"), h + 1)
                step(v.reciprocal(st4[:, h % 2, 6:8], st4[:, h % 2, 4:6]))
                v.tensor_scalar(sm[:, h % 2, 0:P], sm[:, h % 2, 0:P], st4[:, h % 2, 6:7], None, ALU.mult)
                inc(v.tensor_scalar(sm[:, h % 2, P:3 * P], sm[:, h % 2, P:3 * P], st4[:, h % 2, 7:8], None, ALU.mult),
                    "probs")

            def att_take(c):
                b = full(v, f"O{c}")
                freed(v.tensor_copy(mixT[:, PCH + c, 0:T], b[:, 0:T]), f"O{c}")

            b = full(v, "cext")
            freed(v.tensor_copy(cext[:, :, :], b[:, 0:CVN * NS * NCV].rearrange("p (c r) -> p c r", c=CVN)), "cext")
            v.wait_ge(bank_free[filled["cext"][0]], frees_at("cext"))
            att_mask(0)
            for h in range(H):
                if h >= 1:
                    full(v, f"PT{h - 1}")
                if h + 1 < H:
                    att_mask(h + 1)
                att_norm(h)
                if h >= 2 and h % 2 == 0:
                    att_take(h // 2 - 1)
            att_take(H // 2 - 1)

            v.wait_ge(sem("pbuf_in"), 16)
            for g, w in enumerate(WINDOWS):
                last = v.tensor_reduce(pd8[:, 0, 64 * g:64 * g + 64],
                                       pbuf.rearrange("b (t c) -> b c t", t=NBUF)[:, 64 * g:64 * g + 64, NBUF - w + 1:NBUF],
                                       AX, ALU.add)
            inc(last, "pool_rows")
            b = full(v, "pdT8")
            freed(tt(pdT[:, :, T:NT], b[:, 0:PCH * NS].rearrange("p (c q) -> p c q", c=PCH), proj[:, 0:PCH, T:NT], ALU.add), "pdT8")
            v.wait_ge(bank_free[filled["pdT8"][0]], frees_at("pdT8"))
            v.wait_ge(sem("pool_prompt_done"), 1)
            for c in range(PCH):
                last = v.scalar_tensor_tensor(out=pdT[:, c, T:NT], in0=pdT[:, c, T:NT], scalar=rcnt[:, c, T - 1:T],
                                              in1=proj[:, c, T:NT], op0=ALU.mult, op1=ALU.subtract)
            inc(last, "pool_diff")
            for c in range(PCH):
                b = full(v, f"pool{c}")
                freed(v.tensor_scalar(mixT[:, c, :], b[:, 0:NT], constT[:, R_PS + c:R_PS + c + 1], None, ALU.mult),
                      f"pool{c}")

            def cw(i, c):
                return constT[:, R_CW + i * CVN + c:R_CW + i * CVN + c + 1]

            for c in range(CVN):
                last = v.tensor_scalar(cv[:, c, :], proj[:, CV0 + c, :], cw(NCV, c), None, ALU.mult)
            step(last)
            for i in range(NCV):
                back = NCV - i
                for c in range(CVN):
                    v.scalar_tensor_tensor(out=cv[:, c, back:T], in0=proj[:, CV0 + c, 0:T - back], scalar=cw(i, c),
                                           in1=cv[:, c, back:T], op0=ALU.mult, op1=ALU.add)
                    last = v.scalar_tensor_tensor(out=cv[:, c, T:NT], in0=cext[:, c, i:NS * NCV:NCV], scalar=cw(i, c),
                                                  in1=cv[:, c, T:NT], op0=ALU.mult, op1=ALU.add)
                if i < NCV - 1:
                    step(last)
            inc(last, "conv_done")

            b = full(v, "ba")
            v.wait_ge(sem("gcol_in"), 32)
            v.tensor_scalar(ab[:, 0, :], b[0:GH, 0:NT], -1.0, None, ALU.mult)
            freed(v.tensor_scalar(ab[:, 3, :], b[32:32 + GH, 0:NT], gcol[:, 1:2], None, ALU.add), "ba")
            v.wait_ge(bank_free[0], frees_at("ba"))
            step(v.tensor_scalar(ab[:, 1, :], ab[:, 3, :], 0.0, None, ALU.max))
            inc(v.scalar_tensor_tensor(out=ab[:, 4, :], in0=ab[:, 3, :], scalar=0.5, in1=ab[:, 1, :],
                                       op0=ALU.mult, op1=ALU.subtract), "ab_in")
            v.wait_ge(sem("ab_exp"), 1)
            step(v.tensor_scalar(ab[:, 0, :], ab[:, 0, :], 1.0, None, ALU.add))
            step(v.reciprocal(ab[:, 0, :], ab[:, 0, :]))
            step(tt(ab[:, 1, :], ab[:, 1, :], ab[:, 4, :], ALU.add))
            step(v.tensor_scalar(gcol[:, 3:4], gcol[:, 2:3], -1.0, None, ALU.mult))
            inc(v.tensor_scalar(ab[:, 1, :], ab[:, 1, :], gcol[:, 3:4], None, ALU.mult), "ab_g")

            for j in range(2 * DC // 4, 6 * DC // 4):
                mod_reduce(j)

            v.wait_ge(sem("rootd"), 4)
            step(v.reciprocal(rbc[:, :, :], rbc[:, :, :]))
            qk = cv[:, 0:2 * GC, :].rearrange("p c t -> p (c t)")
            step(tt(qk, qk, rbc[:, :, :].rearrange("p c t -> p (c t)"), ALU.mult))
            inc(v.tensor_scalar(cv[:, 0:GC, :], cv[:, 0:GC, :], float(DK) ** -0.5, None, ALU.mult), "qk_d")
            b = full(v, "gn")
            freed(v.tensor_copy(gn[:, :, :, :].rearrange("p n w h -> p (n w h)"), b[:, 0:4 * GH]), "gn")
            v.wait_ge(bank_free[2], frees_at("gn"))
            v.sem_inc(sem("gn_out"), 1)
            v.wait_ge(sem("tails_out"), 64)
            for c in range(GC):
                b = full(v, f"bbc{c}")
                v.tensor_copy(bgs[:, 0, c, :], b[:, T:NT])
                v.tensor_copy(bgs[:, 1, c, :], b[:, NT:NT + NS])
                freed(tt(kbT[:, c, :], cv[:, GC + c, 0:T], b[:, 0:T], ALU.mult), f"bbc{c}")
            v.wait_ge(bank_free[1], frees_at("bbc1"))
            v.sem_inc(sem("kbT"), 1)
            for n in range(TT):
                last = tt(P1[:, n, :, :], bc(triu[:, :].unsqueeze(1), [P, GH, P]),
                          bc(gn[:, n, 1, :].unsqueeze(2), [P, GH, P]), ALU.mult)
            inc(last, "ug")
            b = full(v, "gcum")
            freed(v.tensor_copy(gs[:, 0:2, :].rearrange("p a h -> p (a h)"), b[:, 0:4 * GH]), "gcum")
            v.wait_ge(bank_free[3], frees_at("gcum"))
            inc(tt(gs[:, 3, :], gs[:, 1, :], gs[:, 0, :], ALU.subtract), "gs_in")
            for n in range(TT):
                b = full(v, f"gbc{n}")
                if n:
                    v.wait_ge(bank_free[5], frees_at("gbc1") - 1)
                freed(tt(DT[:, n, :, :], b[:, :].rearrange("p (h i) -> p h i", h=GH),
                         bc(gs[:, 0, n * GH:(n + 1) * GH].unsqueeze(2), [P, GH, P]), ALU.subtract), f"gbc{n}")
            v.wait_ge(bank_free[4], frees_at("gbc0"))
            v.wait_ge(bank_free[5], frees_at("gbc1"))
            inc(v.tensor_scalar(DT[:, :, :, :], DT[:, :, :, :], 0.0, None, ALU.min), "decay_in")
            v.wait_ge(sem("gs_exp"), 1)
            for n in range(TT):
                last = tt(gs[:, 6, n * GH:(n + 1) * GH], gs[:, 2, n * GH:(n + 1) * GH], gn[:, n, 0, :], ALU.mult)
            step(last)
            b = full(v, "dn_rows0")
            rows_v = b[:, :].rearrange("p (n d) -> p n d", d=DK)
            tt(kbg[:, :, :].rearrange("p n (h d) -> p (n h) d", d=DK), rows_v,
               bc(gs[:, 6, :].unsqueeze(2), [P, TT * GH, DK]), ALU.mult)
            freed(tt(kd[:, :, :].rearrange("p n (h d) -> p (n h) d", d=DK), rows_v,
                     bc(gs[:, 3, :].unsqueeze(2), [P, TT * GH, DK]), ALU.mult), "dn_rows0")
            b = full(v, "dn_rows1")
            for n in range(TT):
                last = tt(vb[:, n, :].rearrange("p (h d) -> p h d", d=DV),
                          b[:, n * GH * DV:(n + 1) * GH * DV].rearrange("p (h d) -> p h d", d=DV),
                          bc(gn[:, n, 0, :].unsqueeze(2), [P, GH, DV]), ALU.mult)
            freed(last, "dn_rows1")
            v.wait_ge(bank_free[7], frees_at("dn_rows1"))
            v.sem_inc(sem("dn_scaled"), 1)
            v.wait_ge(sem("decay_exp"), 1)
            for n in range(TT):
                last = tt(DT[:, n, :, :], DT[:, n, :, :], bc(triu[:, :].unsqueeze(1), [P, GH, P]), ALU.mult)
            step(last)
            def halves(m, h2):
                return m[:, :, :, :].rearrange("p n (c w) i -> p n w c i", w=2)[:, :, h2, :, :]

            for h2 in range(2):
                for w, dst in enumerate((MT, AT)):
                    b = full(v, f"kk{w}{h2}")
                    freed(tt(halves(dst, h2), b[:, :].rearrange("p (n c i) -> p n c i", n=TT, c=GC), halves(DT, h2),
                             ALU.mult), f"kk{w}{h2}")
            v.wait_ge(bank_free[3], frees_at("kk11"))

            def level(s, n):
                return tt(BT[:, n, :, :], MT[:, n, :, :], bc(lvl[:, s, :].unsqueeze(1), [P, GH, P]), ALU.mult)

            for n in range(TT):
                step(level(0, n))
                inc(tt(Tt[:, n, :, :], bc(ident[:, :].unsqueeze(1), [P, GH, P]), BT[:, n, :, :], ALU.subtract), "Tt")
                v.wait_ge(sem("Tt"), n + 1)
            for n in range(TT):
                inc(level(1, n), "BT")
            for s in range(1, 7):
                for n in range(TT):
                    b = full(v, f"Pt{s}{n}")
                    if s < 6:
                        inc(level(s + 1, n), "BT")
                    else:
                        v.wait_ge(bank_full[4 + n], filled[f"Pt{s}{n}"][1])
                    bn = full(v, f"Pn{s}{n}") if s < 6 else None
                    freed(tt(Tt[:, n, :, :], Tt[:, n, :, :], b[:, :].rearrange("p (h i) -> p h i", h=GH), ALU.subtract),
                          f"Pt{s}{n}")
                    v.wait_ge(bank_free[4 + n], frees_at(f"Pt{s}{n}"))
                    v.sem_inc(sem("Tt"), 1)
                    if s < 6:
                        freed(tt(Tn[:, n, :, :], Tn[:, n, :, :], bn[:, :].rearrange("p (h i) -> p h i", h=GH),
                                 ALU.subtract), f"Pn{s}{n}")
                        v.wait_ge(bank_free[6 + n], frees_at(f"Pn{s}{n}"))
                        v.sem_inc(sem("Tn"), 1)
            v.wait_ge(sem("qdT"), 1)
            b = full(v, "u0")
            freed(v.tensor_copy(vn[:, 0, :], b[:, 0:GH * DV]), "u0")
            v.wait_ge(bank_free[2], frees_at("u0"))
            v.sem_inc(sem("vn"), 1)
            b = full(v, "u1")
            freed(v.tensor_copy(vn[:, 1, :], b[:, 0:GH * DV]), "u1")
            v.wait_ge(bank_free[3], frees_at("u1"))
            b = full(v, "state1")
            freed(v.tensor_copy(S1[:, :, :], b[:, 0:GC * DV].rearrange("p (c v) -> p c v", c=GC)), "state1")
            v.wait_ge(bank_free[5], frees_at("state1"))
            v.sem_inc(sem("S1"), 1)
            for h2 in range(2):
                b = full(v, f"kcS{h2}")
                own = vn[:, 1, :].rearrange("p (c w d) -> p w c d", w=2, d=DV)[:, h2, :, :]
                freed(tt(own, own, b[:, 0:GC * DV].rearrange("p (c d) -> p c d", c=GC), ALU.subtract), f"kcS{h2}")
            v.wait_ge(bank_free[4], frees_at("kcS1"))
            v.sem_inc(sem("vn"), 1)
            b = full(v, "state2")
            for h in range(GH):
                c, r = h // 2, 64 * (h % 2)
                last = v.scalar_tensor_tensor(out=S2[r:r + 64, c, :], in0=S1[r:r + 64, c, :],
                                              scalar=gs[r:r + 64, 4, GH + h:GH + h + 1],
                                              in1=b[r:r + 64, c * DV:(c + 1) * DV], op0=ALU.mult, op1=ALU.add)
            freed(last, "state2")
            v.wait_ge(bank_free[7], frees_at("state2"))
            v.sem_inc(sem("S2_done"), 1)
            b = full(v, "oT")
            freed(v.tensor_copy(pdT[:, :, 0:T], b[:, :].rearrange("p (c t) -> p c t", c=GC)), "oT")

            b = full(v, "kS")
            kSv = b[:, 0:GC * NS].rearrange("p (c q) -> p c q", c=GC)
            freed(tt(sv[:, 0, :, :], kSv, bgs[:, 1, :, :], ALU.mult), "kS")
            v.wait_ge(bank_free[1], frees_at("kS"))
            step(tt(sv[:, 1, :, :], cv[:, 2 * GC:3 * GC, T:NT], sv[:, 0, :, :], ALU.subtract))
            step(tt(sv[:, 0, :, :], sv[:, 1, :, :], bgs[:, 0, :, :], ALU.mult))
            vd = P1[:, :, :, :].rearrange("p n h i -> p (n h i)").rearrange("p (q c w) -> p q c w", q=NS, c=GC)
            for c in range(GC):
                last = tt(vd[:, :, c, :], bc(i64[:, :].unsqueeze(1), [P, NS, DV]),
                          bc(sv[:, 0, c, :].unsqueeze(2), [P, NS, DV]), ALU.mult)
            inc(last, "vdiag")
            for c in range(GC):
                tt(Ss[:, :, c, :], Ss[:, :, c, :], bc(bgs[:, 1, c, :].unsqueeze(2), [P, NS, DV]), ALU.mult)
            for n in range(2):
                b = full(v, f"vbc{n}")
                hq = NS // 2
                for c in range(GC):
                    last = tt(Sx[:, n * hq:(n + 1) * hq, c, :],
                              b[:, :].rearrange("p (q c w) -> p q c w", q=hq, c=GC)[:, :, c, :],
                              bc(cv[:, GC + c, T + n * hq:T + (n + 1) * hq].unsqueeze(2), [P, hq, DV]), ALU.mult)
                freed(last, f"vbc{n}")
            v.wait_ge(bank_free[3], frees_at("vbc1"))
            inc(tt(x_nat[:, 0, :], x_nat[:, 0, :], x_nat[:, 1, :], ALU.add), "Snew")
            b = full(v, "qS")
            freed(v.tensor_copy(pdT[:, :, T:NT], b[:, 0:GC * NS].rearrange("p (c q) -> p c q", c=GC)), "qS")
            v.wait_ge(bank_free[4], frees_at("qS"))
            v.sem_inc(sem("o_done"), 1)
            v.wait_ge(sem("rooto"), 2)
            step(v.reciprocal(rbc[:, 0:GC, :], rbc[:, 0:GC, :]))
            step(v.scalar_tensor_tensor(out=pdT[:, :, :].rearrange("p c t -> p (c t)"),
                                        in0=pdT[:, :, :].rearrange("p c t -> p (c t)"),
                                        scalar=constT[:, R_Q + 2:R_Q + 3],
                                        in1=rbc[:, 0:GC, :].rearrange("p c t -> p (c t)"), op0=ALU.mult, op1=ALU.mult))
            v.wait_ge(sem("z_silu"), 1)
            step(tt(mixT[:, PCH + AC:DC, :], pdT[:, :, :], proj[:, Z0:Z0 + GC, :], ALU.mult))

            step(tt(prod[0:NS, 0:AW], nat8[:, 0, :], nat8[:, 1, :], ALU.mult))
            step(v.tensor_reduce(own8[:, 0, 0:H], prod[0:NS, 0:AW].rearrange("p (h d) -> p h d", d=HD), AX, ALU.add))
            inc(tt(own8[:, 1, :].rearrange("p (q h) -> p q h", h=H), bc(ident[0:NS, 0:NS].unsqueeze(2), [NS, NS, H]),
                   bc(own8[:, 0, 0:H].unsqueeze(1), [NS, NS, H]), ALU.mult), "own_diag")
            b = full(v, "own")
            freed(v.tensor_copy(sm64[:, 2, :, :].rearrange("p q h -> p (q h)"), b[:, 0:NS * H]), "own")
            b = full(v, "gsum")
            g4 = gate4[:, :, :, :].rearrange("p q k h -> p (q k) h")
            c4 = cnt4[:, :, :, :].rearrange("p q k h -> p (q k) h")
            freed(v.tensor_reduce(g4, b[:, :].rearrange("p (n t h) -> p n h t", t=PPB, h=H), AX, ALU.add), "gsum")
            v.wait_ge(bank_free[0], frees_at("gsum"))
            step(v.memset(cnt4[:, :, :, :], 0.0))
            for n in range(NB):
                for m in range(NB):
                    if m != n:
                        step(tt(cmp1[:, :, :], gate4[:, :, m, :], gate4[:, :, n, :], ALU.is_ge if m < n else ALU.is_gt))
                        step(tt(cnt4[:, :, n, :], cnt4[:, :, n, :], cmp1[:, :, :], ALU.add))
            step(v.tensor_scalar(g4, c4, float(min(TOPK, NB + 1)), None, ALU.is_lt))
            step(v.tensor_scalar(c4, g4, FAR, -FAR, ALU.mult, ALU.add))
            b = full(v, "sT")
            freed(v.tensor_reduce(tokmax[:, :], b[:, :].rearrange("p (n t) -> p n t", n=4), AX, ALU.max), "sT")
            v.wait_ge(bank_free[1], frees_at("sT"))
            v.wait_ge(sem("tails_out"), 64)
            for n in range(4):
                last = v.tensor_scalar(w_a[:, n * P:(n + 1) * P], ident[:, :], tokmax[:, n:n + 1], None, ALU.mult)
            inc(last, "max_diag")
            b = full(v, "pmax")

            def paged(ap):
                return ap.rearrange("p (n t h) -> p n t h", t=PPB, h=H)

            def queried(ap):
                return ap.rearrange("p (q n h) -> p q n h", q=NS, h=H)

            freed(tt(paged(w_b), paged(b[:, :]), bc(c4.unsqueeze(2), [P, NS * NB, PPB, H]), ALU.add), "pmax")
            v.wait_ge(bank_free[2], frees_at("pmax"))
            step(v.tensor_reduce(sm64[:, 0, :, :], queried(w_b).rearrange("p q n h -> p q h n"), AX, ALU.max))
            step(tt(sm64[:, 1, :, :], sm64[:, 0, :, :], sm64[:, 2, :, :], ALU.max))
            tt(sm64[:, 3, :, :], sm64[:, 2, :, :], sm64[:, 1, :, :], ALU.subtract)
            step(tt(queried(w_b), queried(s_all[:, :]), bc(sm64[:, 1, :, :].unsqueeze(2), [P, NS, NPG, H]), ALU.subtract))
            inc(v.tensor_scalar(w_b, w_b, 0.0, None, ALU.min), "shifted")
            v.wait_ge(sem("o_summed"), 2)
            step(v.memset(prod[:, :], 0.0))
            v.wait_ge(sem("exp8"), 1)
            inc(tt(paged(w_b), paged(w_b), bc(g4.unsqueeze(2), [P, NS * NB, PPB, H]), ALU.mult), "exps")
            b = full(v, "den")
            freed(v.tensor_reduce(sm64[:, 4, :, :], queried(b[:, :]).rearrange("p q n h -> p q h n"), AX, ALU.add), "den")
            v.wait_ge(bank_free[3], frees_at("den"))
            step(tt(sm64[:, 4, :, :], sm64[:, 4, :, :], sm64[:, 3, :, :], ALU.add))
            step(v.reciprocal(sm64[:, 4, :, :], sm64[:, 4, :, :]))
            tt(sm64[:, 5, :, :], sm64[:, 3, :, :], sm64[:, 4, :, :], ALU.mult)
            inc(tt(pP.rearrange("p (q n) m -> p q n m", q=NS)[:, :, :, 0:H], queried(w_b),
                   bc(sm64[:, 4, :, :].unsqueeze(2), [P, NS, NPG, H]), ALU.mult), "p_ready")
            for q in range(NS):
                b = full(v, f"pv{q}")
                if q == 0:
                    v.wait_ge(sem("krow_out"), 32)
                if q >= 2:
                    v.wait_ge(sem("folded"), q - 1)
                freed(tt(stg[:, q % 2, :].rearrange("p (h d) -> p h d", d=HD), b[:, :].rearrange("p (h d) -> p h d", d=HD),
                         bc(dm8[:, :].unsqueeze(2), [P, H, HD]), ALU.mult), f"pv{q}")
                v.wait_ge(bank_free[4 + q % 2], frees_at(f"pv{q}"))
                v.sem_inc(sem("pv_masked"), 1)
            b = full(v, "y8")
            freed(v.tensor_copy(w_a, b[:, :]), "y8")
            v.wait_ge(bank_free[6], frees_at("y8"))
            v.sem_inc(sem("y8_out"), 1)
            b = full(v, "yT8")
            for c in range(AC):
                last = v.tensor_reduce(mixT[:, PCH + c, T:NT],
                                       b[:, c * P:(c + 1) * P].rearrange("p (g r) -> p r g", g=4)[:, 0:NS, :], AX, ALU.add)
            freed(last, "yT8")
            v.wait_ge(bank_free[7], frees_at("yT8"))
            own_v = w_b[:, 0:AC * NS].rearrange("p (c q) -> p c q", c=AC)
            for h2 in range(2):
                r = slice(64 * h2, 64 * h2 + 64)
                last = tt(own_v[r, :, :], proj[r, VC0:VC0 + AC, T:NT],
                          sm64[r, 5, :, :].rearrange("p q (c w) -> p w c q", w=2)[:, h2, :, :], ALU.mult)
            step(last)
            inc(tt(mixT[:, PCH:PCH + AC, T:NT], mixT[:, PCH:PCH + AC, T:NT], own_v, ALU.add), "mix")

            def residual(name, j, gate, done):
                b = full(v, name)
                m = gate * DC + j
                v.scalar_tensor_tensor(out=xT[:, j, 0:T], in0=b[:, 0:T], scalar=modT[:, m, 0:1], in1=xT[:, j, 0:T],
                                       op0=ALU.mult, op1=ALU.add)
                freed(tt(sv[:, 0, 0, :], b[:, T:NT], modT[:, m, 1:NC], ALU.mult), name)
                v.wait_ge(bank_free[filled[name][0]], frees_at(name))
                inc(tt(xT[:, j, T:NT], xT[:, j, T:NT], sv[:, 0, 0, :], ALU.add), done)
                v.wait_ge(sem(done), j + 1)

            for j in range(DC):
                residual(f"out{j}", j, 2, "x1")
            modulation(4, R_N2)
            norm_apply("root2", 3, "h2")
            for f in range(FC):
                v.wait_ge(sem("silu"), f + 1)
                b = full(v, f"up{f}")
                freed(tt(hid[:, f, :], rbc[:, f % 4, :], b[:, 0:NT], ALU.mult), f"up{f}")
                v.wait_ge(bank_free[filled[f"up{f}"][0]], frees_at(f"up{f}"))
                v.sem_inc(sem("hidden"), 1)
            for j in range(DC):
                residual(f"down{j}", j, 5, "x2")
            v.wait_ge(sem("states_out"), 64)
            for r in range(TT + 1):
                m = P if r < TT else NS
                for hlf in range(2):
                    b = full(v, f"y{r}{hlf}")
                    freed(v.tensor_copy(ynat[0:m, r, 512 * hlf:512 * hlf + 512], b[0:m, :]), f"y{r}{hlf}")
                    v.wait_ge(bank_free[filled[f"y{r}{hlf}"][0]], frees_at(f"y{r}{hlf}"))
                v.sem_inc(sem("y_rows"), 1)

        @block.scalar
        def _(a):
            step = order(a, "act_step")

            def inc(ins, name):
                ins.then_inc(sem(name), 1)

            a.dma_start(c_nat[0:1, :], c_prompt).then_inc(sem("c_in"), 16)
            a.dma_start(c_nat[1:NC, :], c_sample).then_inc(sem("c_in"), 16)
            for r, src, m in ((R_ADAB, ada_b, 6 * DC), (R_N1, norm1_w, DC), (R_N2, norm2_w, DC), (R_PS, pool_scale, PCH)):
                a.dma_start(rows[r:r + m, :], src.rearrange("o (m p) -> (o m) p", p=P)).then_inc(sem("rows_in"), 16)
            a.dma_start(rows[R_CW:R_Q, :], conv_w[0].rearrange("i (c p) -> (i c) p", p=P)).then_inc(sem("rows_in"), 16)
            for n, src in enumerate((q_norm_w, k_norm_w, dn_norm_w)):
                for w in range(2):
                    a.dma_start(rows[R_Q + n:R_Q + n + 1, 64 * w:64 * w + 64], src).then_inc(sem("rows_in"), 16)
            for r in range(TT):
                a.dma_start(x_nat[:, r, :], x_prompt[0, r * P:(r + 1) * P, :]).then_inc(sem("x_in"), 16)
            a.dma_start(x_nat[0:NS, TT, :], x_sample[:, 0, :]).then_inc(sem("x_in"), 16)
            a.dma_start(gcol[:, 0:1], a_log.rearrange("o h -> h o")).then_inc(sem("gcol_in"), 16)
            a.dma_start(gcol[:, 1:2], dt_bias.rearrange("o h -> h o")).then_inc(sem("gcol_in"), 16)
            a.dma_start(wba[:, :, :], w_in[0].rearrange("(k p) n -> p k n", p=P)[:, :, PJ * P:]).then_inc(sem("wba_in"), 16)
            for g in range(2 * PCH):
                a.dma_start(poolw[64 * (g % 2):64 * (g % 2) + 64, g // 2, :], pool_w[0, g]).then_inc(sem("poolw_in"), 16)
            a.dma_start(cst[:, :], state_conv[0].rearrange("q t c -> (q t) c")).then_inc(sem("cst_in"), 16)
            a.dma_start(pbuf, state_pool[0].rearrange("q t c -> q (t c)")).then_inc(sem("pbuf_in"), 16)

            a.wait_ge(sem("c_in"), 32)
            inc(a.activation(c_nat, c_nat, ACT.Silu), "c_silu")
            for c in range(1, DC, 2):
                b = full(a, f"xT{c}")
                freed(a.activation(xT[:, c, :], b[:, 0:NT], ACT.Copy), f"xT{c}")
            a.wait_ge(bank_free[7], frees_at("xT7"))
            a.wait_ge(bank_free[5], frees_at("xT5"))
            a.wait_ge(bank_free[4], frees_at("xT4"))
            a.wait_ge(bank_free[6], frees_at("xT6"))
            inc(a.activation(hT[:, :, :], xT[:, :, :], ACT.Square), "sq1")

            def ada_rows(i):
                b = full(a, f"ada{i}")
                if i >= 2:
                    if i % 2:
                        full(a, f"adaT{(i - 2) // 2}")
                    else:
                        a.wait_ge(sem("ada_turned"), i // 2)
                freed(a.activation(adaS[:, i % 2, :], b[:, 0:IW], ACT.Copy), f"ada{i}")
                a.wait_ge(bank_free[filled[f"ada{i}"][0]], frees_at(f"ada{i}"))
                a.sem_inc(sem("ada_rows"), 1)

            for i in range(2 * D // IW):
                ada_rows(i)
            a.wait_ge(sem("cT_made"), 1)

            def roots(name, banks, scale, done):
                for c in range(banks):
                    nm = f"{name}{c}" if banks > 1 else name
                    b = full(a, nm)
                    freed(a.activation(rbc[:, c, :], b[:, 0:NT], ACT.Sqrt, bias=eps[:, 0:1], scale=scale), nm)
                    a.wait_ge(bank_free[filled[nm][0]], frees_at(nm))
                    a.sem_inc(sem(done), 1)

            roots("ss1", 1, 1.0 / D, "root1")
            nproj = [0]

            def proj_out(item):
                for n in range(2):
                    j = 2 * item + n
                    b = full(a, f"proj{j}")
                    freed(a.activation(proj[:, j, :], b[:, 0:NT], ACT.Copy), f"proj{j}")
                    a.wait_ge(bank_free[n], frees_at(f"proj{j}"))
                    a.sem_inc(sem("proj_out"), 1)

            def q_copy(q):
                b = full(a, f"qb{q}")
                if q >= 2:
                    a.wait_ge(sem("k_scored"), q - 1)
                freed(a.activation(qb[:, q % 2, :], b[:, :], ACT.Copy), f"qb{q}")
                a.wait_ge(bank_free[2 + q % 2], frees_at(f"qb{q}"))
                a.sem_inc(sem("qb"), 1)

            def take(name, dst, rows_, cols, done):
                b = full(a, name)
                freed(a.activation(dst, b[0:rows_, 0:cols], ACT.Copy), name)
                a.wait_ge(bank_free[filled[name][0]], frees_at(name))
                a.sem_inc(sem(done), 1)

            for n, item in enumerate(win_order):
                proj_out(item)
                if n == 1:
                    inc(a.activation(mixT[:, 0:AC, :], proj[:, QC0:QC0 + AC, :], ACT.Square), "q_sq")
                if n == 2:
                    roots("qss", 4, 1.0 / HD, "rootq")
                if n == 3:
                    inc(a.activation(mixT[:, AC:2 * AC, :], proj[:, KC0:KC0 + AC, :], ACT.Square), "k_sq")
                if n == 4:
                    a.wait_ge(sem("q_done"), 1)
                    roots("kss", 4, 1.0 / HD, "rootk")
                if n >= 4:
                    q_copy(n - 4)
                if n == 5:
                    for r in range(TT):
                        take(f"krow{r}", stg[:, r, :], P, AW, "k_rows")
                if n == 6:
                    for r in range(TT):
                        take(f"vrow{r}", vnat[:, r, :], P, AW, "v_rows")
            q_copy(NS - 1)
            take("utail", utail[0:NBUF + NS, :], NBUF + NS, POOLW, "tails")
            for hlf in range(2):
                take(f"ctail{hlf}", tail[0:NCV + NS, 384 * hlf:384 * hlf + 384], NCV + NS, 384, "tails")

            def att_exp(h):
                a.wait_ge(sem("masked"), h + 1)
                a.activation(sm[:, h % 2, 0:P], sm[:, h % 2, 0:P], ACT.Exp, bias=st4[:, h % 2, 2:3], scale=SCALE,
                             accum_out=st4[:, h % 2, 4:5])
                inc(a.activation(sm[:, h % 2, P:3 * P], sm[:, h % 2, P:3 * P], ACT.Exp, bias=st4[:, h % 2, 3:4],
                                 scale=SCALE, accum_out=st4[:, h % 2, 5:6]), "exped")

            def att_pT(h):
                if h == 2:
                    a.wait_ge(sem("att_even"), 1)
                elif h > 2:
                    if h % 2:
                        full(a, f"O{(h - 2) // 2}")
                    else:
                        a.wait_ge(sem("att_even"), h // 2)
                b = full(a, f"PT{h}")
                freed(a.activation(pT[:, h % 2, :], b[:, 0:3 * P], ACT.Copy), f"PT{h}")
                a.wait_ge(bank_free[6], frees_at(f"PT{h}"))
                a.sem_inc(sem("probsT"), 1)

            att_exp(0)
            for h in range(H):
                if h + 1 < H:
                    att_exp(h + 1)
                att_pT(h)

            a.wait_ge(sem("conv_done"), 1)
            a.activation(proj[:, Z0:Z0 + GC, :], proj[:, Z0:Z0 + GC, :], ACT.Silu).then_inc(sem("z_silu"), 1)
            step(a.activation(cv[:, :, :], cv[:, :, :], ACT.Silu))
            inc(a.activation(sq4, cv[:, 0:2 * GC, :], ACT.Square), "d_sq")
            a.wait_ge(sem("ab_in"), 1)
            a.activation(ab[:, 0, :], ab[:, 0, :], ACT.Exp)
            step(a.activation(ab[:, 4, :], ab[:, 4, :], ACT.Exp, scale=2.0))
            a.activation(gcol[:, 2:3], gcol[:, 0:1], ACT.Exp)
            inc(a.activation(ab[:, 4, :], ab[:, 4, :], ACT.Ln, bias=eps[0:GH, 1:2]), "ab_exp")
            a.wait_ge(sem("ab_g"), 1)
            inc(a.activation(ab[:, 2, :], ab[:, 1, :], ACT.Exp), "ab_done")
            for i in range(2 * D // IW, 6 * D // IW):
                ada_rows(i)
            roots("dss", 4, 1.0, "rootd")
            a.wait_ge(sem("gs_in"), 1)
            a.activation(gs[:, 2, :], gs[:, 0, :], ACT.Exp)
            a.activation(gs[:, 3, :], gs[:, 3, :], ACT.Exp)
            inc(a.activation(gs[:, 4, :], gs[:, 1, :], ACT.Exp), "gs_exp")
            b = full(a, "gbc1")
            freed(a.activation(vn[:, :, :].rearrange("p n d -> p (n d)"), b[:, :], ACT.Exp), "gbc1")
            a.wait_ge(sem("decay_in"), 1)
            step(a.activation(DT[:, :, :, :], DT[:, :, :, :], ACT.Exp))
            a.sem_inc(sem("decay_exp"), 1)
            a.sem_inc(sem("ebc"), 1)
            for n in range(TT):
                b = full(a, f"T0{n}")
                freed(a.activation(Tn[:, n, :, :], b[:, :].rearrange("p (h i) -> p h i", h=GH), ACT.Copy), f"T0{n}")
                a.wait_ge(bank_free[n], frees_at(f"T0{n}"))
                a.sem_inc(sem("Tn"), 1)
            for s in range(1, 7):
                for n in range(TT):
                    if s > 1:
                        full(a, f"Pn{s - 1}{n}")
                    b = full(a, f"P1{s}{n}")
                    freed(a.activation(P1[:, n, :, :], b[:, :].rearrange("p (h i) -> p h i", h=GH), ACT.Copy), f"P1{s}{n}")
                    a.wait_ge(bank_free[2 + n], frees_at(f"P1{s}{n}"))
                    a.sem_inc(sem("P1"), 1)
            b = full(a, "kc")
            freed(a.activation(kcT[:, :, :], b[:, 0:GC * P].rearrange("p (c i) -> p c i", c=GC), ACT.Copy), "kc")
            a.wait_ge(bank_free[4], frees_at("kc"))
            a.sem_inc(sem("kcT"), 1)
            a.wait_ge(sem("o_done"), 1)
            inc(a.activation(sq4[:, 0:GC, :], pdT[:, :, :], ACT.Square), "o_sq")
            for c in range(GC):
                b = full(a, f"oss{c}")
                freed(a.activation(rbc[:, c, :], b[:, 0:NT], ACT.Sqrt, bias=eps[:, 0:1], scale=1.0 / DV), f"oss{c}")
                a.wait_ge(bank_free[5 + c], frees_at(f"oss{c}"))
                a.sem_inc(sem("rooto"), 1)
                a.sem_inc(sem("o_summed"), 1)
            a.wait_ge(sem("shifted"), 1)
            a.activation(sm64[:, 3, :, :], sm64[:, 3, :, :], ACT.Exp, scale=SCALE)
            inc(a.activation(w_b, w_b, ACT.Exp, scale=SCALE), "exp8")
            a.wait_ge(sem("x1"), DC)
            inc(a.activation(hT[:, :, :], xT[:, :, :], ACT.Square), "sq2")
            roots("ss2", 1, 1.0 / D, "root2")
            for f in range(FC):
                b = full(a, f"gate{f}")
                if f >= 4:
                    a.wait_ge(sem("hidden"), f - 3)
                if f == 0:
                    a.wait_ge(sem("h2"), 1)
                freed(a.activation(rbc[:, f % 4, :], b[:, 0:NT], ACT.Silu), f"gate{f}")
                a.wait_ge(bank_free[filled[f"gate{f}"][0]], frees_at(f"gate{f}"))
                a.sem_inc(sem("silu"), 1)

        @block.gpsimd
        def _(g):
            step = order(g, "pool_step")

            def zeros(ap):
                step(g.memset(ap, 0.0))

            def diagonal(ap, base, pattern):
                return g.affine_select(out=ap, in_=ap, compare_op=ALU.not_equal, fill=1.0, base=base, pattern=pattern,
                                       channel_multiplier=1)

            zeros(ident[:, :])
            step(diagonal(ident[:, :], 0, [[-1, P]]))
            g.sem_inc(sem("ident_made"), 1)
            step(g.memset(ones[:, :], 1.0))
            step(g.memset(blk[:, :], 0.0))
            step(g.memset(selc[:, :, :], 0.0))
            step(g.memset(dm8[:, :], 0.0))
            step(g.memset(i64[:, :], 0.0))
            step(g.memset(selh[:, :, :], 0.0))
            step(g.memset(triu[:, :], 1.0))
            step(g.memset(cmask[:, :, :], 0.0))
            zeros(lvl[:, :, :])
            step(g.memset(blk[0:64, 0:64], 1.0))
            step(g.memset(blk[64:P, 64:P], 1.0))
            step(diagonal(i64[:, :], 0, [[-1, HD]]))
            for q in range(4):
                step(diagonal(dm8[:, :], -32 * q, [[-1, H]]))
            step(diagonal(i64[:, :], -64, [[-1, HD]]))
            step(g.affine_select(out=selc[:, :, :], in_=selc[:, :, :], compare_op=ALU.not_equal, fill=1.0, base=0,
                                 pattern=[[1, NS], [-1, 32]], channel_multiplier=0))
            step(g.affine_select(out=selh[:, :, :].rearrange("p c (w d) -> p c w d", w=2),
                                 in_=selh[:, :, :].rearrange("p c (w d) -> p c w d", w=2), compare_op=ALU.not_equal,
                                 fill=1.0, base=0, pattern=[[-2, GC], [-1, 2], [0, DK]], channel_multiplier=1))
            step(g.affine_select(out=triu[:, :], in_=triu[:, :], compare_op=ALU.is_ge, fill=0.0, base=0,
                                 pattern=[[1, P]], channel_multiplier=-1))
            for n in (0, 2):
                step(g.affine_select(out=cmask[:, n, :], in_=cmask[:, n, :], compare_op=ALU.is_ge, fill=-FAR, base=0,
                                     pattern=[[-1, P]], channel_multiplier=1))
            for s in range(7):
                w = 1 << s
                part = lvl[:, s, :].rearrange("p (a b c) -> p a b c", b=2, c=w)[:, :, 1, :]
                step(g.memset(part, 1.0))
                step(g.affine_select(out=part, in_=part, compare_op=ALU.is_ge, fill=0.0, base=0,
                                     pattern=[[-2 * w, P // (2 * w)], [0, w]], channel_multiplier=1))
                step(g.affine_select(out=part, in_=part, compare_op=ALU.is_ge, fill=0.0, base=w - 1,
                                     pattern=[[2 * w, P // (2 * w)], [0, w]], channel_multiplier=-1))
            g.sem_inc(sem("masks_made"), 1)
            cnt_i = prod[:, 0:T].bitcast(I32)
            step(g.iota(cnt_i, pattern=[[1, T]], base=1, channel_multiplier=0))
            for c in range(PCH):
                step(g.tensor_copy(rcnt[:, c, :], cnt_i))
            g.sem_inc(sem("iota_made"), 1)

            n_out = [0]

            def store(dst, src):
                n_out[0] += 1
                g.dma_start(dst, src).then_inc(sem("stored"), 16)

            g.dma_start(pool_sample[0, :, 0:NBUF - 1, :], state_pool[0, :, 1:NBUF, :]).then_inc(sem("stored"), 16)
            g.dma_start(conv_sample[0, :, 0:NCV - 1, :], state_conv[0, :, 1:NCV, :]).then_inc(sem("stored"), 16)
            n_out[0] += 2
            g.wait_ge(sem("k_rows"), 2)
            for r in range(TT):
                g.dma_start(k_prompt[0, 0, r * P:(r + 1) * P].rearrange("t h d -> t (h d)"), stg[:, r, :])\
                 .then_inc(sem("krow_out"), 16)
            g.wait_ge(sem("v_rows"), 2)
            for r in range(TT):
                store(v_prompt[0, 0, r * P:(r + 1) * P].rearrange("t h d -> t (h d)"), vnat[:, r, :])
            g.wait_ge(sem("k_rows8"), 1)
            g.wait_ge(sem("v_rows8"), 1)
            store(k_sample[0, :, 0].rearrange("q h d -> q (h d)"), nat8[:, 1, :])
            store(v_sample[0, :, 0].rearrange("q h d -> q (h d)"), nat8[:, 2, :])
            g.wait_ge(sem("proj_out"), 14)
            g.wait_ge(sem("rcnt_made"), 1)
            g.wait_ge(sem("cT_made"), 1)

            def add_back(dst, src, d):
                step(g.tensor_copy(dst[:, 0:d], src[:, 0:d]))
                step(g.tensor_tensor(dst[:, d:T], src[:, d:T], src[:, 0:T - d], ALU.add))

            for c in range(PCH):
                src, at = proj[:, c, 0:T], 0
                w = 1
                while w < WINDOWS[2 * c + 1]:
                    dst = (pw1, pw2)[at % 2]
                    add_back(dst, src, w)
                    w *= 2
                    at += 1
                    src = dst
                    for gg in range(2):
                        if WINDOWS[2 * c + gg] == w:
                            r = slice(64 * gg, 64 * gg + 64)
                            step(g.tensor_tensor(pdT[r, c, 0:T], src[r, :], rcnt[r, c, :], ALU.mult))
                            step(g.tensor_tensor(pdT[r, c, 0:T], pdT[r, c, 0:T], proj[r, c, 0:T], ALU.subtract))
            g.sem_inc(sem("pool_prompt_done"), 1)
            g.wait_ge(sem("tails"), 3)
            for dst, src in ((pool_prompt[0, 0], utail[0:NBUF, :]), (pool_sample[0, :, NBUF - 1, :], utail[NBUF:NBUF + NS, :]),
                             (conv_prompt[0, 0], tail[0:NCV, :]), (conv_sample[0, :, NCV - 1, :], tail[NCV:NCV + NS, :])):
                g.dma_start(dst, src).then_inc(sem("tails_out"), 16)
            g.wait_ge(sem("ebc"), 1)
            g.wait_ge(sem("qk_d"), 1)
            ebc = vn[:, :, :].rearrange("p n d -> p (n d)")
            for h in range(GH):
                c, r = h // 2, slice(64 * (h % 2), 64 * (h % 2) + 64)
                step(g.tensor_tensor(qdT[r, c, :], cv[r, c, P:T], ebc[r, h * P:(h + 1) * P], ALU.mult))
            g.sem_inc(sem("qdT"), 1)
            g.wait_ge(sem("S2_done"), 1)
            for c in range(GC):
                store(delta_prompt[0, 0].rearrange("(c w) k n -> c (w k) n", w=2)[c], S2[:, c, :])
            g.wait_ge(sem("Snew"), 1)
            for c in range(GC):
                for w in range(2):
                    g.dma_start(delta_sample[0, :, 2 * c + w].rearrange("q k n -> k q n"),
                                Ss[64 * w:64 * w + 64, :, c, :]).then_inc(sem("states_out"), 16)
            for r in range(TT + 1):
                g.wait_ge(sem("y_rows"), r + 1)
                if r < TT:
                    store(y_prompt[0, r * P:(r + 1) * P, :], ynat[:, r, :])
                else:
                    store(y_sample[:, 0, :], ynat[0:NS, TT, :])
            g.wait_ge(sem("stored"), 16 * n_out[0])
            g.wait_ge(sem("krow_out"), 32)
            g.wait_ge(sem("tails_out"), 64)
            g.wait_ge(sem("states_out"), 64)

        @block.sync
        def _(sp):
            sp.dma_start(table[:, :], page_table.rearrange("q n -> (q n)").unsqueeze(0)).then_inc(sem("table_in"), 16)
            cols = {"ada": ada_w, "win": w_in, "wout": w_out, "gate": w_gate, "up": w_up}
            held = [None] * RING
            loaded = False
            for it in stream:
                kind, i = it
                s = place[it][0]
                if held[s] is not None:
                    sp.wait_ge(*released[held[s]])
                held[s] = it
                dst = ring[:, s, :]
                if kind in cols:
                    sp.dma_start(dst.rearrange("p (k n) -> p k n", k=DC),
                                 cols[kind][0].rearrange("(k p) n -> p k n", p=P)[:, :, i * IW:(i + 1) * IW])\
                      .then_inc(slot_full[s], 16)
                elif kind == "down":
                    k0, k1 = DKT[i[1]]
                    sp.dma_start(dst[:, 0:(k1 - k0) * IW].rearrange("p (k n) -> p k n", n=IW),
                                 w_down[0, k0 * P:k1 * P].rearrange("(k p) n -> p k n", p=P)[:, :, i[0] * IW:(i[0] + 1) * IW])\
                      .then_inc(slot_full[s], 16)
                else:
                    if not loaded:
                        sp.wait_ge(sem("table_in"), 16)
                        loaded = True
                    cache = cache_k if kind == "k" else cache_v
                    for k in range(PGI):
                        at = i[0] * NPG + i[1] * PGI + k
                        page = sp.value_load(table[0:1, at:at + 1], min_val=0, max_val=NPHYS - 1)
                        sp.dma_start(dst[:, k * AW:(k + 1) * AW],
                                     cache[0, bass.ds(page, 1)].rearrange("o t h d -> (o t) (h d)"))\
                          .then_inc(slot_full[s], 16)
                if it == ("win", 6):
                    sp.wait_ge(sem("sq1"), 1)
                    for c in range(GC):
                        for w in range(2):
                            sp.dma_start(Ss[64 * w:64 * w + 64, :, c, :],
                                         state_delta[0, :, 2 * c + w].rearrange("q k n -> k q n")).then_inc(sem("S_in"), 16)


_INS = ['x_prompt', 'x_sample', 'cache_k', 'cache_v', 'state_pool', 'state_conv', 'state_delta', 'page_table',
        'c_prompt', 'c_sample', 'norm1_w', 'ada_w', 'ada_b', 'w_in', 'pool_w', 'pool_scale', 'q_norm_w', 'k_norm_w',
        'conv_w', 'a_log', 'dt_bias', 'dn_norm_w', 'w_out', 'norm2_w', 'w_gate', 'w_up', 'w_down']


def kernel(**inputs):
    import numpy as _np
    import concourse.bacc as _bacc
    from concourse import mybir as _mybir
    from concourse.bass_utils import run_bass_kernel_spmd as _run

    xp, xs, ck = inputs["x_prompt"].shape, inputs["x_sample"].shape, inputs["cache_k"].shape
    sp, sc, sd = (inputs[n].shape for n in ("state_pool", "state_conv", "state_delta"))
    outs = [xp, xs, (1, xp[0], xp[1], *ck[3:]), (1, xp[0], xp[1], *ck[3:]), (1, xs[0], xs[1], *ck[3:]),
            (1, xs[0], xs[1], *ck[3:]), (1, xp[0], *sp[2:]), sp, (1, xp[0], *sc[2:]), sc, (1, xp[0], *sd[2:]), sd]
    nc = _bacc.Bacc("TRN2", target_bir_lowering=False, num_devices=1)
    arrays, args = {}, []
    for name in _INS:
        a = _np.ascontiguousarray(inputs[name])
        arrays[f"in_{name}_dram"] = a
        args.append(nc.dram_tensor(f"in_{name}_dram", a.shape, _mybir.dt.from_np(a.dtype), kind="ExternalInput").ap())
    for i, shape in enumerate(outs):
        args.append(nc.dram_tensor(f"out_{i}_dram", shape, _mybir.dt.float32, kind="ExternalOutput").ap())
    build(nc, *args)
    r = _run(nc, [arrays], core_ids=[0])
    return tuple(r.results[0][f"out_{i}_dram"] for i in range(len(outs)))
```

```python
from contextlib import ExitStack

import concourse.bass as bass
from concourse import mybir

F32 = mybir.dt.float32
I32 = mybir.dt.int32
ALU = mybir.AluOpType
ACT = mybir.ActivationFunctionType
AX = mybir.AxisListType.X
P = 128
EPS = 1e-6
FAR = 1.0e30
MOBA_BLOCK = 256
TOPK = 3
WINDOWS = (2, 4, 8, 16)
RING = 5
SLOT = 2048


def build(nc, x_prompt, x_sample, cache_k, cache_v, state_pool, state_conv, state_delta, page_table,
          c_prompt, c_sample, norm1_w, ada_w, ada_b, w_in, pool_w, pool_scale, q_norm_w, k_norm_w,
          conv_w, a_log, dt_bias, dn_norm_w, w_out, norm2_w, w_gate, w_up, w_down,
          y_prompt, y_sample, k_prompt, v_prompt, k_sample, v_sample, pool_prompt, pool_sample,
          conv_prompt, conv_sample, delta_prompt, delta_sample):
    _, T, D = x_prompt.shape
    NS = x_sample.shape[0]
    NPHYS, PAGE, H, HD = cache_k.shape[1:]
    NPG = page_table.shape[1]
    POOLW = state_pool.shape[3]
    NBUF = state_pool.shape[2]
    CW3 = state_conv.shape[3]
    NCV = state_conv.shape[2]
    GH, DK, DV = state_delta.shape[2:]
    DFF = w_gate.shape[2]
    NT = T + NS
    NC = 1 + NS
    DC = D // P
    TT = T // P
    AW = H * HD
    AC = AW // P
    PCH = POOLW // P
    GC = GH * DV // P
    QC0, KC0, VC0 = PCH, PCH + AC, PCH + 2 * AC
    CV0 = PCH + 3 * AC
    CVN = CW3 // P
    Z0 = CV0 + CVN
    PJ = Z0 + GC
    FC = DFF // P
    NB = NPG * PAGE // MOBA_BLOCK
    PPB = MOBA_BLOCK // PAGE
    SCALE = float(HD) ** -0.5
    assert T == 2 * P and T <= MOBA_BLOCK and PAGE == P and D == DC * P and HD == DK == DV == 64
    assert PJ * P + 2 * GH == w_in.shape[2] and PJ == FC and NS * NPG * H == 512 and AW == 512

    IW = SLOT // DC
    PGI = SLOT // AW
    HALVES = NPG // PGI
    stream = [("ada", i) for i in range(2 * D // IW)]
    NA = 6 * D // IW // 2
    ORDER = ("W7 W8 W9 W10 BA CEXT W1 CONV AB W2 QSUM DSUM W3 QR GN QB0 QB1 K0 GC W4 GBC KSUM ROWS KK QB2 K1 TI W5 "
             "L1 KR KROW M1 W6 QB3 K2 L2 VR VROW M2 W0 QB4 K3 L3 TAILS M3 QB5 K4 S L4 POOL QB6 A4 M4 H0 K5 QB7 L5 A5 H1 "
             "M5 K6 L6 A6 H2 M6 K7 UA H3 UB A7 H4 UC H5 UD A8 XA H6 XB A9 H7 XC HE A10 XD OWN A11 DMAX DEXP "
             "V0 V1 V2 V3 V4 V5 V6 V7 VE").split()
    ORDER = [(st.rstrip("0123456789"), int("0" + st.lstrip("ABCDEFGHIJKLMNOPQRSTUVWXYZ"))) for st in ORDER]
    for st, n in ORDER:
        if st == "W":
            stream.append(("win", n))
        elif st == "A":
            stream += [("ada", 2 * n), ("ada", 2 * n + 1)]
        elif st in ("K", "V"):
            stream += [(st.lower(), (n, hf)) for hf in range(NPG * AW // SLOT)]
    win_order = [n for st, n in ORDER if st == "W"]

    def out_count(j):
        return 2 * win_order.index(j // 2) + j % 2 + 1

    stream += [("wout", i) for i in range(D // IW)]
    for i in range(DFF // IW):
        stream += [("gate", i), ("up", i)]
    DKT = [(a, min(a + DC, FC)) for a in range(0, FC, DC)]
    stream += [("down", (i, j)) for i in range(D // IW) for j in range(len(DKT))]
    place = {it: (n % RING, n // RING) for n, it in enumerate(stream)}

    ctx = ExitStack()
    with ctx:
        sb = lambda name, shape, dt=F32: ctx.enter_context(nc.sbuf_tensor(name, shape, dt))
        sems = {}

        def sem(name):
            if name not in sems:
                sems[name] = ctx.enter_context(nc.semaphore(name))
            return sems[name]

        ring = sb("ring", [P, RING, SLOT])
        x_nat = sb("x_nat", [P, TT + 1, D])
        c_nat = x_nat[32:32 + NC, TT, :]
        rows = sb("rows", [P, P])
        R_ADAB, R_N1, R_N2 = 0, 6 * DC, 7 * DC
        R_PS = 8 * DC
        R_CW = R_PS + PCH
        R_Q = R_CW + (NCV + 1) * CVN
        NR = R_Q + 3
        xT = sb("xT", [P, DC, NT])
        hT = sb("hT", [P, DC, NT])
        mixT = sb("mixT", [P, DC, NT])
        proj = sb("proj", [P, PJ, NT])
        hid = proj
        cv = sb("cv", [P, CVN, NT])
        modT = sb("modT", [P, 6 * DC, NC])
        scA = sb("scA", [P, DC, NC])
        cT = sb("cT", [P, DC, 32])
        adaS = sb("adaS", [P, 512])
        constT = sb("constT", [P, 96])
        rbc = sb("rbc", [P, 4, NT])
        ident = sb("ident", [P, P])
        ones = sb("ones", [P, P])
        blk = sb("blk", [P, P])
        i64 = sb("i64", [P, HD])
        triu = sb("triu", [P, P])
        lvl = sb("lvl", [P, 7, P])
        cmask = sb("cmask", [P, 3, P])
        selh = sb("selh", [GH, GC, P])
        selc = sb("selc", [P, NS, 32])
        dm8 = sb("dm8", [P, H])
        vn = sb("vn", [P, TT, GH * DV])
        rcnt = sb("rcnt", [P, PCH, T])
        wba = sb("wba", [P, DC, 2 * GH])
        poolw = sb("poolw", [P, PCH, 64])
        gcol = sb("gcol", [GH, 4])
        nat8 = sb("nat8", [NS, 3, AW])
        stg = sb("stg", [P, 2, AW])
        vnat = sb("vnat", [P, TT, AW])
        qb = sb("qb", [P, 2, AW])
        prod = sb("prod", [P, SLOT])
        s_all = sb("s_all", [P, 512])
        pP = prod[:, :].rearrange("p (a m) -> p a m", m=32)
        sq4 = prod[:, 0:AC * NT].rearrange("p (c t) -> p c t", c=AC)
        w_ab = sb("w_ab", [P, 1024])
        w_a, w_b = w_ab[:, 0:512], w_ab[:, 512:1024]
        eps = sb("eps", [P, 2])
        gate4 = sb("gate4", [P, NS, NB, H])
        cnt4 = sb("cnt4", [P, NS, NB, H])
        g4, c4 = (m[:, :, :, :].rearrange("p q k h -> p (q k) h") for m in (gate4, cnt4))
        cmp1 = sb("cmp1", [P, NS, H])
        sm64 = sb("sm64", [P, 6, NS, H])
        own8 = sb("own8", [NS, 2, 64])
        tokmax = sb("tokmax", [P, 4])
        smpT = sb("smpT", [P, 2, 2, 3 * P])
        sm, pT = smpT[:, 0, :, :], smpT[:, 1, :, :]
        st4 = sb("st4", [P, 2, 8])
        table = sb("table", [1, NS * NPG], I32)
        ab = smpT[0:GH, :, :, :].rearrange("p a b c -> p (a b c)")[:, 0:5 * NT].rearrange("p (a t) -> p a t", a=5)
        gn = sb("gn", [P, TT, 2, GH])
        gs = sb("gs", [P, 8, TT * GH])
        vb = sb("vb", [P, TT, GH * DV])
        kbkd = sb("kbkd", [P, 2, TT, GH * DK])
        kbg, kd = kbkd[:, 0, :, :], kbkd[:, 1, :, :]
        kbT = w_b.rearrange("p (c t) -> p c t", c=GC)
        qdT = x_nat[:, TT, 2 * T:2 * T + GC * P].rearrange("p (c i) -> p c i", c=GC)
        mats = sb("mats", [P, 4, TT, GH, P])
        DT, MT, Tn, Tt = (mats[:, n, :, :, :] for n in range(4))
        AT = DT
        BTP1 = sb("BTP1", [P, 2, TT, GH, P])
        BT, P1 = BTP1[:, 0, :, :, :], BTP1[:, 1, :, :, :]
        kcT = x_nat[:, TT, 2 * T + GC * P:2 * T + 2 * GC * P].rearrange("p (c i) -> p c i", c=GC)
        S1 = sb("S1", [P, GC, DV])
        S2 = sb("S2", [P, GC, DV])
        Ss = x_nat[:, 0, :].rearrange("p (b c v) -> p b c v", b=NS, c=GC)
        Sx = x_nat[:, 1, :].rearrange("p (b c v) -> p b c v", b=NS, c=GC)
        cst = kbkd[0:NS * NCV, :, :, :].rearrange("p a n d -> p (a n d)")[:, 0:CW3]
        cext = sb("cext", [P, CVN, NS * NCV])
        pbuf = mats[0:NS, :, :, :, :].rearrange("p a n h i -> p (a n h i)")[:, 0:NBUF * POOLW]
        pd8 = vb[0:NS, :, :]
        pw1, pw2 = x_nat[:, TT, 0:T], x_nat[:, TT, T:2 * T]
        pdT = sb("pdT", [P, PCH, NT])
        tail, utail = w_ab[0:32, 0:CW3], w_ab[0:32, CW3:CW3 + POOLW]
        ynat = x_nat
        bgs = sb("bgs", [P, 2, GC, NS])
        sv = sb("sv", [P, 3, GC, NS])
        bank = [ctx.enter_context(nc.psum_tensor(f"bank{i}", [P, 512], F32)) for i in range(8)]

        slot_full = [sem(f"slot_full{i}") for i in range(RING)]
        bank_full = [sem(f"bank_full{i}") for i in range(8)]
        bank_free = [sem(f"bank_free{i}") for i in range(8)]
        filled, freed_by, fills, frees = {}, {}, [0] * 8, [0] * 8

        counts, running = {}, [0] * RING
        for it in stream:
            s, _ = place[it]
            running[s] += 16 * (PGI if it[0] in "kv" else 1)
            counts[it] = running[s]

        def full_count(item):
            return counts[item]

        def arrived(eng, item):
            eng.wait_ge(slot_full[place[item][0]], full_count(item))
            return ring[:, place[item][0], :]

        released, singles = {}, {"pe_read": 0, "keys_read": 0}

        def used_up(ins, item, name):
            singles[name] += 1
            ins.then_inc(sem(name), 1)
            released[item] = (sem(name), singles[name])

        def read_by(name, item):
            b, n = filled[name]
            released[item] = (bank_full[b], n)

        def full(eng, name):
            b, n = filled[name]
            eng.wait_ge(bank_full[b], n)
            return bank[b]

        def freed(ins, name):
            ins.then_inc(bank_free[filled[name][0]], 1)

        def frees_at(name):
            return freed_by[name]

        def order(eng, name):
            n = [0]
            s = sem(name)

            def chain(ins):
                n[0] += 1
                ins.then_inc(s, 1)
                eng.wait_ge(s, n[0])
            return chain

        block = ctx.enter_context(nc.Block())

        @block.tensor
        def _(pe):
            def opened(name, b, readers=1):
                if frees[b]:
                    pe.wait_ge(bank_free[b], frees[b])
                fills[b] += 1
                frees[b] += readers
                assert name not in filled, name
                filled[name] = (b, fills[b])
                freed_by[name] = frees[b]
                return bank[b]

            def closed(ins, name):
                ins.then_inc(bank_full[filled[name][0]], 1)

            def mm(out, lhsT, rhs, start=True, stop=True):
                return pe.matmul(out, lhsT, rhs, start=start, stop=stop, skip_group_check=True)

            pe.wait_ge(sem("ident_made"), 1)
            pe.wait_ge(sem("rows_in"), 16 * 11)
            b = opened("rowsT", 2)
            closed(pe.transpose(b[:, 0:NR], rows[0:NR, :], ident[0:NR, 0:NR]), "rowsT")
            pe.wait_ge(sem("c_silu"), 1)
            b = opened("cT", 3)
            for c in range(DC):
                last = pe.transpose(b[:, c * NC:(c + 1) * NC], c_nat[:, c * P:(c + 1) * P], ident[32:32 + NC, 32:32 + NC])
            closed(last, "cT")
            pe.wait_ge(sem("x_in"), 16 * (TT + 1))
            for c in range(DC):
                b = opened(f"xT{c}", 4 + c % 4)
                for r in range(TT):
                    pe.transpose(b[:, r * P:(r + 1) * P], x_nat[:, r, c * P:(c + 1) * P], ident[:, :])
                closed(pe.transpose(b[:, T:NT], x_nat[0:NS, TT, c * P:(c + 1) * P], ident[0:NS, 0:NS]), f"xT{c}")

            def ada(j):
                b = opened(f"ada{j}", 3)
                for n in range(2):
                    slot = arrived(pe, ("ada", 2 * j + n)).rearrange("p (k n) -> p k n", k=DC)
                    for kk in range(2):
                        for g in range(4):
                            k = 2 * g + kk
                            last = mm(b[32 * g:32 * g + 32, n * IW:(n + 1) * IW], cT[:, k, :], slot[:, k, :],
                                      kk == 0, kk == 1)
                    if n == 0:
                        used_up(last, ("ada", 2 * j), "pe_read")
                closed(last, f"ada{j}")
                read_by(f"ada{j}", ("ada", 2 * j + 1))

            def ada_turn(j):
                pe.wait_ge(sem("ada_rows"), j + 1)
                b = opened(f"adaT{j}", 3)
                for n in range(4):
                    last = pe.transpose(b[:, n * P:(n + 1) * P], adaS[:, n * P:(n + 1) * P], ident[:, :])
                closed(last, f"adaT{j}")

            pe.wait_ge(sem("cT_made"), 1)
            pe.wait_ge(sem("masks_made"), 1)
            for j in range(2 * D // IW // 2):
                ada(j)
                ada_turn(j)

            def square_sums(name, ready, src):
                pe.wait_ge(sem(ready), 1)
                b = opened(name, 0)
                for c in range(DC):
                    last = mm(b[:, 0:NT], ones[:, :], src[:, c, :], c == 0, c == DC - 1)
                closed(last, name)

            square_sums("ss1", "sq1", hT)
            pe.wait_ge(sem("h1"), 1)

            def project(item):
                slot = arrived(pe, ("win", item)).rearrange("p (k n) -> p k n", k=DC)
                for n in range(2):
                    j = 2 * item + n
                    b = opened(f"proj{j}", n)
                    for k in range(DC):
                        last = mm(b[:, 0:NT], slot[:, k, n * P:(n + 1) * P], hT[:, k, :], k == 0, k == DC - 1)
                    closed(last, f"proj{j}")
                read_by(f"proj{j}", ("win", item))

            def head_sums(name, ready, src, n=4, banks=(2, 3, 2, 3)):
                pe.wait_ge(sem(ready), 1)
                for c in range(n):
                    b = opened(f"{name}{c}", banks[c])
                    closed(mm(b[:, 0:NT], blk[:, :], src(c)), f"{name}{c}")

            def to_rows8(name, ready, c0, n=1):
                pe.wait_ge(sem(ready), n)
                b = opened(name, 2)
                for c in range(AC):
                    last = pe.transpose(b[0:NS, c * P:(c + 1) * P], proj[:, c0 + c, T:NT], ident[:, :])
                closed(last, name)

            def q_spread(b_):
                pe.wait_ge(sem("q_rows8"), 1)
                b = opened(f"qb{b_}", 2)
                closed(mm(b[:, :], ident[0:NS, b_:b_ + 1].to_broadcast([NS, P]), nat8[:, 0, :]), f"qb{b_}")

            def kv_rows(name, c0, ready, n):
                pe.wait_ge(sem(ready), n)
                for r in range(TT):
                    b = opened(f"{name}{r}", 2 + r)
                    for c in range(AC):
                        last = pe.transpose(b[:, c * P:(c + 1) * P], proj[:, c0 + c, r * P:(r + 1) * P], ident[:, :])
                    closed(last, f"{name}{r}")

            def decay_inputs():
                pe.wait_ge(sem("wba_in"), 16)
                b = opened("ba", 2)
                for k in range(DC):
                    mm(b[0:GH, 0:NT], wba[:, k, 0:GH], hT[:, k, :], k == 0, k == DC - 1)
                    last = mm(b[32:32 + GH, 0:NT], wba[:, k, GH:2 * GH], hT[:, k, :], k == 0, k == DC - 1)
                closed(last, "ba")

            def cached_rows():
                pe.wait_ge(sem("cst_in"), 16)
                b = opened("cext", 3)
                for c in range(CVN):
                    last = pe.transpose(b[:, c * NS * NCV:(c + 1) * NS * NCV], cst[:, c * P:(c + 1) * P],
                                        ident[0:NS * NCV, 0:NS * NCV])
                closed(last, "cext")
                pe.wait_ge(sem("pool_rows"), 1)
                b = opened("pdT8", 3)
                for c in range(PCH):
                    last = pe.transpose(b[:, c * NS:(c + 1) * NS], pd8[:, 0, c * P:(c + 1) * P], ident[0:NS, 0:NS])
                closed(last, "pdT8")

            def tails():
                pe.wait_ge(sem("proj_out"), PJ)
                b = opened("utail", 3)
                for c in range(PCH):
                    last = pe.transpose(b[0:NBUF + NS, c * P:(c + 1) * P], proj[:, c, T - NBUF:NT], ident[:, :])
                closed(last, "utail")
                for hlf in range(2):
                    b = opened(f"ctail{hlf}", 2 + hlf)
                    for c in range(3):
                        last = pe.transpose(b[0:NCV + NS, c * P:(c + 1) * P],
                                            proj[:, CV0 + 3 * hlf + c, T - NCV:NT], ident[:, :])
                    closed(last, f"ctail{hlf}")

            def pool_maps():
                pe.wait_ge(sem("pool_diff"), 1)
                pe.wait_ge(sem("poolw_in"), 16 * 2 * PCH)
                for c in range(PCH):
                    b = opened(f"pool{c}", 2 + c)
                    for g in range(2):
                        r = 64 * g
                        last = mm(b[r:r + 64, 0:NT], poolw[r:r + 64, c, :], pdT[r:r + 64, c, :])
                    closed(last, f"pool{c}")

            def att_scores(h):
                c, r = h // 2, 64 * (h % 2)
                b = opened(f"S{h}", h % 2)
                mm(b[:, 0:P], proj[r:r + 64, QC0 + c, 0:P], proj[r:r + 64, KC0 + c, 0:P])
                closed(mm(b[:, P:3 * P], proj[r:r + 64, QC0 + c, P:T], proj[r:r + 64, KC0 + c, 0:T]), f"S{h}")

            def att_turn(h):
                pe.wait_ge(sem("probs"), h + 1)
                b = opened(f"PT{h}", h % 2)
                for n in range(3):
                    last = pe.transpose(b[:, n * P:(n + 1) * P], sm[:, h % 2, n * P:(n + 1) * P], ident[:, :])
                closed(last, f"PT{h}")

            def att_out(h):
                pe.wait_ge(sem("probsT"), h + 1)
                c, r = h // 2, 64 * (h % 2)
                if h % 2 == 0:
                    opened(f"O{c}", 2)
                b = bank[2]
                mm(b[r:r + 64, 0:T], vnat[:, 0, h * HD:(h + 1) * HD], pT[:, h % 2, 0:2 * P], True, False)
                last = mm(b[r:r + 64, P:T], vnat[:, 1, h * HD:(h + 1) * HD], pT[:, h % 2, 2 * P:3 * P], False, True)
                if h % 2:
                    closed(last, f"O{c}")
                else:
                    last.then_inc(sem("att_even"), 1)

            def att_start():
                pe.wait_ge(sem("v_rows"), 2)
                pe.wait_ge(sem("k_done"), 1)
                att_scores(0)

            def att_head(h):
                if h + 1 < H:
                    att_scores(h + 1)
                att_turn(h)
                if h >= 1:
                    att_out(h - 1)

            def dn_heads():
                pe.wait_ge(sem("ab_done"), 1)
                b = opened("gn", 4)
                for n in range(TT):
                    for w in range(2):
                        o = (2 * n + w) * GH
                        last = pe.transpose(b[:, o:o + GH], ab[:, w, n * P:(n + 1) * P], ident[0:GH, 0:GH])
                closed(last, "gn")
                for c in range(GC):
                    b = opened(f"bbc{c}", 5 + c)
                    mm(b[:, 0:NT], selh[:, c, :], ab[:, 0, :])
                    closed(mm(b[:, NT:NT + NS], selh[:, c, :], ab[:, 2, T:NT]), f"bbc{c}")

            def dn_cumulate():
                pe.wait_ge(sem("gn_out"), 1)
                b = opened("gcum", 7)
                for n in range(TT):
                    mm(b[:, n * GH:(n + 1) * GH], triu[:, :], gn[:, n, 1, :])
                    last = mm(b[:, (TT + n) * GH:(TT + n + 1) * GH], ones[:, :], gn[:, n, 1, :])
                closed(last, "gcum")

            def dn_spread():
                pe.wait_ge(sem("ug"), 1)
                for n in range(TT):
                    b = opened(f"gbc{n}", 4 + n, 2 if n else 1)
                    closed(mm(b[:, :], ones[:, :], P1[:, n, :, :].rearrange("p h i -> p (h i)")), f"gbc{n}")

            def dn_rows():
                pe.wait_ge(sem("qk_d"), 1)
                for w in range(2):
                    b = opened(f"dn_rows{w}", 6 + w)
                    for n in range(TT):
                        for c in range(GC):
                            o = (n * GC + c) * P
                            last = pe.transpose(b[:, o:o + P], cv[:, (1 + w) * GC + c, n * P:(n + 1) * P], ident[:, :])
                    closed(last, f"dn_rows{w}")

            def dn_products():
                pe.wait_ge(sem("kbT"), 1)
                for h2 in range(2):
                    r = slice(64 * h2, 64 * h2 + 64)
                    for w, right in enumerate((kbT, cv)):
                        b = opened(f"kk{w}{h2}", 4 + 2 * w + h2)
                        for n in range(TT):
                            for c in range(GC):
                                o = (n * GC + c) * P
                                last = mm(b[:, o:o + P], cv[r, GC + c, n * P:(n + 1) * P],
                                          right[r, c, n * P:(n + 1) * P])
                        closed(last, f"kk{w}{h2}")

            def dn_first():
                for n in range(TT):
                    pe.wait_ge(sem("Tt"), n + 1)
                    b = opened(f"T0{n}", 4 + n)
                    for h in range(GH):
                        last = pe.transpose(b[:, h * P:(h + 1) * P], Tt[:, n, h, :], ident[:, :])
                    closed(last, f"T0{n}")

            def dn_inner(s):
                for n in range(TT):
                    pe.wait_ge(sem("BT"), TT * (s - 1) + n + 1)
                    pe.wait_ge(sem("Tn"), TT * (s - 1) + n + 1)
                    b = opened(f"P1{s}{n}", 4 + n)
                    for h in range(GH):
                        last = mm(b[:, h * P:(h + 1) * P], BT[:, n, h, :], Tn[:, n, h, :])
                    closed(last, f"P1{s}{n}")

            def dn_outer(s):
                for n in range(TT):
                    pe.wait_ge(sem("P1"), TT * (s - 1) + n + 1)
                    pe.wait_ge(sem("Tt"), TT * (s - 1) + n + 1)
                    b = opened(f"Pt{s}{n}", 6 + n)
                    for h in range(GH):
                        last = mm(b[:, h * P:(h + 1) * P], P1[:, n, h, :], Tt[:, n, h, :])
                    closed(last, f"Pt{s}{n}")
                    if s < 6:
                        b = opened(f"Pn{s}{n}", 4 + n)
                        for h in range(GH):
                            last = mm(b[:, h * P:(h + 1) * P], Tt[:, n, h, :], P1[:, n, h, :])
                        closed(last, f"Pn{s}{n}")

            def state(name, n, b_, ready, cnt):
                pe.wait_ge(sem(ready), cnt)
                b = opened(name, b_)
                for h in range(GH):
                    c, r = h // 2, 64 * (h % 2)
                    last = mm(b[r:r + 64, c * DV:(c + 1) * DV], kd[:, n, h * DK:(h + 1) * DK],
                              vn[:, n, h * DV:(h + 1) * DV])
                closed(last, name)

            def dn_values():
                pe.wait_ge(sem("Tt"), TT * 7)
                pe.wait_ge(sem("dn_scaled"), 1)
                for n in range(TT):
                    b = opened(f"u{n}", 6 + n)
                    for h in range(GH):
                        last = mm(b[:, h * DV:(h + 1) * DV], Tt[:, n, h, :], vb[:, n, h * DV:(h + 1) * DV])
                    closed(last, f"u{n}")
                b = opened("kc", 4)
                for h in range(GH):
                    c, r = h // 2, 64 * (h % 2)
                    last = mm(b[r:r + 64, c * P:(c + 1) * P], kbg[:, 1, h * DK:(h + 1) * DK], Tt[:, 1, h, :])
                closed(last, "kc")

            def dn_carry():
                pe.wait_ge(sem("S1"), 1)
                pe.wait_ge(sem("kcT"), 1)
                for h2 in range(2):
                    r = slice(64 * h2, 64 * h2 + 64)
                    b = opened(f"kcS{h2}", 6 + h2)
                    for c in range(GC):
                        last = mm(b[:, c * DV:(c + 1) * DV], kcT[r, c, :], S1[r, c, :])
                    closed(last, f"kcS{h2}")

            def dn_out():
                state("state2", 1, 4, "vn", 2)
                pe.wait_ge(sem("qdT"), 1)
                b = opened("oT", 5)
                for h in range(GH):
                    c, r = h // 2, 64 * (h % 2)
                    mm(b[r:r + 64, c * T:c * T + P], vn[:, 0, h * DV:(h + 1) * DV], AT[:, 0, h, :])
                for h in range(GH):
                    c, r = h // 2, 64 * (h % 2)
                    mm(b[r:r + 64, c * T + P:(c + 1) * T], vn[:, 1, h * DV:(h + 1) * DV], AT[:, 1, h, :], True, False)
                    last = mm(b[r:r + 64, c * T + P:(c + 1) * T], S1[r:r + 64, c, :], qdT[r:r + 64, c, :], False, True)
                closed(last, "oT")

            def state_product(name, b_, src, col):
                b = opened(name, b_)
                for c in range(GC):
                    for h2 in range(2):
                        r = 64 * h2
                        for q in range(NS):
                            last = mm(b[r:r + 64, c * NS + q:c * NS + q + 1], src[r:r + 64, q, c, :],
                                      cv[r:r + 64, col + c, T + q:T + q + 1])
                closed(last, name)

            def step_old():
                pe.wait_ge(sem("S_in"), 16 * 4)
                pe.wait_ge(sem("qk_d"), 1)
                state_product("kS", 6, Ss, GC)

            def step_spread():
                pe.wait_ge(sem("vdiag"), 1)
                vd = P1[:, :, :, :].rearrange("p n h i -> p (n h i)")
                for n in range(2):
                    b = opened(f"vbc{n}", 6 + n)
                    closed(mm(b[:, :], blk[:, :], vd[:, 512 * n:512 * n + 512]), f"vbc{n}")

            def step_new():
                pe.wait_ge(sem("Snew"), 1)
                state_product("qS", 4, Ss, 0)

            def out_sums():
                pe.wait_ge(sem("o_sq"), 1)
                for c in range(GC):
                    b = opened(f"oss{c}", 6 + c)
                    closed(mm(b[:, 0:NT], blk[:, :], sq4[:, c, :]), f"oss{c}")

            def own_scores():
                pe.wait_ge(sem("own_diag"), 1)
                b = opened("own", 6)
                closed(mm(b[:, 0:NS * H], ones[0:NS, :], own8[:, 1, :]), "own")
                pe.wait_ge(sem("k_scored"), NS)
                b = opened("gsum", 7)
                closed(mm(b[:, :], ones[:, :], s_all[:, :]), "gsum")
                b = opened("sT", 4)
                for n in range(4):
                    last = pe.transpose(b[:, n * P:(n + 1) * P], s_all[:, n * P:(n + 1) * P], ident[:, :])
                closed(last, "sT")

            def spread_max():
                pe.wait_ge(sem("max_diag"), 1)
                b = opened("pmax", 5)
                closed(mm(b[:, :], ones[:, :], w_a[:, :]), "pmax")

            def denominators():
                pe.wait_ge(sem("exps"), 1)
                b = opened("den", 6)
                closed(mm(b[:, :], ones[:, :], w_b[:, :]), "den")

            def fold(q):
                pe.wait_ge(sem("pv_masked"), q + 1)
                if q == 0:
                    opened("y8", 6)
                g = 32 * (q % 4)
                last = mm(bank[6][g:g + 32, :], selc[:, q, :], stg[:, q % 2, :], q < 4, q >= 4)
                if q < NS - 1:
                    last.then_inc(sem("folded"), 1)
                return last

            def page_values(q):
                if q == 0:
                    pe.wait_ge(sem("p_ready"), 1)
                b = opened(f"pv{q}", 4 + q % 2)
                for hf in range(HALVES):
                    slot = arrived(pe, ("v", (q, hf))).rearrange("p (k n) -> p k n", k=PGI)
                    for k in range(PGI):
                        last = mm(b[32 * k:32 * k + 32, :], pP[:, q * NPG + hf * PGI + k, :], slot[:, k, :],
                                  hf == 0, hf == HALVES - 1)
                    if hf < HALVES - 1:
                        used_up(last, ("v", (q, hf)), "pe_read")
                closed(last, f"pv{q}")
                read_by(f"pv{q}", ("v", (q, HALVES - 1)))
                if q:
                    fold(q - 1)

            def page_end():
                closed(fold(NS - 1), "y8")
                pe.wait_ge(sem("y8_out"), 1)
                b = opened("yT8", 7)
                for c in range(AC):
                    last = pe.transpose(b[:, c * P:(c + 1) * P], w_a[:, c * P:(c + 1) * P], ident[:, :])
                closed(last, "yT8")

            def ada_pair(j):
                ada(j)
                ada_turn(j)

            go = {
                "W": project, "BA": lambda _: decay_inputs(), "CEXT": lambda _: cached_rows(), "A": ada_pair,
                "QSUM": lambda _: head_sums("qss", "q_sq", lambda c: mixT[:, c, :]),
                "KSUM": lambda _: head_sums("kss", "k_sq", lambda c: mixT[:, AC + c, :]),
                "DSUM": lambda _: head_sums("dss", "d_sq", lambda c: sq4[:, c, :], 4, (4, 5, 6, 7)),
                "QR": lambda _: to_rows8("q8", "q_done", QC0), "QB": q_spread,
                "KR": lambda _: to_rows8("k8", "k_done", KC0),
                "VR": lambda _: to_rows8("v8", "proj_out", VC0, out_count(VC0 + AC - 1)),
                "KROW": lambda _: kv_rows("krow", KC0, "k_done", 1),
                "VROW": lambda _: kv_rows("vrow", VC0, "proj_out", out_count(VC0 + AC - 1)),
                "GN": lambda _: dn_heads(), "GC": lambda _: dn_cumulate(), "GBC": lambda _: dn_spread(),
                "ROWS": lambda _: dn_rows(), "KK": lambda _: dn_products(), "TI": lambda _: dn_first(),
                "L": dn_inner, "M": dn_outer, "TAILS": lambda _: tails(), "POOL": lambda _: pool_maps(),
                "S": lambda _: att_start(), "H": att_head, "HE": lambda _: att_out(H - 1),
                "UA": lambda _: dn_values(), "UB": lambda _: state("state1", 0, 5, "vn", 1),
                "UC": lambda _: dn_carry(), "UD": lambda _: dn_out(), "XA": lambda _: step_old(),
                "XB": lambda _: step_spread(), "XC": lambda _: step_new(), "XD": lambda _: out_sums(),
                "OWN": lambda _: own_scores(), "DMAX": lambda _: spread_max(), "DEXP": lambda _: denominators(),
                "V": page_values, "VE": lambda _: page_end(),
            }
            for st, n in ORDER:
                if st in go:
                    go[st](n)

            pe.wait_ge(sem("mix"), 1)
            for i in range(D // IW):
                slot = arrived(pe, ("wout", i)).rearrange("p (k n) -> p k n", k=DC)
                for n in range(2):
                    j = 2 * i + n
                    b = opened(f"out{j}", n)
                    for k in range(DC):
                        last = mm(b[:, 0:NT], slot[:, k, n * P:(n + 1) * P], mixT[:, k, :], k == 0, k == DC - 1)
                    closed(last, f"out{j}")
                read_by(f"out{j}", ("wout", i))
            square_sums("ss2", "sq2", hT)
            pe.wait_ge(sem("h2"), 1)

            for i in range(DFF // IW):
                for w, kind in enumerate(("gate", "up")):
                    slot = arrived(pe, (kind, i)).rearrange("p (k n) -> p k n", k=DC)
                    for n in range(2):
                        name = f"{kind}{2 * i + n}"
                        b = opened(name, 2 * w + n)
                        for k in range(DC):
                            last = mm(b[:, 0:NT], slot[:, k, n * P:(n + 1) * P], hT[:, k, :], k == 0, k == DC - 1)
                        closed(last, name)
                    read_by(name, (kind, i))
            pe.wait_ge(sem("hidden"), FC)
            for i in range(D // IW):
                for n in range(2):
                    opened(f"down{2 * i + n}", 4 + 2 * (i % 2) + n)
                for m, (k0, k1) in enumerate(DKT):
                    slot = arrived(pe, ("down", (i, m))).rearrange("p (k n) -> p k n", k=DC)
                    for n in range(2):
                        for k in range(k0, k1):
                            last = mm(bank[4 + 2 * (i % 2) + n][:, 0:NT], slot[:, k - k0, n * P:(n + 1) * P],
                                      hid[:, k, :], k == 0, k == FC - 1)
                        if m == len(DKT) - 1:
                            closed(last, f"down{2 * i + n}")
                    if m < len(DKT) - 1:
                        used_up(last, ("down", (i, m)), "pe_read")
                    else:
                        read_by(f"down{2 * i + 1}", ("down", (i, m)))
            pe.wait_ge(sem("x2"), DC)
            for r in range(TT + 1):
                m = P if r < TT else NS
                for hlf in range(2):
                    b = opened(f"y{r}{hlf}", 2 * (r % 2) + hlf)
                    for c in range(4):
                        last = pe.transpose(b[0:m, c * P:(c + 1) * P], xT[:, 4 * hlf + c, r * P:r * P + m], ident[:, :])
                    closed(last, f"y{r}{hlf}")

        @block.vector
        def _(v):
            step = order(v, "dve_step")

            def tt(out, a, b_, op):
                return v.tensor_tensor(out, a, b_, op)

            def bc(ap, shape):
                return ap.to_broadcast(shape)

            def inc(ins, name):
                ins.then_inc(sem(name), 1)

            step(v.memset(cT[:, :, :], 0.0))
            v.memset(eps[:, 0:1], EPS)
            step(v.memset(eps[:, 1:2], 1.0))
            step(v.memset(st4[:, :, :], 0.0))
            b = full(v, "rowsT")
            step(v.tensor_copy(constT[:, 0:NR], b[:, 0:NR]))
            v.sem_inc(bank_free[2], 1)
            b = full(v, "cT")
            freed(v.tensor_copy(cT[:, :, 0:NC], b[:, 0:DC * NC].rearrange("p (c r) -> p c r", c=DC)), "cT")
            v.wait_ge(bank_free[3], frees_at("cT"))
            v.sem_inc(sem("cT_made"), 1)
            for c in range(0, DC, 2):
                b = full(v, f"xT{c}")
                freed(v.tensor_copy(xT[:, c, :], b[:, 0:NT]), f"xT{c}")
            v.wait_ge(sem("iota_made"), 1)
            for c in range(PCH):
                for g in range(2):
                    r = slice(64 * g, 64 * g + 64)
                    v.tensor_scalar(rcnt[r, c, :], rcnt[r, c, :], float(WINDOWS[2 * c + g]), None, ALU.min)
            step(v.tensor_scalar(eps[:, 0:1], eps[:, 0:1], 1.0, None, ALU.mult))
            v.reciprocal(rcnt[:, :, :], rcnt[:, :, :]).then_inc(sem("rcnt_made"), 1)

            def mod_reduce(j):
                b = full(v, f"adaT{j}")
                seen = b[:, :].rearrange("p (t g r) -> p t r g", t=4, g=4)[:, :, 0:NC, :]
                dst = modT[:, 4 * j:4 * j + 4, :]
                freed(v.tensor_reduce(dst, seen, AX, ALU.add), f"adaT{j}")
                v.wait_ge(bank_free[filled[f"adaT{j}"][0]], frees_at(f"adaT{j}"))
                step(tt(dst, dst, bc(constT[:, 4 * j:4 * j + 4].unsqueeze(2), [P, 4, NC]), ALU.add))

            def modulation(sc, wrow):
                step(v.scalar_tensor_tensor(out=scA[:, :, :], in0=modT[:, sc * DC:(sc + 1) * DC, :], scalar=1.0,
                                            in1=bc(constT[:, wrow:wrow + DC].unsqueeze(2), [P, DC, NC]),
                                            op0=ALU.add, op1=ALU.mult))

            def norm_apply(root, sh, done):
                v.wait_ge(sem(root), 1)
                step(v.reciprocal(rbc[:, 0, :], rbc[:, 0, :]))
                step(tt(hT[:, :, :], xT[:, :, :], bc(rbc[:, 0:1, :], [P, DC, NT]), ALU.mult))
                for c in range(DC):
                    v.tensor_scalar(hT[:, c, 0:T], hT[:, c, 0:T], scA[:, c, 0:1],
                                    modT[:, sh * DC + c, 0:1], ALU.mult, ALU.add)
                step(tt(hT[:, :, T:NT], hT[:, :, T:NT], scA[:, :, 1:NC], ALU.mult))
                inc(tt(hT[:, :, T:NT], hT[:, :, T:NT], modT[:, sh * DC:(sh + 1) * DC, 1:NC], ALU.add), done)

            v.wait_ge(sem("pbuf_in"), 16)
            for g, w in enumerate(WINDOWS):
                last = v.tensor_reduce(pd8[:, 0, 64 * g:64 * g + 64],
                                       pbuf.rearrange("b (t c) -> b c t", t=NBUF)[:, 64 * g:64 * g + 64, NBUF - w + 1:NBUF],
                                       AX, ALU.add)
            inc(last, "pool_rows")
            for j in range(2 * DC // 4):
                mod_reduce(j)
            modulation(1, R_N1)
            norm_apply("root1", 0, "h1")

            def head_norm(root, c0, row, done):
                v.wait_ge(sem(root), 4)
                step(v.reciprocal(rbc[:, :, :], rbc[:, :, :]))
                inc(v.scalar_tensor_tensor(out=proj[:, c0:c0 + AC, :].rearrange("p c t -> p (c t)"),
                                           in0=proj[:, c0:c0 + AC, :].rearrange("p c t -> p (c t)"),
                                           scalar=constT[:, row:row + 1],
                                           in1=rbc[:, :, :].rearrange("p c t -> p (c t)"),
                                           op0=ALU.mult, op1=ALU.mult), done)

            def rows8(name, n, done):
                b = full(v, name)
                freed(v.tensor_copy(nat8[:, n, :], b[0:NS, :]), name)
                v.wait_ge(bank_free[filled[name][0]], frees_at(name))
                v.sem_inc(sem(done), 1)

            def k_item(q, hf):
                slot = arrived(v, ("k", (q, hf)))
                v.wait_ge(sem("qb"), q + 1)
                ins = tt(prod[:, :].rearrange("p (k n) -> p k n", k=PGI), slot.rearrange("p (k n) -> p k n", k=PGI),
                         bc(qb[:, q % 2:q % 2 + 1, :], [P, PGI, AW]), ALU.mult)
                used_up(ins, ("k", (q, hf)), "keys_read")
                v.wait_ge(*released[("k", (q, hf))])
                o = (q * NPG + hf * PGI) * H
                ins = v.tensor_reduce(s_all[:, o:o + PGI * H], prod[:, :].rearrange("p (g d) -> p g d", d=HD), AX, ALU.add)
                if hf == HALVES - 1:
                    ins.then_inc(sem("k_scored"), 1)
                    v.wait_ge(sem("k_scored"), q + 1)
                else:
                    step(ins)

            def scores(q):
                for hf in range(HALVES):
                    k_item(q, hf)

            def att_mask(h):
                b = full(v, f"S{h}")
                freed(tt(sm[:, h % 2, :], b[:, 0:3 * P], cmask[:, :, :].rearrange("p a k -> p (a k)"), ALU.add), f"S{h}")
                v.wait_ge(bank_free[filled[f"S{h}"][0]], frees_at(f"S{h}"))
                v.tensor_reduce(st4[:, h % 2, 0:1], sm[:, h % 2, 0:P], AX, ALU.max)
                step(v.tensor_reduce(st4[:, h % 2, 1:2], sm[:, h % 2, P:3 * P], AX, ALU.max))
                inc(v.tensor_scalar(st4[:, h % 2, 2:4], st4[:, h % 2, 0:2], -SCALE, None, ALU.mult), "masked")

            def att_norm(h):
                v.wait_ge(sem("exped"), h + 1)
                step(v.reciprocal(st4[:, h % 2, 6:8], st4[:, h % 2, 4:6]))
                v.tensor_scalar(sm[:, h % 2, 0:P], sm[:, h % 2, 0:P], st4[:, h % 2, 6:7], None, ALU.mult)
                inc(v.tensor_scalar(sm[:, h % 2, P:3 * P], sm[:, h % 2, P:3 * P], st4[:, h % 2, 7:8], None, ALU.mult),
                    "probs")

            def att_take(c):
                b = full(v, f"O{c}")
                freed(v.tensor_copy(mixT[:, PCH + c, 0:T], b[:, 0:T]), f"O{c}")

            def att_first(_):
                att_mask(0)

            def att_head(h):
                if h >= 1:
                    full(v, f"PT{h - 1}")
                if h + 1 < H:
                    att_mask(h + 1)
                att_norm(h)
                if h >= 2 and h % 2 == 0:
                    att_take(h // 2 - 1)

            def cw(i, c):
                return constT[:, R_CW + i * CVN + c:R_CW + i * CVN + c + 1]

            def halves(m, h2):
                return m[:, :, :, :].rearrange("p n (c w) i -> p n w c i", w=2)[:, :, h2, :, :]

            def level(s, n):
                return tt(BT[:, n, :, :], MT[:, n, :, :], bc(lvl[:, s, :].unsqueeze(1), [P, GH, P]), ALU.mult)

            def outer(s):
                for n in range(TT):
                    b = full(v, f"Pt{s}{n}")
                    if s < 6:
                        inc(level(s + 1, n), "BT")
                    freed(tt(Tt[:, n, :, :], Tt[:, n, :, :], b[:, :].rearrange("p (h i) -> p h i", h=GH), ALU.subtract)
                          if s == 6 else after_turn(s, n, b), f"Pt{s}{n}")
                    v.wait_ge(bank_free[6 + n], frees_at(f"Pt{s}{n}"))
                    v.sem_inc(sem("Tt"), 1)
                    if s < 6:
                        bn = full(v, f"Pn{s}{n}")
                        freed(tt(Tn[:, n, :, :], Tn[:, n, :, :], bn[:, :].rearrange("p (h i) -> p h i", h=GH),
                                 ALU.subtract), f"Pn{s}{n}")
                        v.wait_ge(bank_free[4 + n], frees_at(f"Pn{s}{n}"))
                        v.sem_inc(sem("Tn"), 1)

            def after_turn(s, n, b):
                full(v, f"Pn{s}{n}")
                return tt(Tt[:, n, :, :], Tt[:, n, :, :], b[:, :].rearrange("p (h i) -> p h i", h=GH), ALU.subtract)

            def paged(ap):
                return ap.rearrange("p (n t h) -> p n t h", t=PPB, h=H)

            def queried(ap):
                return ap.rearrange("p (q n h) -> p q n h", q=NS, h=H)

            def cached_rows(_):
                b = full(v, "cext")
                freed(v.tensor_copy(cext[:, :, :], b[:, 0:CVN * NS * NCV].rearrange("p (c r) -> p c r", c=CVN)), "cext")
                v.wait_ge(bank_free[filled["cext"][0]], frees_at("cext"))
                b = full(v, "pdT8")
                freed(v.tensor_copy(pdT[:, :, T:NT], b[:, 0:PCH * NS].rearrange("p (c q) -> p c q", c=PCH)), "pdT8")
                v.wait_ge(bank_free[3], frees_at("pdT8"))

            def pool_maps(_):
                v.wait_ge(sem("proj_out"), out_count(PCH - 1))
                step(tt(pdT[:, :, T:NT], pdT[:, :, T:NT], proj[:, 0:PCH, T:NT], ALU.add))
                v.wait_ge(sem("pool_prompt_done"), 1)
                for c in range(PCH):
                    last = v.scalar_tensor_tensor(out=pdT[:, c, T:NT], in0=pdT[:, c, T:NT], scalar=rcnt[:, c, T - 1:T],
                                                  in1=proj[:, c, T:NT], op0=ALU.mult, op1=ALU.subtract)
                inc(last, "pool_diff")
                for c in range(PCH):
                    b = full(v, f"pool{c}")
                    freed(v.tensor_scalar(mixT[:, c, :], b[:, 0:NT], constT[:, R_PS + c:R_PS + c + 1], None, ALU.mult),
                          f"pool{c}")


            def convolve(_):
                v.wait_ge(sem("proj_out"), out_count(CV0 + CVN - 1))
                for c in range(CVN):
                    last = v.tensor_scalar(cv[:, c, :], proj[:, CV0 + c, :], cw(NCV, c), None, ALU.mult)
                step(last)
                for i in range(NCV):
                    back = NCV - i
                    for c in range(CVN):
                        v.scalar_tensor_tensor(out=cv[:, c, back:T], in0=proj[:, CV0 + c, 0:T - back], scalar=cw(i, c),
                                               in1=cv[:, c, back:T], op0=ALU.mult, op1=ALU.add)
                        last = v.scalar_tensor_tensor(out=cv[:, c, T:NT], in0=cext[:, c, i:NS * NCV:NCV], scalar=cw(i, c),
                                                      in1=cv[:, c, T:NT], op0=ALU.mult, op1=ALU.add)
                    if i < NCV - 1:
                        step(last)
                inc(last, "conv_done")


            def decays(_):
                b = full(v, "ba")
                v.wait_ge(sem("gcol_in"), 32)
                v.tensor_scalar(ab[:, 0, :], b[0:GH, 0:NT], -1.0, None, ALU.mult)
                freed(v.tensor_scalar(ab[:, 3, :], b[32:32 + GH, 0:NT], gcol[:, 1:2], None, ALU.add), "ba")
                v.wait_ge(bank_free[2], frees_at("ba"))
                step(v.tensor_scalar(ab[:, 1, :], ab[:, 3, :], 0.0, None, ALU.max))
                inc(v.scalar_tensor_tensor(out=ab[:, 4, :], in0=ab[:, 3, :], scalar=0.5, in1=ab[:, 1, :],
                                           op0=ALU.mult, op1=ALU.subtract), "ab_in")
                v.wait_ge(sem("ab_exp"), 1)
                step(v.tensor_scalar(ab[:, 0, :], ab[:, 0, :], 1.0, None, ALU.add))
                step(v.reciprocal(ab[:, 0, :], ab[:, 0, :]))
                step(tt(ab[:, 1, :], ab[:, 1, :], ab[:, 4, :], ALU.add))
                step(v.tensor_scalar(gcol[:, 3:4], gcol[:, 2:3], -1.0, None, ALU.mult))
                inc(v.tensor_scalar(ab[:, 1, :], ab[:, 1, :], gcol[:, 3:4], None, ALU.mult), "ab_g")


            def key_norm(_):
                v.wait_ge(sem("rootd"), 4)
                step(v.reciprocal(rbc[:, :, :], rbc[:, :, :]))
                qk = cv[:, 0:2 * GC, :].rearrange("p c t -> p (c t)")
                step(tt(qk, qk, rbc[:, :, :].rearrange("p c t -> p (c t)"), ALU.mult))
                inc(v.tensor_scalar(cv[:, 0:GC, :], cv[:, 0:GC, :], float(DK) ** -0.5, None, ALU.mult), "qk_d")

            def dn_heads(_):
                b = full(v, "gn")
                freed(v.tensor_copy(gn[:, :, :, :].rearrange("p n w h -> p (n w h)"), b[:, 0:4 * GH]), "gn")
                v.wait_ge(bank_free[4], frees_at("gn"))
                v.sem_inc(sem("gn_out"), 1)
                for c in range(GC):
                    b = full(v, f"bbc{c}")
                    v.tensor_copy(bgs[:, 0, c, :], b[:, T:NT])
                    v.tensor_copy(bgs[:, 1, c, :], b[:, NT:NT + NS])
                    freed(tt(kbT[:, c, :], cv[:, GC + c, 0:T], b[:, 0:T], ALU.mult), f"bbc{c}")
                v.wait_ge(bank_free[6], frees_at("bbc1"))
                v.sem_inc(sem("kbT"), 1)
                for n in range(TT):
                    last = tt(P1[:, n, :, :], bc(triu[:, :].unsqueeze(1), [P, GH, P]),
                              bc(gn[:, n, 1, :].unsqueeze(2), [P, GH, P]), ALU.mult)
                inc(last, "ug")

            def dn_cumulate(_):
                b = full(v, "gcum")
                freed(v.tensor_copy(gs[:, 0:2, :].rearrange("p a h -> p (a h)"), b[:, 0:4 * GH]), "gcum")
                v.wait_ge(bank_free[7], frees_at("gcum"))
                inc(tt(gs[:, 3, :], gs[:, 1, :], gs[:, 0, :], ALU.subtract), "gs_in")

            def dn_spread(_):
                for n in range(TT):
                    b = full(v, f"gbc{n}")
                    if n:
                        v.wait_ge(bank_free[5], frees_at("gbc1") - 1)
                    freed(tt(DT[:, n, :, :], b[:, :].rearrange("p (h i) -> p h i", h=GH),
                             bc(gs[:, 0, n * GH:(n + 1) * GH].unsqueeze(2), [P, GH, P]), ALU.subtract), f"gbc{n}")
                v.wait_ge(bank_free[4], frees_at("gbc0"))
                v.wait_ge(bank_free[5], frees_at("gbc1"))
                inc(v.tensor_scalar(DT[:, :, :, :], DT[:, :, :, :], 0.0, None, ALU.min), "decay_in")

            def dn_rows(_):
                v.wait_ge(sem("gs_exp"), 1)
                for n in range(TT):
                    last = tt(gs[:, 6, n * GH:(n + 1) * GH], gs[:, 2, n * GH:(n + 1) * GH], gn[:, n, 0, :], ALU.mult)
                step(last)
                b = full(v, "dn_rows0")
                rows_v = b[:, :].rearrange("p (n d) -> p n d", d=DK)
                tt(kbg[:, :, :].rearrange("p n (h d) -> p (n h) d", d=DK), rows_v,
                   bc(gs[:, 6, :].unsqueeze(2), [P, TT * GH, DK]), ALU.mult)
                freed(tt(kd[:, :, :].rearrange("p n (h d) -> p (n h) d", d=DK), rows_v,
                         bc(gs[:, 3, :].unsqueeze(2), [P, TT * GH, DK]), ALU.mult), "dn_rows0")
                b = full(v, "dn_rows1")
                for n in range(TT):
                    last = tt(vb[:, n, :].rearrange("p (h d) -> p h d", d=DV),
                              b[:, n * GH * DV:(n + 1) * GH * DV].rearrange("p (h d) -> p h d", d=DV),
                              bc(gn[:, n, 0, :].unsqueeze(2), [P, GH, DV]), ALU.mult)
                freed(last, "dn_rows1")
                v.wait_ge(bank_free[7], frees_at("dn_rows1"))
                v.sem_inc(sem("dn_scaled"), 1)

            def dn_products(_):
                v.wait_ge(sem("decay_exp"), 1)
                for n in range(TT):
                    last = tt(DT[:, n, :, :], DT[:, n, :, :], bc(triu[:, :].unsqueeze(1), [P, GH, P]), ALU.mult)
                step(last)
                for h2 in range(2):
                    for w, dst in enumerate((MT, AT)):
                        b = full(v, f"kk{w}{h2}")
                        freed(tt(halves(dst, h2), b[:, :].rearrange("p (n c i) -> p n c i", n=TT, c=GC), halves(DT, h2),
                                 ALU.mult), f"kk{w}{h2}")
                v.wait_ge(bank_free[7], frees_at("kk11"))

                for n in range(TT):
                    step(level(0, n))
                    inc(tt(Tt[:, n, :, :], bc(ident[:, :].unsqueeze(1), [P, GH, P]), BT[:, n, :, :], ALU.subtract), "Tt")
                    v.wait_ge(sem("Tt"), n + 1)
                for n in range(TT):
                    inc(level(1, n), "BT")

            def dn_values(_):
                b = full(v, "u0")
                freed(v.tensor_copy(vn[:, 0, :], b[:, 0:GH * DV]), "u0")
                v.wait_ge(bank_free[6], frees_at("u0"))
                v.sem_inc(sem("vn"), 1)
                b = full(v, "u1")
                freed(v.tensor_copy(vn[:, 1, :], b[:, 0:GH * DV]), "u1")
                v.wait_ge(bank_free[7], frees_at("u1"))

            def dn_state(_):
                b = full(v, "state1")
                freed(v.tensor_copy(S1[:, :, :], b[:, 0:GC * DV].rearrange("p (c v) -> p c v", c=GC)), "state1")
                v.wait_ge(bank_free[5], frees_at("state1"))
                v.sem_inc(sem("S1"), 1)

            def dn_carry(_):
                for h2 in range(2):
                    b = full(v, f"kcS{h2}")
                    own = vn[:, 1, :].rearrange("p (c w d) -> p w c d", w=2, d=DV)[:, h2, :, :]
                    freed(tt(own, own, b[:, 0:GC * DV].rearrange("p (c d) -> p c d", c=GC), ALU.subtract), f"kcS{h2}")
                v.wait_ge(bank_free[7], frees_at("kcS1"))
                v.sem_inc(sem("vn"), 1)

            def dn_out(_):
                b = full(v, "state2")
                for h in range(GH):
                    c, r = h // 2, 64 * (h % 2)
                    last = v.scalar_tensor_tensor(out=S2[r:r + 64, c, :], in0=S1[r:r + 64, c, :],
                                                  scalar=gs[r:r + 64, 4, GH + h:GH + h + 1],
                                                  in1=b[r:r + 64, c * DV:(c + 1) * DV], op0=ALU.mult, op1=ALU.add)
                freed(last, "state2")
                v.wait_ge(bank_free[4], frees_at("state2"))
                v.sem_inc(sem("S2_done"), 1)
                b = full(v, "oT")
                freed(v.tensor_copy(pdT[:, :, 0:T], b[:, :].rearrange("p (c t) -> p c t", c=GC)), "oT")


            def step_old(_):
                b = full(v, "kS")
                kSv = b[:, 0:GC * NS].rearrange("p (c q) -> p c q", c=GC)
                freed(tt(sv[:, 0, :, :], kSv, bgs[:, 1, :, :], ALU.mult), "kS")
                v.wait_ge(bank_free[6], frees_at("kS"))
                step(tt(sv[:, 1, :, :], cv[:, 2 * GC:3 * GC, T:NT], sv[:, 0, :, :], ALU.subtract))
                step(tt(sv[:, 0, :, :], sv[:, 1, :, :], bgs[:, 0, :, :], ALU.mult))
                vd = P1[:, :, :, :].rearrange("p n h i -> p (n h i)").rearrange("p (q c w) -> p q c w", q=NS, c=GC)
                for c in range(GC):
                    last = tt(vd[:, :, c, :], bc(i64[:, :].unsqueeze(1), [P, NS, DV]),
                              bc(sv[:, 0, c, :].unsqueeze(2), [P, NS, DV]), ALU.mult)
                inc(last, "vdiag")
                for c in range(GC):
                    tt(Ss[:, :, c, :], Ss[:, :, c, :], bc(bgs[:, 1, c, :].unsqueeze(2), [P, NS, DV]), ALU.mult)

            def step_spread(_):
                for n in range(2):
                    b = full(v, f"vbc{n}")
                    hq = NS // 2
                    for c in range(GC):
                        last = tt(Sx[:, n * hq:(n + 1) * hq, c, :],
                                  b[:, :].rearrange("p (q c w) -> p q c w", q=hq, c=GC)[:, :, c, :],
                                  bc(cv[:, GC + c, T + n * hq:T + (n + 1) * hq].unsqueeze(2), [P, hq, DV]), ALU.mult)
                    freed(last, f"vbc{n}")
                v.wait_ge(bank_free[7], frees_at("vbc1"))
                inc(tt(x_nat[:, 0, :], x_nat[:, 0, :], x_nat[:, 1, :], ALU.add), "Snew")

            def step_new(_):
                b = full(v, "qS")
                freed(v.tensor_copy(pdT[:, :, T:NT], b[:, 0:GC * NS].rearrange("p (c q) -> p c q", c=GC)), "qS")
                v.wait_ge(bank_free[4], frees_at("qS"))
                v.sem_inc(sem("o_done"), 1)

            def out_norm(_):
                v.wait_ge(sem("rooto"), 2)
                step(v.reciprocal(rbc[:, 0:GC, :], rbc[:, 0:GC, :]))
                step(v.scalar_tensor_tensor(out=pdT[:, :, :].rearrange("p c t -> p (c t)"),
                                            in0=pdT[:, :, :].rearrange("p c t -> p (c t)"),
                                            scalar=constT[:, R_Q + 2:R_Q + 3],
                                            in1=rbc[:, 0:GC, :].rearrange("p c t -> p (c t)"), op0=ALU.mult, op1=ALU.mult))
                v.wait_ge(sem("z_silu"), 1)
                step(tt(mixT[:, PCH + AC:DC, :], pdT[:, :, :], proj[:, Z0:Z0 + GC, :], ALU.mult))


            def own_scores(_):
                step(tt(prod[0:NS, 0:AW], nat8[:, 0, :], nat8[:, 1, :], ALU.mult))
                step(v.tensor_reduce(own8[:, 0, 0:H], prod[0:NS, 0:AW].rearrange("p (h d) -> p h d", d=HD), AX, ALU.add))
                inc(tt(own8[:, 1, :].rearrange("p (q h) -> p q h", h=H), bc(ident[0:NS, 0:NS].unsqueeze(2), [NS, NS, H]),
                       bc(own8[:, 0, 0:H].unsqueeze(1), [NS, NS, H]), ALU.mult), "own_diag")
                b = full(v, "own")
                freed(v.tensor_copy(sm64[:, 2, :, :].rearrange("p q h -> p (q h)"), b[:, 0:NS * H]), "own")
                b = full(v, "gsum")
                freed(v.tensor_reduce(g4, b[:, :].rearrange("p (n t h) -> p n h t", t=PPB, h=H), AX, ALU.add), "gsum")
                v.wait_ge(bank_free[7], frees_at("gsum"))
                step(v.memset(cnt4[:, :, :, :], 0.0))
                for n in range(NB):
                    for m in range(NB):
                        if m != n:
                            step(tt(cmp1[:, :, :], gate4[:, :, m, :], gate4[:, :, n, :], ALU.is_ge if m < n else ALU.is_gt))
                            step(tt(cnt4[:, :, n, :], cnt4[:, :, n, :], cmp1[:, :, :], ALU.add))
                step(v.tensor_scalar(g4, c4, float(min(TOPK, NB + 1)), None, ALU.is_lt))
                step(v.tensor_scalar(c4, g4, FAR, -FAR, ALU.mult, ALU.add))
                b = full(v, "sT")
                freed(v.tensor_reduce(tokmax[:, :], b[:, :].rearrange("p (n t) -> p n t", n=4), AX, ALU.max), "sT")
                v.wait_ge(bank_free[4], frees_at("sT"))
                v.wait_ge(sem("tails_out"), 64)
                for n in range(4):
                    last = v.tensor_scalar(w_a[:, n * P:(n + 1) * P], ident[:, :], tokmax[:, n:n + 1], None, ALU.mult)
                inc(last, "max_diag")

            def spread_max(_):
                b = full(v, "pmax")

                freed(tt(paged(w_b), paged(b[:, :]), bc(c4.unsqueeze(2), [P, NS * NB, PPB, H]), ALU.add), "pmax")
                v.wait_ge(bank_free[5], frees_at("pmax"))
                step(v.tensor_reduce(sm64[:, 0, :, :], queried(w_b).rearrange("p q n h -> p q h n"), AX, ALU.max))
                step(tt(sm64[:, 1, :, :], sm64[:, 0, :, :], sm64[:, 2, :, :], ALU.max))
                tt(sm64[:, 3, :, :], sm64[:, 2, :, :], sm64[:, 1, :, :], ALU.subtract)
                step(tt(queried(w_b), queried(s_all[:, :]), bc(sm64[:, 1, :, :].unsqueeze(2), [P, NS, NPG, H]), ALU.subtract))
                inc(v.tensor_scalar(w_b, w_b, 0.0, None, ALU.min), "shifted")

            def denominators(_):
                v.wait_ge(sem("rooto"), 2)
                step(v.memset(prod[:, :], 0.0))
                v.wait_ge(sem("exp8"), 1)
                inc(tt(paged(w_b), paged(w_b), bc(g4.unsqueeze(2), [P, NS * NB, PPB, H]), ALU.mult), "exps")
                b = full(v, "den")
                freed(v.tensor_reduce(sm64[:, 4, :, :], queried(b[:, :]).rearrange("p q n h -> p q h n"), AX, ALU.add), "den")
                v.wait_ge(bank_free[6], frees_at("den"))
                step(tt(sm64[:, 4, :, :], sm64[:, 4, :, :], sm64[:, 3, :, :], ALU.add))
                step(v.reciprocal(sm64[:, 4, :, :], sm64[:, 4, :, :]))
                tt(sm64[:, 5, :, :], sm64[:, 3, :, :], sm64[:, 4, :, :], ALU.mult)
                inc(tt(pP.rearrange("p (q n) m -> p q n m", q=NS)[:, :, :, 0:H], queried(w_b),
                       bc(sm64[:, 4, :, :].unsqueeze(2), [P, NS, NPG, H]), ALU.mult), "p_ready")

            def page_values(q):
                b = full(v, f"pv{q}")
                if q == 0:
                    v.wait_ge(sem("krow_out"), 32)
                if q >= 2:
                    v.wait_ge(sem("folded"), q - 1)
                freed(tt(stg[:, q % 2, :].rearrange("p (h d) -> p h d", d=HD), b[:, :].rearrange("p (h d) -> p h d", d=HD),
                         bc(dm8[:, :].unsqueeze(2), [P, H, HD]), ALU.mult), f"pv{q}")
                v.wait_ge(bank_free[4 + q % 2], frees_at(f"pv{q}"))
                v.sem_inc(sem("pv_masked"), 1)

            def page_end(_):
                b = full(v, "y8")
                freed(v.tensor_copy(w_a, b[:, :]), "y8")
                v.wait_ge(bank_free[6], frees_at("y8"))
                v.sem_inc(sem("y8_out"), 1)
                b = full(v, "yT8")
                for c in range(AC):
                    last = v.tensor_reduce(mixT[:, PCH + c, T:NT],
                                           b[:, c * P:(c + 1) * P].rearrange("p (g r) -> p r g", g=4)[:, 0:NS, :], AX, ALU.add)
                freed(last, "yT8")
                v.wait_ge(bank_free[7], frees_at("yT8"))
                own_v = w_b[:, 0:AC * NS].rearrange("p (c q) -> p c q", c=AC)
                for h2 in range(2):
                    r = slice(64 * h2, 64 * h2 + 64)
                    last = tt(own_v[r, :, :], proj[r, VC0:VC0 + AC, T:NT],
                              sm64[r, 5, :, :].rearrange("p q (c w) -> p w c q", w=2)[:, h2, :, :], ALU.mult)
                step(last)
                inc(tt(mixT[:, PCH:PCH + AC, T:NT], mixT[:, PCH:PCH + AC, T:NT], own_v, ALU.add), "mix")


            go = {
                "QSUM": lambda _: head_norm("rootq", QC0, R_Q, "q_done"), "KSUM": lambda _: head_norm("rootk", KC0, R_Q + 1, "k_done"),
                "QR": lambda _: rows8("q8", 0, "q_rows8"), "KR": lambda _: rows8("k8", 1, "k_rows8"),
                "VR": lambda _: rows8("v8", 2, "v_rows8"), "K": scores, "CEXT": cached_rows, "CONV": convolve, "AB": decays,
                "DSUM": key_norm, "GN": dn_heads, "GC": dn_cumulate, "GBC": dn_spread, "ROWS": dn_rows, "KK": dn_products,
                "M": outer, "S": att_first, "H": att_head, "HE": lambda _: att_take(H // 2 - 1), "POOL": pool_maps,
                "UA": dn_values, "UB": dn_state, "UC": dn_carry, "UD": dn_out, "XA": step_old, "XB": step_spread,
                "XC": step_new, "XD": out_norm, "OWN": own_scores, "DMAX": spread_max, "DEXP": denominators,
                "A": mod_reduce, "V": page_values, "VE": page_end,
            }
            for st, n in ORDER:
                if st in go:
                    go[st](n)

            def residual(name, j, gate, done):
                b = full(v, name)
                m = gate * DC + j
                v.scalar_tensor_tensor(out=xT[:, j, 0:T], in0=b[:, 0:T], scalar=modT[:, m, 0:1], in1=xT[:, j, 0:T],
                                       op0=ALU.mult, op1=ALU.add)
                freed(tt(sv[:, 0, 0, :], b[:, T:NT], modT[:, m, 1:NC], ALU.mult), name)
                v.wait_ge(bank_free[filled[name][0]], frees_at(name))
                inc(tt(xT[:, j, T:NT], xT[:, j, T:NT], sv[:, 0, 0, :], ALU.add), done)
                v.wait_ge(sem(done), j + 1)

            for j in range(DC):
                residual(f"out{j}", j, 2, "x1")
            modulation(4, R_N2)
            norm_apply("root2", 3, "h2")
            for f in range(FC):
                v.wait_ge(sem("silu"), f + 1)
                b = full(v, f"up{f}")
                freed(tt(hid[:, f, :], rbc[:, f % 4, :], b[:, 0:NT], ALU.mult), f"up{f}")
                v.wait_ge(bank_free[filled[f"up{f}"][0]], frees_at(f"up{f}"))
                v.sem_inc(sem("hidden"), 1)
            for j in range(DC):
                residual(f"down{j}", j, 5, "x2")
            v.wait_ge(sem("states_out"), 64)
            for r in range(TT + 1):
                m = P if r < TT else NS
                for hlf in range(2):
                    b = full(v, f"y{r}{hlf}")
                    freed(v.tensor_copy(ynat[0:m, r, 512 * hlf:512 * hlf + 512], b[0:m, :]), f"y{r}{hlf}")
                    v.wait_ge(bank_free[filled[f"y{r}{hlf}"][0]], frees_at(f"y{r}{hlf}"))
                v.sem_inc(sem("y_rows"), 1)

        @block.scalar
        def _(a):
            step = order(a, "act_step")

            def inc(ins, name):
                ins.then_inc(sem(name), 1)

            for r in range(TT):
                a.dma_start(x_nat[:, r, :], x_prompt[0, r * P:(r + 1) * P, :]).then_inc(sem("x_in"), 16)
            a.dma_start(x_nat[0:NS, TT, :], x_sample[:, 0, :]).then_inc(sem("x_in"), 16)
            a.dma_start(gcol[:, 0:1], a_log.rearrange("o h -> h o")).then_inc(sem("gcol_in"), 16)
            a.dma_start(gcol[:, 1:2], dt_bias.rearrange("o h -> h o")).then_inc(sem("gcol_in"), 16)
            a.dma_start(wba[:, :, :], w_in[0].rearrange("(k p) n -> p k n", p=P)[:, :, PJ * P:]).then_inc(sem("wba_in"), 16)
            for g in range(2 * PCH):
                a.dma_start(poolw[64 * (g % 2):64 * (g % 2) + 64, g // 2, :], pool_w[0, g]).then_inc(sem("poolw_in"), 16)
            a.dma_start(cst[:, :], state_conv[0].rearrange("q t c -> (q t) c")).then_inc(sem("cst_in"), 16)
            a.dma_start(pbuf, state_pool[0].rearrange("q t c -> q (t c)")).then_inc(sem("pbuf_in"), 16)

            a.wait_ge(sem("c_in"), 32)
            inc(a.activation(c_nat, c_nat, ACT.Silu), "c_silu")
            for c in range(1, DC, 2):
                b = full(a, f"xT{c}")
                freed(a.activation(xT[:, c, :], b[:, 0:NT], ACT.Copy), f"xT{c}")
            a.wait_ge(bank_free[7], frees_at("xT7"))
            a.wait_ge(bank_free[5], frees_at("xT5"))
            a.wait_ge(bank_free[4], frees_at("xT4"))
            a.wait_ge(bank_free[6], frees_at("xT6"))
            inc(a.activation(hT[:, :, :], xT[:, :, :], ACT.Square), "sq1")

            def ada_rows(j):
                b = full(a, f"ada{j}")
                if j:
                    full(a, f"adaT{j - 1}")
                freed(a.activation(adaS[:, :], b[:, :], ACT.Copy), f"ada{j}")
                a.wait_ge(bank_free[3], frees_at(f"ada{j}"))
                a.sem_inc(sem("ada_rows"), 1)

            for j in range(2 * D // IW // 2):
                ada_rows(j)
            a.wait_ge(sem("cT_made"), 1)

            def roots(name, banks, scale, done):
                for c in range(banks):
                    nm = f"{name}{c}" if banks > 1 else name
                    b = full(a, nm)
                    freed(a.activation(rbc[:, c, :], b[:, 0:NT], ACT.Sqrt, bias=eps[:, 0:1], scale=scale), nm)
                    a.wait_ge(bank_free[filled[nm][0]], frees_at(nm))
                    a.sem_inc(sem(done), 1)

            roots("ss1", 1, 1.0 / D, "root1")

            def proj_out(item):
                for n in range(2):
                    j = 2 * item + n
                    b = full(a, f"proj{j}")
                    freed(a.activation(proj[:, j, :], b[:, 0:NT], ACT.Copy), f"proj{j}")
                    a.wait_ge(bank_free[n], frees_at(f"proj{j}"))
                    a.sem_inc(sem("proj_out"), 1)

            def q_copy(q):
                b = full(a, f"qb{q}")
                if q >= 2:
                    a.wait_ge(sem("k_scored"), q - 1)
                freed(a.activation(qb[:, q % 2, :], b[:, :], ACT.Copy), f"qb{q}")
                a.wait_ge(bank_free[2], frees_at(f"qb{q}"))
                a.sem_inc(sem("qb"), 1)

            def take(name, dst, rows_, cols, done):
                b = full(a, name)
                freed(a.activation(dst, b[0:rows_, 0:cols], ACT.Copy), name)
                a.wait_ge(bank_free[filled[name][0]], frees_at(name))
                a.sem_inc(sem(done), 1)

            def att_exp(h):
                a.wait_ge(sem("masked"), h + 1)
                a.activation(sm[:, h % 2, 0:P], sm[:, h % 2, 0:P], ACT.Exp, bias=st4[:, h % 2, 2:3], scale=SCALE,
                             accum_out=st4[:, h % 2, 4:5])
                inc(a.activation(sm[:, h % 2, P:3 * P], sm[:, h % 2, P:3 * P], ACT.Exp, bias=st4[:, h % 2, 3:4],
                                 scale=SCALE, accum_out=st4[:, h % 2, 5:6]), "exped")

            def att_pT(h):
                if h == 2:
                    a.wait_ge(sem("att_even"), 1)
                elif h > 2:
                    if h % 2:
                        full(a, f"O{(h - 2) // 2}")
                    else:
                        a.wait_ge(sem("att_even"), h // 2)
                b = full(a, f"PT{h}")
                freed(a.activation(pT[:, h % 2, :], b[:, 0:3 * P], ACT.Copy), f"PT{h}")
                a.wait_ge(bank_free[h % 2], frees_at(f"PT{h}"))
                a.sem_inc(sem("probsT"), 1)

            def project(item):
                proj_out(item)
                if item == (QC0 + AC - 1) // 2:
                    inc(a.activation(mixT[:, 0:AC, :], proj[:, QC0:QC0 + AC, :], ACT.Square), "q_sq")
                if item == (KC0 + AC - 1) // 2:
                    inc(a.activation(mixT[:, AC:2 * AC, :], proj[:, KC0:KC0 + AC, :], ACT.Square), "k_sq")

            def key_roots(_):
                a.wait_ge(sem("qk_d"), 1)
                roots("kss", 4, 1.0 / HD, "rootk")

            def dn_roots(_):
                a.wait_ge(sem("q_done"), 1)
                roots("dss", 4, 1.0, "rootd")

            def k_rows(_):
                for r in range(TT):
                    take(f"krow{r}", stg[:, r, :], P, AW, "k_rows")

            def v_rows(_):
                for r in range(TT):
                    take(f"vrow{r}", vnat[:, r, :], P, AW, "v_rows")

            def tails(_):
                a.wait_ge(sem("qdT"), 1)
                take("utail", utail[0:NBUF + NS, :], NBUF + NS, POOLW, "tails")
                for hlf in range(2):
                    take(f"ctail{hlf}", tail[0:NCV + NS, 384 * hlf:384 * hlf + 384], NCV + NS, 384, "tails")

            def conv_gates(_):
                a.wait_ge(sem("conv_done"), 1)
                a.activation(proj[:, Z0:Z0 + GC, :], proj[:, Z0:Z0 + GC, :], ACT.Silu).then_inc(sem("z_silu"), 1)
                step(a.activation(cv[:, :, :], cv[:, :, :], ACT.Silu))
                inc(a.activation(sq4, cv[:, 0:2 * GC, :], ACT.Square), "d_sq")

            def decays(_):
                a.wait_ge(sem("ab_in"), 1)
                a.activation(ab[:, 0, :], ab[:, 0, :], ACT.Exp)
                step(a.activation(ab[:, 4, :], ab[:, 4, :], ACT.Exp, scale=2.0))
                a.activation(gcol[:, 2:3], gcol[:, 0:1], ACT.Exp)
                inc(a.activation(ab[:, 4, :], ab[:, 4, :], ACT.Ln, bias=eps[0:GH, 1:2]), "ab_exp")
                a.wait_ge(sem("ab_g"), 1)
                inc(a.activation(ab[:, 2, :], ab[:, 1, :], ACT.Exp), "ab_done")

            def chunk_decays(_):
                a.wait_ge(sem("gs_in"), 1)
                a.activation(gs[:, 2, :], gs[:, 0, :], ACT.Exp)
                a.activation(gs[:, 3, :], gs[:, 3, :], ACT.Exp)
                inc(a.activation(gs[:, 4, :], gs[:, 1, :], ACT.Exp), "gs_exp")

            def decay_matrices(_):
                b = full(a, "gbc1")
                freed(a.activation(w_a, b[:, :], ACT.Exp), "gbc1")
                a.wait_ge(sem("decay_in"), 1)
                step(a.activation(DT[:, :, :, :], DT[:, :, :, :], ACT.Exp))
                a.sem_inc(sem("decay_exp"), 1)
                a.sem_inc(sem("ebc"), 1)

            def dn_first(_):
                for n in range(TT):
                    b = full(a, f"T0{n}")
                    freed(a.activation(Tn[:, n, :, :], b[:, :].rearrange("p (h i) -> p h i", h=GH), ACT.Copy), f"T0{n}")
                    a.wait_ge(bank_free[4 + n], frees_at(f"T0{n}"))
                    a.sem_inc(sem("Tn"), 1)

            def dn_inner(s):
                for n in range(TT):
                    b = full(a, f"P1{s}{n}")
                    freed(a.activation(P1[:, n, :, :], b[:, :].rearrange("p (h i) -> p h i", h=GH), ACT.Copy), f"P1{s}{n}")
                    a.wait_ge(bank_free[4 + n], frees_at(f"P1{s}{n}"))
                    a.sem_inc(sem("P1"), 1)

            def dn_values(_):
                b = full(a, "kc")
                freed(a.activation(kcT[:, :, :], b[:, 0:GC * P].rearrange("p (c i) -> p c i", c=GC), ACT.Copy), "kc")
                a.wait_ge(bank_free[4], frees_at("kc"))
                a.sem_inc(sem("kcT"), 1)

            def out_squares(_):
                a.wait_ge(sem("o_done"), 1)
                inc(a.activation(sq4[:, 0:GC, :], pdT[:, :, :], ACT.Square), "o_sq")

            def out_roots(_):
                a.wait_ge(sem("k_done"), 1)
                for c in range(GC):
                    b = full(a, f"oss{c}")
                    freed(a.activation(rbc[:, c, :], b[:, 0:NT], ACT.Sqrt, bias=eps[:, 0:1], scale=1.0 / DV), f"oss{c}")
                    a.wait_ge(bank_free[6 + c], frees_at(f"oss{c}"))
                    a.sem_inc(sem("rooto"), 1)

            def page_exps(_):
                a.wait_ge(sem("shifted"), 1)
                a.activation(sm64[:, 3, :, :], sm64[:, 3, :, :], ACT.Exp, scale=SCALE)
                inc(a.activation(w_b, w_b, ACT.Exp, scale=SCALE), "exp8")

            def att_head(h):
                if h + 1 < H:
                    att_exp(h + 1)
                att_pT(h)

            go = {
                "W": project, "QSUM": lambda _: roots("qss", 4, 1.0 / HD, "rootq"), "KSUM": key_roots, "DSUM": dn_roots,
                "QB": q_copy, "KROW": k_rows, "VROW": v_rows, "TAILS": tails, "CONV": conv_gates, "AB": decays,
                "GC": chunk_decays, "GBC": decay_matrices, "TI": dn_first, "L": dn_inner, "UA": dn_values,
                "XC": out_squares, "XD": out_roots, "S": lambda _: att_exp(0), "H": att_head, "A": ada_rows,
                "DMAX": page_exps,
            }
            for st, n in ORDER:
                if st in go:
                    go[st](n)

            a.wait_ge(sem("x1"), DC)
            inc(a.activation(hT[:, :, :], xT[:, :, :], ACT.Square), "sq2")
            roots("ss2", 1, 1.0 / D, "root2")
            for f in range(FC):
                b = full(a, f"gate{f}")
                if f >= 4:
                    a.wait_ge(sem("hidden"), f - 3)
                if f == 0:
                    a.wait_ge(sem("h2"), 1)
                freed(a.activation(rbc[:, f % 4, :], b[:, 0:NT], ACT.Silu), f"gate{f}")
                a.wait_ge(bank_free[filled[f"gate{f}"][0]], frees_at(f"gate{f}"))
                a.sem_inc(sem("silu"), 1)

        @block.gpsimd
        def _(g):
            step = order(g, "pool_step")

            def zeros(ap):
                step(g.memset(ap, 0.0))

            def diagonal(ap, base, pattern):
                return g.affine_select(out=ap, in_=ap, compare_op=ALU.not_equal, fill=1.0, base=base, pattern=pattern,
                                       channel_multiplier=1)

            zeros(ident[:, :])
            step(diagonal(ident[:, :], 0, [[-1, P]]))
            g.sem_inc(sem("ident_made"), 1)
            step(g.memset(ones[:, :], 1.0))
            step(g.memset(blk[:, :], 0.0))
            step(g.memset(selc[:, :, :], 0.0))
            step(g.memset(dm8[:, :], 0.0))
            step(g.memset(i64[:, :], 0.0))
            step(g.memset(selh[:, :, :], 0.0))
            step(g.memset(triu[:, :], 1.0))
            step(g.memset(cmask[:, :, :], 0.0))
            zeros(lvl[:, :, :])
            step(g.memset(blk[0:64, 0:64], 1.0))
            step(g.memset(blk[64:P, 64:P], 1.0))
            step(diagonal(i64[:, :], 0, [[-1, HD]]))
            for q in range(4):
                step(diagonal(dm8[:, :], -32 * q, [[-1, H]]))
            step(diagonal(i64[:, :], -64, [[-1, HD]]))
            step(g.affine_select(out=selc[:, :, :], in_=selc[:, :, :], compare_op=ALU.not_equal, fill=1.0, base=0,
                                 pattern=[[1, NS], [-1, 32]], channel_multiplier=0))
            step(g.affine_select(out=selh[:, :, :].rearrange("p c (w d) -> p c w d", w=2),
                                 in_=selh[:, :, :].rearrange("p c (w d) -> p c w d", w=2), compare_op=ALU.not_equal,
                                 fill=1.0, base=0, pattern=[[-2, GC], [-1, 2], [0, DK]], channel_multiplier=1))
            step(g.affine_select(out=triu[:, :], in_=triu[:, :], compare_op=ALU.is_ge, fill=0.0, base=0,
                                 pattern=[[1, P]], channel_multiplier=-1))
            for n in (0, 2):
                step(g.affine_select(out=cmask[:, n, :], in_=cmask[:, n, :], compare_op=ALU.is_ge, fill=-FAR, base=0,
                                     pattern=[[-1, P]], channel_multiplier=1))
            for s in range(7):
                w = 1 << s
                part = lvl[:, s, :].rearrange("p (a b c) -> p a b c", b=2, c=w)[:, :, 1, :]
                step(g.memset(part, 1.0))
                step(g.affine_select(out=part, in_=part, compare_op=ALU.is_ge, fill=0.0, base=0,
                                     pattern=[[-2 * w, P // (2 * w)], [0, w]], channel_multiplier=1))
                step(g.affine_select(out=part, in_=part, compare_op=ALU.is_ge, fill=0.0, base=w - 1,
                                     pattern=[[2 * w, P // (2 * w)], [0, w]], channel_multiplier=-1))
            g.sem_inc(sem("masks_made"), 1)
            cnt_i = prod[:, 0:T].bitcast(I32)
            step(g.iota(cnt_i, pattern=[[1, T]], base=1, channel_multiplier=0))
            for c in range(PCH):
                step(g.tensor_copy(rcnt[:, c, :], cnt_i))
            g.sem_inc(sem("iota_made"), 1)

            outs = [0]

            def store(dst, src):
                outs[0] += 1
                g.dma_start(dst, src).then_inc(sem("stored"), 16)

            g.dma_start(pool_sample[0, :, 0:NBUF - 1, :], state_pool[0, :, 1:NBUF, :]).then_inc(sem("stored"), 16)
            g.dma_start(conv_sample[0, :, 0:NCV - 1, :], state_conv[0, :, 1:NCV, :]).then_inc(sem("stored"), 16)
            outs[0] += 2
            g.wait_ge(sem("ebc"), 1)
            g.wait_ge(sem("qk_d"), 1)
            ebc = w_a
            for h in range(GH):
                c, r = h // 2, slice(64 * (h % 2), 64 * (h % 2) + 64)
                step(g.tensor_tensor(qdT[r, c, :], cv[r, c, P:T], ebc[r, h * P:(h + 1) * P], ALU.mult))
            g.sem_inc(sem("qdT"), 1)
            g.wait_ge(sem("k_rows"), 2)
            for r in range(TT):
                g.dma_start(k_prompt[0, 0, r * P:(r + 1) * P].rearrange("t h d -> t (h d)"), stg[:, r, :])\
                 .then_inc(sem("krow_out"), 16)
            g.wait_ge(sem("v_rows"), 2)
            for r in range(TT):
                store(v_prompt[0, 0, r * P:(r + 1) * P].rearrange("t h d -> t (h d)"), vnat[:, r, :])
            g.wait_ge(sem("k_rows8"), 1)
            g.wait_ge(sem("v_rows8"), 1)
            store(k_sample[0, :, 0].rearrange("q h d -> q (h d)"), nat8[:, 1, :])
            store(v_sample[0, :, 0].rearrange("q h d -> q (h d)"), nat8[:, 2, :])
            g.wait_ge(sem("proj_out"), out_count(PCH - 1))
            g.wait_ge(sem("rcnt_made"), 1)
            g.wait_ge(sem("cT_made"), 1)

            def add_back(dst, src, d):
                step(g.tensor_copy(dst[:, 0:d], src[:, 0:d]))
                step(g.tensor_tensor(dst[:, d:T], src[:, d:T], src[:, 0:T - d], ALU.add))

            for c in range(PCH):
                src, at = proj[:, c, 0:T], 0
                w = 1
                while w < WINDOWS[2 * c + 1]:
                    dst = (pw1, pw2)[at % 2]
                    add_back(dst, src, w)
                    w *= 2
                    at += 1
                    src = dst
                    for gg in range(2):
                        if WINDOWS[2 * c + gg] == w:
                            r = slice(64 * gg, 64 * gg + 64)
                            step(g.tensor_tensor(pdT[r, c, 0:T], src[r, :], rcnt[r, c, :], ALU.mult))
                            step(g.tensor_tensor(pdT[r, c, 0:T], pdT[r, c, 0:T], proj[r, c, 0:T], ALU.subtract))
            g.sem_inc(sem("pool_prompt_done"), 1)
            g.wait_ge(sem("tails"), 3)
            for dst, src in ((pool_prompt[0, 0], utail[0:NBUF, :]), (pool_sample[0, :, NBUF - 1, :], utail[NBUF:NBUF + NS, :]),
                             (conv_prompt[0, 0], tail[0:NCV, :]), (conv_sample[0, :, NCV - 1, :], tail[NCV:NCV + NS, :])):
                g.dma_start(dst, src).then_inc(sem("tails_out"), 16)
            g.wait_ge(sem("S2_done"), 1)
            for c in range(GC):
                store(delta_prompt[0, 0].rearrange("(c w) k n -> c (w k) n", w=2)[c], S2[:, c, :])
            g.wait_ge(sem("Snew"), 1)
            for c in range(GC):
                for w in range(2):
                    g.dma_start(delta_sample[0, :, 2 * c + w].rearrange("q k n -> k q n"),
                                Ss[64 * w:64 * w + 64, :, c, :]).then_inc(sem("states_out"), 16)
            for r in range(TT + 1):
                g.wait_ge(sem("y_rows"), r + 1)
                if r < TT:
                    store(y_prompt[0, r * P:(r + 1) * P, :], ynat[:, r, :])
                else:
                    store(y_sample[:, 0, :], ynat[0:NS, TT, :])
            g.wait_ge(sem("stored"), 16 * outs[0])
            g.wait_ge(sem("krow_out"), 32)
            g.wait_ge(sem("tails_out"), 64)
            g.wait_ge(sem("states_out"), 64)

        @block.sync
        def _(sp):
            sp.dma_start(c_nat[0:1, :], c_prompt).then_inc(sem("c_in"), 16)
            sp.dma_start(c_nat[1:NC, :], c_sample).then_inc(sem("c_in"), 16)
            for r, src, m in ((R_ADAB, ada_b, 6 * DC), (R_N1, norm1_w, DC), (R_N2, norm2_w, DC), (R_PS, pool_scale, PCH)):
                sp.dma_start(rows[r:r + m, :], src.rearrange("o (m p) -> (o m) p", p=P)).then_inc(sem("rows_in"), 16)
            sp.dma_start(rows[R_CW:R_Q, :], conv_w[0].rearrange("i (c p) -> (i c) p", p=P)).then_inc(sem("rows_in"), 16)
            for n, src in enumerate((q_norm_w, k_norm_w, dn_norm_w)):
                for w in range(2):
                    sp.dma_start(rows[R_Q + n:R_Q + n + 1, 64 * w:64 * w + 64], src).then_inc(sem("rows_in"), 16)
            sp.dma_start(table[:, :], page_table.rearrange("q n -> (q n)").unsqueeze(0)).then_inc(sem("table_in"), 16)
            cols = {"ada": ada_w, "win": w_in, "wout": w_out, "gate": w_gate, "up": w_up}
            held = [None] * RING
            loaded = False
            for it in stream:
                kind, i = it
                s = place[it][0]
                if held[s] is not None:
                    sp.wait_ge(*released[held[s]])
                held[s] = it
                dst = ring[:, s, :]
                if kind in cols:
                    sp.dma_start(dst.rearrange("p (k n) -> p k n", k=DC),
                                 cols[kind][0].rearrange("(k p) n -> p k n", p=P)[:, :, i * IW:(i + 1) * IW])\
                      .then_inc(slot_full[s], 16)
                elif kind == "down":
                    k0, k1 = DKT[i[1]]
                    sp.dma_start(dst[:, 0:(k1 - k0) * IW].rearrange("p (k n) -> p k n", n=IW),
                                 w_down[0, k0 * P:k1 * P].rearrange("(k p) n -> p k n", p=P)[:, :, i[0] * IW:(i[0] + 1) * IW])\
                      .then_inc(slot_full[s], 16)
                else:
                    if not loaded:
                        sp.wait_ge(sem("table_in"), 16)
                        loaded = True
                    cache = cache_k if kind == "k" else cache_v
                    for k in range(PGI):
                        at = i[0] * NPG + i[1] * PGI + k
                        page = sp.value_load(table[0:1, at:at + 1], min_val=0, max_val=NPHYS - 1)
                        sp.dma_start(dst[:, k * AW:(k + 1) * AW],
                                     cache[0, bass.ds(page, 1)].rearrange("o t h d -> (o t) (h d)"))\
                          .then_inc(slot_full[s], 16)
                if it == ("win", 6):
                    sp.wait_ge(sem("sq1"), 1)
                    for c in range(GC):
                        for w in range(2):
                            sp.dma_start(Ss[64 * w:64 * w + 64, :, c, :],
                                         state_delta[0, :, 2 * c + w].rearrange("q k n -> k q n")).then_inc(sem("S_in"), 16)


_INS = ['x_prompt', 'x_sample', 'cache_k', 'cache_v', 'state_pool', 'state_conv', 'state_delta', 'page_table',
        'c_prompt', 'c_sample', 'norm1_w', 'ada_w', 'ada_b', 'w_in', 'pool_w', 'pool_scale', 'q_norm_w', 'k_norm_w',
        'conv_w', 'a_log', 'dt_bias', 'dn_norm_w', 'w_out', 'norm2_w', 'w_gate', 'w_up', 'w_down']


def kernel(**inputs):
    import numpy as _np
    import concourse.bacc as _bacc
    from concourse import mybir as _mybir
    from concourse.bass_utils import run_bass_kernel_spmd as _run

    xp, xs, ck = inputs["x_prompt"].shape, inputs["x_sample"].shape, inputs["cache_k"].shape
    sp, sc, sd = (inputs[n].shape for n in ("state_pool", "state_conv", "state_delta"))
    outs = [xp, xs, (1, xp[0], xp[1], *ck[3:]), (1, xp[0], xp[1], *ck[3:]), (1, xs[0], xs[1], *ck[3:]),
            (1, xs[0], xs[1], *ck[3:]), (1, xp[0], *sp[2:]), sp, (1, xp[0], *sc[2:]), sc, (1, xp[0], *sd[2:]), sd]
    nc = _bacc.Bacc("TRN2", target_bir_lowering=False, num_devices=1)
    arrays, args = {}, []
    for name in _INS:
        a = _np.ascontiguousarray(inputs[name])
        arrays[f"in_{name}_dram"] = a
        args.append(nc.dram_tensor(f"in_{name}_dram", a.shape, _mybir.dt.from_np(a.dtype), kind="ExternalInput").ap())
    for i, shape in enumerate(outs):
        args.append(nc.dram_tensor(f"out_{i}_dram", shape, _mybir.dt.float32, kind="ExternalOutput").ap())
    build(nc, *args)
    r = _run(nc, [arrays], core_ids=[0])
    return tuple(r.results[0][f"out_{i}_dram"] for i in range(len(outs)))
```

```python
from contextlib import ExitStack

import concourse.bass as bass
from concourse import mybir

F32 = mybir.dt.float32
F32R = mybir.dt.float32r
I32 = mybir.dt.int32
ALU = mybir.AluOpType
ACT = mybir.ActivationFunctionType
AX = mybir.AxisListType.X
P = 128
EPS = 1e-6
FAR = 1.0e30
MOBA_BLOCK = 256
TOPK = 3
WINDOWS = (2, 4, 8, 16)
RING = 5
PARTS = 3
SLOT = 2048


def build(nc, x_prompt, x_sample, cache_k, cache_v, state_pool, state_conv, state_delta, page_table,
          c_prompt, c_sample, norm1_w, ada_w, ada_b, w_in, pool_w, pool_scale, q_norm_w, k_norm_w,
          conv_w, a_log, dt_bias, dn_norm_w, w_out, norm2_w, w_gate, w_up, w_down,
          y_prompt, y_sample, k_prompt, v_prompt, k_sample, v_sample, pool_prompt, pool_sample,
          conv_prompt, conv_sample, delta_prompt, delta_sample):
    _, T, D = x_prompt.shape
    NS = x_sample.shape[0]
    NPHYS, PAGE, H, HD = cache_k.shape[1:]
    NPG = page_table.shape[1]
    POOLW = state_pool.shape[3]
    NBUF = state_pool.shape[2]
    CW3 = state_conv.shape[3]
    NCV = state_conv.shape[2]
    GH, DK, DV = state_delta.shape[2:]
    DFF = w_gate.shape[2]
    NT = T + NS
    NC = 1 + NS
    DC = D // P
    TT = T // P
    AW = H * HD
    AC = AW // P
    PCH = POOLW // P
    GC = GH * DV // P
    QC0, KC0, VC0 = PCH, PCH + AC, PCH + 2 * AC
    CV0 = PCH + 3 * AC
    CVN = CW3 // P
    Z0 = CV0 + CVN
    PJ = Z0 + GC
    FC = DFF // P
    NB = NPG * PAGE // MOBA_BLOCK
    PPB = MOBA_BLOCK // PAGE
    SCALE = float(HD) ** -0.5
    assert T == 2 * P and T <= MOBA_BLOCK and PAGE == P and D == DC * P and HD == DK == DV == 64
    assert PJ * P + 2 * GH == w_in.shape[2] and PJ == FC and NS * NPG * H == 512 and AW == 512

    IW = SLOT // DC
    PGI = SLOT // AW
    HALVES = NPG // PGI
    stream = [("ada", i) for i in range(2 * D // IW)]
    NA = 6 * D // IW // 2
    ORDER = ("W1 W2 QSUM W7 QNORM QR W8 QB0 QB1 W9 CEXT K0 W10 CONV BA K1 AB DSUM W3 K2 DNORM W4 KSUM GN K3 GC W5 "
             "KNORM GBC KR QB2 K4 ROWS KK W6 K5 TI VR QB3 L1 KROW W0 K6 M1 VROW L2 K7 M2 QB4 TAILS L3 S K8 M3 H0 K9 "
             "L4 QB5 M4 H1 A4 H2 L5 K10 M5 A5 QB6 POOL H3 K11 H4 L6 M6 K12 UA H5 UB A6 H6 UC K13 QB7 UD H7 A7 HE XA "
             "K14 XB A8 XC XD K15 A9 OWN A10 DMAX A11 DEXP V0 V1 V2 MX V3 V4 V5 V6 V7 VE").split()
    ORDER = [(st.rstrip("0123456789"), int("0" + st.lstrip("ABCDEFGHIJKLMNOPQRSTUVWXYZ"))) for st in ORDER]
    for st, n in ORDER:
        if st == "W":
            stream.append(("win", n))
        elif st == "A":
            stream += [("ada", 2 * n), ("ada", 2 * n + 1)]
        elif st == "K":
            stream.append(("k", (n // HALVES, n % HALVES)))
        elif st == "V":
            stream += [("v", (n, hf)) for hf in range(HALVES)]
    win_order = [n for st, n in ORDER if st == "W"]

    def out_count(j):
        return 2 * win_order.index(j // 2) + j % 2 + 1

    stream += [("wout", i) for i in range(D // IW)]
    for i in range(DFF // IW):
        stream += [("gate", i), ("up", i)]
    DKT = [(a, min(a + DC, FC)) for a in range(0, FC, DC)]
    stream += [("down", (i, j)) for i in range(D // IW) for j in range(len(DKT))]
    split = stream[stream.index(("wout", 0)):]
    place = {it: (n % RING, n // RING) for n, it in enumerate(stream)}

    ctx = ExitStack()
    with ctx:
        sb = lambda name, shape, dt=F32: ctx.enter_context(nc.sbuf_tensor(name, shape, dt))
        mixers = ExitStack()
        tmp = lambda name, shape, dt=F32: mixers.enter_context(nc.sbuf_tensor(name, shape, dt))
        sems = {}

        def sem(name):
            if name not in sems:
                sems[name] = ctx.enter_context(nc.semaphore(name))
            return sems[name]

        ring = sb("ring", [P, RING, SLOT])
        x_nat = sb("x_nat", [P, TT + 1, D])
        xT = sb("xT", [P, DC, NT])
        hT = sb("hT", [P, DC, NT])
        mixT = sb("mixT", [P, DC, NT])
        modT = sb("modT", [P, 6 * DC, NC])
        scA = sb("scA", [P, DC, NC])
        constT = sb("constT", [P, 96])
        rbc = sb("rbc", [P, 4, NT])
        ident = sb("ident", [P, P])
        ones = sb("ones", [P, P])
        nat8 = sb("nat8", [NS, 3, AW])
        vnat = sb("vnat", [P, TT, AW])
        eps = sb("eps", [P, 2])
        table = sb("table", [1, NS * NPG], I32)
        S2 = sb("S2", [P, GC, DV])
        sv = sb("sv", [P, 3, GC, NS])
        mats = tmp("mats", [P, 4, TT, GH, P])
        BTP1 = tmp("BTP1", [P, 2, TT, GH, P])
        c_nat = x_nat[32:32 + NC, TT, :]
        rows = tmp("rows", [P, P])
        R_ADAB, R_N1, R_N2 = 0, 6 * DC, 7 * DC
        R_PS = 8 * DC
        R_CW = R_PS + PCH
        R_Q = R_CW + (NCV + 1) * CVN
        NR = R_Q + 3
        proj = tmp("proj", [P, PJ, NT])
        cv = tmp("cv", [P, CVN, NT])
        cT = tmp("cT", [P, DC, 32])
        adaS = tmp("adaS", [P, 512])
        blk = tmp("blk", [P, P])
        i64 = tmp("i64", [P, HD])
        triu = tmp("triu", [P, P])
        lvl = tmp("lvl", [P, 7, P])
        cmask = tmp("cmask", [P, 3, P])
        sel8 = tmp("sel8", [2 * AC, AC, P])
        selh = sel8[0:GH, 0:GC, :]
        headsum = tmp("headsum", [P, AC, 2 * AC])
        selc = tmp("selc", [P, NS, 32])
        dm8 = tmp("dm8", [P, H])
        vn = tmp("vn", [P, TT, GH * DV])
        rcnt = tmp("rcnt", [P, PCH, T])
        wba = tmp("wba", [P, DC, 2 * GH])
        poolw = tmp("poolw", [P, PCH, 64])
        gcol = tmp("gcol", [GH, 4])
        stg = tmp("stg", [P, 2, AW])
        qb = tmp("qb", [P, 2, AW])
        prod = tmp("prod", [P, SLOT])
        s_all = tmp("s_all", [P, 512])
        pP = prod[:, :].rearrange("p (a m) -> p a m", m=32)
        w_ab = tmp("w_ab", [P, 1024])
        w_a, w_b = w_ab[:, 0:512], w_ab[:, 512:1024]
        gate4 = tmp("gate4", [P, NS, NB, H])
        cnt4 = tmp("cnt4", [P, NS, NB, H])
        g4, c4 = (m[:, :, :, :].rearrange("p q k h -> p (q k) h") for m in (gate4, cnt4))
        cmp1 = tmp("cmp1", [P, NS, H])
        sm64 = tmp("sm64", [P, 6, NS, H])
        own8 = tmp("own8", [NS, 2, 64])
        tokmax = tmp("tokmax", [P, 4])
        smpT = tmp("smpT", [P, 2, 2, 3 * P])
        sm, pT = smpT[:, 0, :, :], smpT[:, 1, :, :]
        st4 = tmp("st4", [P, 2, 8])
        ab = smpT[0:GH, :, :, :].rearrange("p a b c -> p (a b c)")[:, 0:5 * NT].rearrange("p (a t) -> p a t", a=5)
        gn = tmp("gn", [P, TT, 2, GH])
        gs = tmp("gs", [P, 8, TT * GH])
        vb = tmp("vb", [P, TT, GH * DV])
        kbkd = tmp("kbkd", [P, 2, TT, GH * DK])
        kbg, kd = kbkd[:, 0, :, :], kbkd[:, 1, :, :]
        kbT = w_b.rearrange("p (c t) -> p c t", c=GC)
        qdT = x_nat[:, TT, 2 * T:2 * T + GC * P].rearrange("p (c i) -> p c i", c=GC)
        DT, MT, Tn, Tt = (mats[:, n, :, :, :] for n in range(4))
        sq4 = mats[:, 2:4, :, :, :].rearrange("p a n h i -> p (a n h i)")[:, 0:AC * NT].rearrange("p (c t) -> p c t", c=AC)
        AT = DT
        BT, P1 = BTP1[:, 0, :, :, :], BTP1[:, 1, :, :, :]
        kcT = x_nat[:, TT, 2 * T + GC * P:2 * T + 2 * GC * P].rearrange("p (c i) -> p c i", c=GC)
        S1 = tmp("S1", [P, GC, DV])
        Ss = x_nat[:, 0, :].rearrange("p (b c v) -> p b c v", b=NS, c=GC)
        Sx = x_nat[:, 1, :].rearrange("p (b c v) -> p b c v", b=NS, c=GC)
        cst = kbkd[0:NS * NCV, :, :, :].rearrange("p a n d -> p (a n d)")[:, 0:CW3]
        cext = tmp("cext", [P, CVN, NS * NCV])
        pbuf = mats[0:NS, :, :, :, :].rearrange("p a n h i -> p (a n h i)")[:, 0:NBUF * POOLW]
        pd8 = vb[0:NS, :, :]
        pw1, pw2 = x_nat[:, TT, 0:T], x_nat[:, TT, T:2 * T]
        pdT = tmp("pdT", [P, PCH, NT])
        tail, utail = w_ab[0:32, 0:CW3], w_ab[0:32, CW3:CW3 + POOLW]
        ynat = x_nat
        bgs = tmp("bgs", [P, 2, GC, NS])
        mixers.close()
        a_hi = sb("a_hi", [P, DC, NT], F32R)
        a_lo = sb("a_lo", [P, DC, NT], F32R)
        w_hi = sb("w_hi", [P, PARTS, SLOT], F32R)
        w_lo = sb("w_lo", [P, PARTS, SLOT], F32R)
        hid_hi = sb("hid_hi", [P, FC, NT], F32R)
        hid_lo = sb("hid_lo", [P, FC, NT], F32R)
        hidden = sb("hidden_f", [P, 2, NT])
        bank = [ctx.enter_context(nc.psum_tensor(f"bank{i}", [P, 512], F32)) for i in range(8)]

        slot_full = [sem(f"slot_full{i}") for i in range(RING)]
        bank_full = [sem(f"bank_full{i}") for i in range(8)]
        bank_free = [sem(f"bank_free{i}") for i in range(8)]
        filled, freed_by, fills, frees = {}, {}, [0] * 8, [0] * 8

        counts, running = {}, [0] * RING
        for it in stream:
            s, _ = place[it]
            running[s] += 16 * (PGI if it[0] in "kv" else 1)
            counts[it] = running[s]

        def width(item):
            return SLOT if item[0] != "down" else (DKT[item[1][1]][1] - DKT[item[1][1]][0]) * IW

        def full_count(item):
            return counts[item]

        def arrived(eng, item):
            eng.wait_ge(slot_full[place[item][0]], full_count(item))
            return ring[:, place[item][0], :]

        released, singles = {}, {"pe_read": 0, "keys_read": 0, "w_split": 0, "part_read": 0}
        part_free = {}

        def used_up(ins, item, name):
            singles[name] += 1
            ins.then_inc(sem(name), 1)
            released[item] = (sem(name), singles[name])

        def read_by(name, item):
            b, n = filled[name]
            released[item] = (bank_full[b], n)

        def full(eng, name):
            b, n = filled[name]
            eng.wait_ge(bank_full[b], n)
            return bank[b]

        def freed(ins, name):
            ins.then_inc(bank_free[filled[name][0]], 1)

        def frees_at(name):
            return freed_by[name]

        def order(eng, name):
            n = [0]
            s = sem(name)

            def chain(ins):
                n[0] += 1
                ins.then_inc(s, 1)
                eng.wait_ge(s, n[0])
            return chain

        block = ctx.enter_context(nc.Block())

        @block.tensor
        def _(pe):
            def opened(name, b, readers=1):
                if frees[b]:
                    pe.wait_ge(bank_free[b], frees[b])
                fills[b] += 1
                frees[b] += readers
                assert name not in filled, name
                filled[name] = (b, fills[b])
                freed_by[name] = frees[b]
                return bank[b]

            def closed(ins, name):
                ins.then_inc(bank_full[filled[name][0]], 1)

            def mm(out, lhsT, rhs, start=True, stop=True):
                return pe.matmul(out, lhsT, rhs, start=start, stop=stop, skip_group_check=True)

            pe.wait_ge(sem("ident_made"), 1)
            pe.wait_ge(sem("rows_in"), 16 * 11)
            b = opened("rowsT", 2)
            closed(pe.transpose(b[:, 0:NR], rows[0:NR, :], ident[0:NR, 0:NR]), "rowsT")
            pe.wait_ge(sem("c_silu"), 1)
            b = opened("cT", 3)
            for c in range(DC):
                last = pe.transpose(b[:, c * NC:(c + 1) * NC], c_nat[:, c * P:(c + 1) * P], ident[32:32 + NC, 32:32 + NC])
            closed(last, "cT")
            pe.wait_ge(sem("x_in"), 16 * (TT + 1))
            for c in range(DC):
                b = opened(f"xT{c}", 4 + c % 4)
                for r in range(TT):
                    pe.transpose(b[:, r * P:(r + 1) * P], x_nat[:, r, c * P:(c + 1) * P], ident[:, :])
                closed(pe.transpose(b[:, T:NT], x_nat[0:NS, TT, c * P:(c + 1) * P], ident[0:NS, 0:NS]), f"xT{c}")

            def ada(j):
                b = opened(f"ada{j}", 3)
                for n in range(2):
                    slot = arrived(pe, ("ada", 2 * j + n)).rearrange("p (k n) -> p k n", k=DC)
                    for kk in range(2):
                        for g in range(4):
                            k = 2 * g + kk
                            last = mm(b[32 * g:32 * g + 32, n * IW:(n + 1) * IW], cT[:, k, :], slot[:, k, :],
                                      kk == 0, kk == 1)
                    if n == 0:
                        used_up(last, ("ada", 2 * j), "pe_read")
                closed(last, f"ada{j}")
                read_by(f"ada{j}", ("ada", 2 * j + 1))

            def ada_turn(j):
                pe.wait_ge(sem("ada_rows"), j + 1)
                b = opened(f"adaT{j}", 3)
                for n in range(4):
                    last = pe.transpose(b[:, n * P:(n + 1) * P], adaS[:, n * P:(n + 1) * P], ident[:, :])
                closed(last, f"adaT{j}")

            pe.wait_ge(sem("cT_made"), 1)
            pe.wait_ge(sem("masks_made"), 1)
            for j in range(2 * D // IW // 2):
                ada(j)
                ada_turn(j)

            def square_sums(name, ready, src):
                pe.wait_ge(sem(ready), 1)
                b = opened(name, 0)
                for c in range(DC):
                    last = mm(b[:, 0:NT], ones[:, :], src[:, c, :], c == 0, c == DC - 1)
                closed(last, name)

            square_sums("ss1", "sq1", hT)
            pe.wait_ge(sem("h1"), 1)

            def project(item):
                slot = arrived(pe, ("win", item)).rearrange("p (k n) -> p k n", k=DC)
                for n in range(2):
                    j = 2 * item + n
                    b = opened(f"proj{j}", n)
                    for k in range(DC):
                        last = mm(b[:, 0:NT], slot[:, k, n * P:(n + 1) * P], hT[:, k, :], k == 0, k == DC - 1)
                    closed(last, f"proj{j}")
                read_by(f"proj{j}", ("win", item))

            def head_sums(name, ready, src, b_):
                pe.wait_ge(sem(ready), 1)
                b = opened(name, b_)
                for c in range(AC):
                    last = mm(b[0:2 * AC, 0:NT], headsum[:, c, :], src(c), c == 0, c == AC - 1)
                closed(last, name)

            def head_spread(name, ready, row, banks):
                pe.wait_ge(sem(ready), 1)
                for c in range(AC):
                    b = opened(f"{name}{c}", banks[c % len(banks)])
                    closed(mm(b[:, 0:NT], sel8[:, c, :], rbc[0:2 * AC, row, :]), f"{name}{c}")

            def to_rows8(name, ready, c0, n=1):
                pe.wait_ge(sem(ready), n)
                b = opened(name, 2)
                for c in range(AC):
                    last = pe.transpose(b[0:NS, c * P:(c + 1) * P], proj[:, c0 + c, T:NT], ident[:, :])
                closed(last, name)

            def q_spread(b_):
                pe.wait_ge(sem("q_rows8"), 1)
                b = opened(f"qb{b_}", 2)
                closed(mm(b[:, :], ident[0:NS, b_:b_ + 1].to_broadcast([NS, P]), nat8[:, 0, :]), f"qb{b_}")

            def kv_rows(name, c0, ready, n):
                pe.wait_ge(sem(ready), n)
                for r in range(TT):
                    b = opened(f"{name}{r}", 2 + r)
                    for c in range(AC):
                        last = pe.transpose(b[:, c * P:(c + 1) * P], proj[:, c0 + c, r * P:(r + 1) * P], ident[:, :])
                    closed(last, f"{name}{r}")

            def decay_inputs():
                pe.wait_ge(sem("wba_in"), 16)
                b = opened("ba", 2)
                for k in range(DC):
                    mm(b[0:GH, 0:NT], wba[:, k, 0:GH], hT[:, k, :], k == 0, k == DC - 1)
                    last = mm(b[32:32 + GH, 0:NT], wba[:, k, GH:2 * GH], hT[:, k, :], k == 0, k == DC - 1)
                closed(last, "ba")

            def cached_rows():
                pe.wait_ge(sem("cst_in"), 16)
                b = opened("cext", 3)
                for c in range(CVN):
                    last = pe.transpose(b[:, c * NS * NCV:(c + 1) * NS * NCV], cst[:, c * P:(c + 1) * P],
                                        ident[0:NS * NCV, 0:NS * NCV])
                closed(last, "cext")
                pe.wait_ge(sem("pool_rows"), 1)
                b = opened("pdT8", 3)
                for c in range(PCH):
                    last = pe.transpose(b[:, c * NS:(c + 1) * NS], pd8[:, 0, c * P:(c + 1) * P], ident[0:NS, 0:NS])
                closed(last, "pdT8")

            def tails():
                pe.wait_ge(sem("proj_out"), PJ)
                b = opened("utail", 3)
                for c in range(PCH):
                    last = pe.transpose(b[0:NBUF + NS, c * P:(c + 1) * P], proj[:, c, T - NBUF:NT], ident[:, :])
                closed(last, "utail")
                for hlf in range(2):
                    b = opened(f"ctail{hlf}", 2 + hlf)
                    for c in range(3):
                        last = pe.transpose(b[0:NCV + NS, c * P:(c + 1) * P],
                                            proj[:, CV0 + 3 * hlf + c, T - NCV:NT], ident[:, :])
                    closed(last, f"ctail{hlf}")

            def pool_maps():
                pe.wait_ge(sem("pool_diff"), 1)
                pe.wait_ge(sem("poolw_in"), 16 * 2 * PCH)
                for c in range(PCH):
                    b = opened(f"pool{c}", 2 + c)
                    for g in range(2):
                        r = 64 * g
                        last = mm(b[r:r + 64, 0:NT], poolw[r:r + 64, c, :], pdT[r:r + 64, c, :])
                    closed(last, f"pool{c}")

            def att_scores(h):
                c, r = h // 2, 64 * (h % 2)
                b = opened(f"S{h}", h % 2)
                mm(b[:, 0:P], proj[r:r + 64, QC0 + c, 0:P], proj[r:r + 64, KC0 + c, 0:P])
                closed(mm(b[:, P:3 * P], proj[r:r + 64, QC0 + c, P:T], proj[r:r + 64, KC0 + c, 0:T]), f"S{h}")

            def att_turn(h):
                pe.wait_ge(sem("probs"), h + 1)
                b = opened(f"PT{h}", h % 2)
                for n in range(3):
                    last = pe.transpose(b[:, n * P:(n + 1) * P], sm[:, h % 2, n * P:(n + 1) * P], ident[:, :])
                closed(last, f"PT{h}")

            def att_out(h):
                pe.wait_ge(sem("probsT"), h + 1)
                c, r = h // 2, 64 * (h % 2)
                if h % 2 == 0:
                    opened(f"O{c}", 2)
                b = bank[2]
                mm(b[r:r + 64, 0:T], vnat[:, 0, h * HD:(h + 1) * HD], pT[:, h % 2, 0:2 * P], True, False)
                last = mm(b[r:r + 64, P:T], vnat[:, 1, h * HD:(h + 1) * HD], pT[:, h % 2, 2 * P:3 * P], False, True)
                if h % 2:
                    closed(last, f"O{c}")
                else:
                    last.then_inc(sem("att_even"), 1)

            def att_start():
                pe.wait_ge(sem("v_rows"), 2)
                pe.wait_ge(sem("k_done"), 1)
                att_scores(0)

            def att_head(h):
                if h + 1 < H:
                    att_scores(h + 1)
                att_turn(h)
                if h >= 1:
                    att_out(h - 1)

            def dn_heads():
                pe.wait_ge(sem("ab_done"), 1)
                b = opened("gn", 4)
                for n in range(TT):
                    for w in range(2):
                        o = (2 * n + w) * GH
                        last = pe.transpose(b[:, o:o + GH], ab[:, w, n * P:(n + 1) * P], ident[0:GH, 0:GH])
                closed(last, "gn")
                for c in range(GC):
                    b = opened(f"bbc{c}", 5 + c)
                    mm(b[:, 0:NT], selh[:, c, :], ab[:, 0, :])
                    closed(mm(b[:, NT:NT + NS], selh[:, c, :], ab[:, 2, T:NT]), f"bbc{c}")

            def dn_cumulate():
                pe.wait_ge(sem("gn_out"), 1)
                b = opened("gcum", 7)
                for n in range(TT):
                    mm(b[:, n * GH:(n + 1) * GH], triu[:, :], gn[:, n, 1, :])
                    last = mm(b[:, (TT + n) * GH:(TT + n + 1) * GH], ones[:, :], gn[:, n, 1, :])
                closed(last, "gcum")

            def dn_spread():
                pe.wait_ge(sem("ug"), 1)
                for n in range(TT):
                    b = opened(f"gbc{n}", 4 + n, 2 if n else 1)
                    closed(mm(b[:, :], ones[:, :], P1[:, n, :, :].rearrange("p h i -> p (h i)")), f"gbc{n}")

            def dn_rows():
                pe.wait_ge(sem("qk_d"), 1)
                for w in range(2):
                    b = opened(f"dn_rows{w}", 6 + w)
                    for n in range(TT):
                        for c in range(GC):
                            o = (n * GC + c) * P
                            last = pe.transpose(b[:, o:o + P], cv[:, (1 + w) * GC + c, n * P:(n + 1) * P], ident[:, :])
                    closed(last, f"dn_rows{w}")

            def dn_products():
                pe.wait_ge(sem("kbT"), 1)
                for h2 in range(2):
                    r = slice(64 * h2, 64 * h2 + 64)
                    for w, right in enumerate((kbT, cv)):
                        b = opened(f"kk{w}{h2}", 4 + 2 * w + h2)
                        for n in range(TT):
                            for c in range(GC):
                                o = (n * GC + c) * P
                                last = mm(b[:, o:o + P], cv[r, GC + c, n * P:(n + 1) * P],
                                          right[r, c, n * P:(n + 1) * P])
                        closed(last, f"kk{w}{h2}")

            def dn_first():
                for n in range(TT):
                    pe.wait_ge(sem("Tt"), n + 1)
                    b = opened(f"T0{n}", 4 + n)
                    for h in range(GH):
                        last = pe.transpose(b[:, h * P:(h + 1) * P], Tt[:, n, h, :], ident[:, :])
                    closed(last, f"T0{n}")

            def dn_inner(s):
                for n in range(TT):
                    pe.wait_ge(sem("BT"), TT * (s - 1) + n + 1)
                    pe.wait_ge(sem("Tn"), TT * (s - 1) + n + 1)
                    b = opened(f"P1{s}{n}", 4 + n)
                    for h in range(GH):
                        last = mm(b[:, h * P:(h + 1) * P], BT[:, n, h, :], Tn[:, n, h, :])
                    closed(last, f"P1{s}{n}")

            def dn_outer(s):
                for n in range(TT):
                    pe.wait_ge(sem("P1"), TT * (s - 1) + n + 1)
                    pe.wait_ge(sem("Tt"), TT * (s - 1) + n + 1)
                    b = opened(f"Pt{s}{n}", 6 + n)
                    for h in range(GH):
                        last = mm(b[:, h * P:(h + 1) * P], P1[:, n, h, :], Tt[:, n, h, :])
                    closed(last, f"Pt{s}{n}")
                    if s < 6:
                        b = opened(f"Pn{s}{n}", 4 + n)
                        for h in range(GH):
                            last = mm(b[:, h * P:(h + 1) * P], Tt[:, n, h, :], P1[:, n, h, :])
                        closed(last, f"Pn{s}{n}")

            def state(name, n, b_, ready, cnt):
                pe.wait_ge(sem(ready), cnt)
                b = opened(name, b_)
                for h in range(GH):
                    c, r = h // 2, 64 * (h % 2)
                    last = mm(b[r:r + 64, c * DV:(c + 1) * DV], kd[:, n, h * DK:(h + 1) * DK],
                              vn[:, n, h * DV:(h + 1) * DV])
                closed(last, name)

            def dn_values():
                pe.wait_ge(sem("Tt"), TT * 7)
                pe.wait_ge(sem("dn_scaled"), 1)
                for n in range(TT):
                    b = opened(f"u{n}", 6 + n)
                    for h in range(GH):
                        last = mm(b[:, h * DV:(h + 1) * DV], Tt[:, n, h, :], vb[:, n, h * DV:(h + 1) * DV])
                    closed(last, f"u{n}")
                b = opened("kc", 4)
                for h in range(GH):
                    c, r = h // 2, 64 * (h % 2)
                    last = mm(b[r:r + 64, c * P:(c + 1) * P], kbg[:, 1, h * DK:(h + 1) * DK], Tt[:, 1, h, :])
                closed(last, "kc")

            def dn_carry():
                pe.wait_ge(sem("S1"), 1)
                pe.wait_ge(sem("kcT"), 1)
                for h2 in range(2):
                    r = slice(64 * h2, 64 * h2 + 64)
                    b = opened(f"kcS{h2}", 6 + h2)
                    for c in range(GC):
                        last = mm(b[:, c * DV:(c + 1) * DV], kcT[r, c, :], S1[r, c, :])
                    closed(last, f"kcS{h2}")

            def dn_out():
                state("state2", 1, 4, "vn", 2)
                pe.wait_ge(sem("qdT"), 1)
                b = opened("oT", 5)
                for h in range(GH):
                    c, r = h // 2, 64 * (h % 2)
                    mm(b[r:r + 64, c * T:c * T + P], vn[:, 0, h * DV:(h + 1) * DV], AT[:, 0, h, :])
                for h in range(GH):
                    c, r = h // 2, 64 * (h % 2)
                    mm(b[r:r + 64, c * T + P:(c + 1) * T], vn[:, 1, h * DV:(h + 1) * DV], AT[:, 1, h, :], True, False)
                    last = mm(b[r:r + 64, c * T + P:(c + 1) * T], S1[r:r + 64, c, :], qdT[r:r + 64, c, :], False, True)
                closed(last, "oT")

            def state_product(name, b_, src, col):
                b = opened(name, b_)
                for c in range(GC):
                    for h2 in range(2):
                        r = 64 * h2
                        for q in range(NS):
                            last = mm(b[r:r + 64, c * NS + q:c * NS + q + 1], src[r:r + 64, q, c, :],
                                      cv[r:r + 64, col + c, T + q:T + q + 1])
                closed(last, name)

            def step_old():
                pe.wait_ge(sem("S_in"), 16 * 4)
                pe.wait_ge(sem("qk_d"), 1)
                state_product("kS", 6, Ss, GC)

            def step_spread():
                pe.wait_ge(sem("vdiag"), 1)
                vd = P1[:, :, :, :].rearrange("p n h i -> p (n h i)")
                for n in range(2):
                    b = opened(f"vbc{n}", 6 + n)
                    closed(mm(b[:, :], blk[:, :], vd[:, 512 * n:512 * n + 512]), f"vbc{n}")

            def step_new():
                pe.wait_ge(sem("Snew"), 1)
                state_product("qS", 4, Ss, 0)

            def out_sums():
                pe.wait_ge(sem("o_sq"), 1)
                for c in range(GC):
                    b = opened(f"oss{c}", 6 + c)
                    closed(mm(b[:, 0:NT], blk[:, :], sq4[:, c, :]), f"oss{c}")

            def own_scores():
                pe.wait_ge(sem("own_diag"), 1)
                b = opened("own", 6)
                closed(mm(b[:, 0:NS * H], ones[0:NS, :], own8[:, 1, :]), "own")
                pe.wait_ge(sem("k_scored"), NS)
                b = opened("gsum", 7)
                closed(mm(b[:, :], ones[:, :], s_all[:, :]), "gsum")
                b = opened("sT", 4)
                for n in range(4):
                    last = pe.transpose(b[:, n * P:(n + 1) * P], s_all[:, n * P:(n + 1) * P], ident[:, :])
                closed(last, "sT")

            def spread_max():
                pe.wait_ge(sem("max_diag"), 1)
                b = opened("pmax", 5)
                closed(mm(b[:, :], ones[:, :], w_a[:, :]), "pmax")

            def denominators():
                pe.wait_ge(sem("exps"), 1)
                b = opened("den", 6)
                closed(mm(b[:, :], ones[:, :], w_b[:, :]), "den")

            def fold(q):
                pe.wait_ge(sem("pv_masked"), q + 1)
                if q == 0:
                    opened("y8", 6)
                g = 32 * (q % 4)
                last = mm(bank[6][g:g + 32, :], selc[:, q, :], stg[:, q % 2, :], q < 4, q >= 4)
                if q < NS - 1:
                    last.then_inc(sem("folded"), 1)
                return last

            def page_values(q):
                if q == 0:
                    pe.wait_ge(sem("p_ready"), 1)
                b = opened(f"pv{q}", 4 + q % 2)
                for hf in range(HALVES):
                    slot = arrived(pe, ("v", (q, hf))).rearrange("p (k n) -> p k n", k=PGI)
                    for k in range(PGI):
                        last = mm(b[32 * k:32 * k + 32, :], pP[:, q * NPG + hf * PGI + k, :], slot[:, k, :],
                                  hf == 0, hf == HALVES - 1)
                    if hf < HALVES - 1:
                        used_up(last, ("v", (q, hf)), "pe_read")
                closed(last, f"pv{q}")
                read_by(f"pv{q}", ("v", (q, HALVES - 1)))
                if q:
                    fold(q - 1)

            def page_end():
                closed(fold(NS - 1), "y8")
                pe.wait_ge(sem("y8_out"), 1)
                b = opened("yT8", 7)
                for c in range(AC):
                    last = pe.transpose(b[:, c * P:(c + 1) * P], w_a[:, c * P:(c + 1) * P], ident[:, :])
                closed(last, "yT8")

            def ada_pair(j):
                ada(j)
                ada_turn(j)

            go = {
                "W": project, "BA": lambda _: decay_inputs(), "CEXT": lambda _: cached_rows(), "A": ada_pair,
                "QSUM": lambda _: head_sums("qss", "q_sq", lambda c: mixT[:, c, :], 2),
                "KSUM": lambda _: head_sums("kss", "k_sq", lambda c: mixT[:, AC + c, :], 2),
                "DSUM": lambda _: head_sums("dss", "d_sq", lambda c: sq4[:, c, :], 4),
                "QNORM": lambda _: head_spread("qn", "q_rec", 0, (2, 3)),
                "KNORM": lambda _: head_spread("kn", "k_rec", 1, (2, 3)),
                "DNORM": lambda _: head_spread("dn", "d_rec", 2, (4, 5, 6, 7)),
                "QR": lambda _: to_rows8("q8", "q_done", QC0), "QB": q_spread,
                "KR": lambda _: to_rows8("k8", "k_done", KC0),
                "VR": lambda _: to_rows8("v8", "proj_out", VC0, out_count(VC0 + AC - 1)),
                "KROW": lambda _: kv_rows("krow", KC0, "k_done", 1),
                "VROW": lambda _: kv_rows("vrow", VC0, "proj_out", out_count(VC0 + AC - 1)),
                "GN": lambda _: dn_heads(), "GC": lambda _: dn_cumulate(), "GBC": lambda _: dn_spread(),
                "ROWS": lambda _: dn_rows(), "KK": lambda _: dn_products(), "TI": lambda _: dn_first(),
                "L": dn_inner, "M": dn_outer, "TAILS": lambda _: tails(), "POOL": lambda _: pool_maps(),
                "S": lambda _: att_start(), "H": att_head, "HE": lambda _: att_out(H - 1),
                "UA": lambda _: dn_values(), "UB": lambda _: state("state1", 0, 5, "vn", 1),
                "UC": lambda _: dn_carry(), "UD": lambda _: dn_out(), "XA": lambda _: step_old(),
                "XB": lambda _: step_spread(), "XC": lambda _: step_new(), "XD": lambda _: out_sums(),
                "OWN": lambda _: own_scores(), "DMAX": lambda _: spread_max(), "DEXP": lambda _: denominators(),
                "V": page_values, "VE": lambda _: page_end(),
            }
            for st, n in ORDER:
                if st in go:
                    go[st](n)

            def parts(item):
                n = split.index(item)
                pe.wait_ge(sem("w_split"), n + 1)
                return [w[:, n % PARTS, :].rearrange("p (k n) -> p k n", n=IW) for w in (w_hi, w_lo)]

            def mm3(out, w, k, cols, acts, ka, start, stop):
                mm(out, w[0][:, k, cols], acts[0][:, ka, :], start, False)
                mm(out, w[0][:, k, cols], acts[1][:, ka, :], False, False)
                return mm(out, w[1][:, k, cols], acts[0][:, ka, :], False, stop)

            def parts_read(item, name):
                b, n = filled[name]
                part_free[item] = (bank_full[b], n)

            pe.wait_ge(sem("mix_lo"), 2)
            for i in range(D // IW):
                w = parts(("wout", i))
                for n in range(2):
                    j = 2 * i + n
                    b = opened(f"out{j}", 2 * (i % 2) + n)
                    for k in range(DC):
                        last = mm3(b[:, 0:NT], w, k, slice(n * P, (n + 1) * P), (a_hi, a_lo), k, k == 0, k == DC - 1)
                    closed(last, f"out{j}")
                parts_read(("wout", i), f"out{j}")
            square_sums("ss2", "sq2", hT)
            pe.wait_ge(sem("h2_lo"), 1)

            for i in range(DFF // IW):
                for m, kind in enumerate(("gate", "up")):
                    w = parts((kind, i))
                    for n in range(2):
                        name = f"{kind}{2 * i + n}"
                        b = opened(name, 4 * (i % 2) + 2 * m + n)
                        for k in range(DC):
                            last = mm3(b[:, 0:NT], w, k, slice(n * P, (n + 1) * P), (a_hi, a_lo), k, k == 0, k == DC - 1)
                        closed(last, name)
                    parts_read((kind, i), name)
            pe.wait_ge(sem("hidden"), FC)
            for i in range(D // IW):
                for n in range(2):
                    opened(f"down{2 * i + n}", 4 * (i % 2) + n)
                for m, (k0, k1) in enumerate(DKT):
                    w = parts(("down", (i, m)))
                    for n in range(2):
                        for k in range(k0, k1):
                            last = mm3(bank[4 * (i % 2) + n][:, 0:NT], w, k - k0, slice(n * P, (n + 1) * P),
                                       (hid_hi, hid_lo), k, k == 0, k == FC - 1)
                        if m == len(DKT) - 1:
                            closed(last, f"down{2 * i + n}")
                    if m < len(DKT) - 1:
                        singles["part_read"] += 1
                        last.then_inc(sem("part_read"), 1)
                        part_free[("down", (i, m))] = (sem("part_read"), singles["part_read"])
                    else:
                        parts_read(("down", (i, m)), f"down{2 * i + 1}")
            pe.wait_ge(sem("x2"), DC)
            for r in range(TT + 1):
                m = P if r < TT else NS
                for hlf in range(2):
                    b = opened(f"y{r}{hlf}", 2 + 4 * (r % 2) + hlf)
                    for c in range(4):
                        last = pe.transpose(b[0:m, c * P:(c + 1) * P], xT[:, 4 * hlf + c, r * P:r * P + m], ident[:, :])
                    closed(last, f"y{r}{hlf}")

        @block.vector
        def _(v):
            step = order(v, "dve_step")

            def tt(out, a, b_, op):
                return v.tensor_tensor(out, a, b_, op)

            def bc(ap, shape):
                return ap.to_broadcast(shape)

            def inc(ins, name):
                ins.then_inc(sem(name), 1)

            step(v.memset(cT[:, :, :], 0.0))
            v.memset(eps[:, 0:1], EPS)
            step(v.memset(eps[:, 1:2], 1.0))
            step(v.memset(st4[:, :, :], 0.0))
            b = full(v, "rowsT")
            step(v.tensor_copy(constT[:, 0:NR], b[:, 0:NR]))
            v.sem_inc(bank_free[2], 1)
            b = full(v, "cT")
            freed(v.tensor_copy(cT[:, :, 0:NC], b[:, 0:DC * NC].rearrange("p (c r) -> p c r", c=DC)), "cT")
            v.wait_ge(bank_free[3], frees_at("cT"))
            v.sem_inc(sem("cT_made"), 1)
            for c in range(0, DC, 2):
                b = full(v, f"xT{c}")
                freed(v.tensor_copy(xT[:, c, :], b[:, 0:NT]), f"xT{c}")
            v.wait_ge(sem("iota_made"), 1)
            for c in range(PCH):
                for g in range(2):
                    r = slice(64 * g, 64 * g + 64)
                    v.tensor_scalar(rcnt[r, c, :], rcnt[r, c, :], float(WINDOWS[2 * c + g]), None, ALU.min)
            step(v.tensor_scalar(eps[:, 0:1], eps[:, 0:1], 1.0, None, ALU.mult))
            v.reciprocal(rcnt[:, :, :], rcnt[:, :, :]).then_inc(sem("rcnt_made"), 1)

            def mod_reduce(j):
                b = full(v, f"adaT{j}")
                seen = b[:, :].rearrange("p (t g r) -> p t r g", t=4, g=4)[:, :, 0:NC, :]
                dst = modT[:, 4 * j:4 * j + 4, :]
                freed(v.tensor_reduce(dst, seen, AX, ALU.add), f"adaT{j}")
                v.wait_ge(bank_free[filled[f"adaT{j}"][0]], frees_at(f"adaT{j}"))
                step(tt(dst, dst, bc(constT[:, 4 * j:4 * j + 4].unsqueeze(2), [P, 4, NC]), ALU.add))

            def modulation(sc, wrow):
                step(v.scalar_tensor_tensor(out=scA[:, :, :], in0=modT[:, sc * DC:(sc + 1) * DC, :], scalar=1.0,
                                            in1=bc(constT[:, wrow:wrow + DC].unsqueeze(2), [P, DC, NC]),
                                            op0=ALU.add, op1=ALU.mult))

            def norm_apply(root, sh, done):
                v.wait_ge(sem(root), 1)
                step(v.reciprocal(rbc[:, 0, :], rbc[:, 0, :]))
                step(tt(hT[:, :, :], xT[:, :, :], bc(rbc[:, 0:1, :], [P, DC, NT]), ALU.mult))
                for c in range(DC):
                    v.tensor_scalar(hT[:, c, 0:T], hT[:, c, 0:T], scA[:, c, 0:1],
                                    modT[:, sh * DC + c, 0:1], ALU.mult, ALU.add)
                step(tt(hT[:, :, T:NT], hT[:, :, T:NT], scA[:, :, 1:NC], ALU.mult))
                inc(tt(hT[:, :, T:NT], hT[:, :, T:NT], modT[:, sh * DC:(sh + 1) * DC, 1:NC], ALU.add), done)

            v.wait_ge(sem("pbuf_in"), 16)
            for g, w in enumerate(WINDOWS):
                last = v.tensor_reduce(pd8[:, 0, 64 * g:64 * g + 64],
                                       pbuf.rearrange("b (t c) -> b c t", t=NBUF)[:, 64 * g:64 * g + 64, NBUF - w + 1:NBUF],
                                       AX, ALU.add)
            inc(last, "pool_rows")
            for j in range(2 * DC // 4):
                mod_reduce(j)
            modulation(1, R_N1)
            norm_apply("root1", 0, "h1")

            def head_rec(root, row, done):
                v.wait_ge(sem(root), 1)
                inc(v.reciprocal(rbc[0:2 * AC, row, :], rbc[0:2 * AC, row, :]), done)

            def head_norm(name, c0, row, done):
                for c in range(AC):
                    b = full(v, f"{name}{c}")
                    last = v.scalar_tensor_tensor(out=proj[:, c0 + c, :], in0=proj[:, c0 + c, :],
                                                  scalar=constT[:, row:row + 1], in1=b[:, 0:NT], op0=ALU.mult, op1=ALU.mult)
                    freed(last, f"{name}{c}")
                v.wait_ge(bank_free[filled[f"{name}2"][0]], frees_at(f"{name}2"))
                v.wait_ge(bank_free[filled[f"{name}3"][0]], frees_at(f"{name}3"))
                v.sem_inc(sem(done), 1)

            def rows8(name, n, done):
                b = full(v, name)
                freed(v.tensor_copy(nat8[:, n, :], b[0:NS, :]), name)
                v.wait_ge(bank_free[filled[name][0]], frees_at(name))
                v.sem_inc(sem(done), 1)

            def k_item(q, hf):
                slot = arrived(v, ("k", (q, hf)))
                v.wait_ge(sem("qb"), q + 1)
                ins = tt(prod[:, :].rearrange("p (k n) -> p k n", k=PGI), slot.rearrange("p (k n) -> p k n", k=PGI),
                         bc(qb[:, q % 2:q % 2 + 1, :], [P, PGI, AW]), ALU.mult)
                used_up(ins, ("k", (q, hf)), "keys_read")
                v.wait_ge(*released[("k", (q, hf))])
                o = (q * NPG + hf * PGI) * H
                ins = v.tensor_reduce(s_all[:, o:o + PGI * H], prod[:, :].rearrange("p (g d) -> p g d", d=HD), AX, ALU.add)
                if hf == HALVES - 1:
                    ins.then_inc(sem("k_scored"), 1)
                    v.wait_ge(sem("k_scored"), q + 1)
                else:
                    step(ins)

            def scores(n):
                k_item(n // HALVES, n % HALVES)

            def att_mask(h):
                b = full(v, f"S{h}")
                freed(tt(sm[:, h % 2, :], b[:, 0:3 * P], cmask[:, :, :].rearrange("p a k -> p (a k)"), ALU.add), f"S{h}")
                v.wait_ge(bank_free[filled[f"S{h}"][0]], frees_at(f"S{h}"))
                v.tensor_reduce(st4[:, h % 2, 0:1], sm[:, h % 2, 0:P], AX, ALU.max)
                step(v.tensor_reduce(st4[:, h % 2, 1:2], sm[:, h % 2, P:3 * P], AX, ALU.max))
                inc(v.tensor_scalar(st4[:, h % 2, 2:4], st4[:, h % 2, 0:2], -SCALE, None, ALU.mult), "masked")

            def att_norm(h):
                v.wait_ge(sem("exped"), h + 1)
                step(v.reciprocal(st4[:, h % 2, 6:8], st4[:, h % 2, 4:6]))
                v.tensor_scalar(sm[:, h % 2, 0:P], sm[:, h % 2, 0:P], st4[:, h % 2, 6:7], None, ALU.mult)
                inc(v.tensor_scalar(sm[:, h % 2, P:3 * P], sm[:, h % 2, P:3 * P], st4[:, h % 2, 7:8], None, ALU.mult),
                    "probs")

            def att_take(c):
                b = full(v, f"O{c}")
                freed(v.tensor_copy(mixT[:, PCH + c, 0:T], b[:, 0:T]), f"O{c}")

            def att_first(_):
                att_mask(0)

            def att_head(h):
                if h >= 1:
                    full(v, f"PT{h - 1}")
                if h + 1 < H:
                    att_mask(h + 1)
                att_norm(h)
                if h >= 2 and h % 2 == 0:
                    att_take(h // 2 - 1)

            def cw(i, c):
                return constT[:, R_CW + i * CVN + c:R_CW + i * CVN + c + 1]

            def halves(m, h2):
                return m[:, :, :, :].rearrange("p n (c w) i -> p n w c i", w=2)[:, :, h2, :, :]

            def level(s, n):
                return tt(BT[:, n, :, :], MT[:, n, :, :], bc(lvl[:, s, :].unsqueeze(1), [P, GH, P]), ALU.mult)

            def outer(s):
                for n in range(TT):
                    b = full(v, f"Pt{s}{n}")
                    if s < 6:
                        inc(level(s + 1, n), "BT")
                    freed(tt(Tt[:, n, :, :], Tt[:, n, :, :], b[:, :].rearrange("p (h i) -> p h i", h=GH), ALU.subtract)
                          if s == 6 else after_turn(s, n, b), f"Pt{s}{n}")
                    v.wait_ge(bank_free[6 + n], frees_at(f"Pt{s}{n}"))
                    v.sem_inc(sem("Tt"), 1)
                    if s < 6:
                        bn = full(v, f"Pn{s}{n}")
                        freed(tt(Tn[:, n, :, :], Tn[:, n, :, :], bn[:, :].rearrange("p (h i) -> p h i", h=GH),
                                 ALU.subtract), f"Pn{s}{n}")
                        v.wait_ge(bank_free[4 + n], frees_at(f"Pn{s}{n}"))
                        v.sem_inc(sem("Tn"), 1)

            def after_turn(s, n, b):
                full(v, f"Pn{s}{n}")
                return tt(Tt[:, n, :, :], Tt[:, n, :, :], b[:, :].rearrange("p (h i) -> p h i", h=GH), ALU.subtract)

            def paged(ap):
                return ap.rearrange("p (n t h) -> p n t h", t=PPB, h=H)

            def queried(ap):
                return ap.rearrange("p (q n h) -> p q n h", q=NS, h=H)

            def cached_rows(_):
                b = full(v, "cext")
                freed(v.tensor_copy(cext[:, :, :], b[:, 0:CVN * NS * NCV].rearrange("p (c r) -> p c r", c=CVN)), "cext")
                v.wait_ge(bank_free[filled["cext"][0]], frees_at("cext"))
                b = full(v, "pdT8")
                freed(v.tensor_copy(pdT[:, :, T:NT], b[:, 0:PCH * NS].rearrange("p (c q) -> p c q", c=PCH)), "pdT8")
                v.wait_ge(bank_free[3], frees_at("pdT8"))

            def pool_maps(_):
                v.wait_ge(sem("proj_out"), out_count(PCH - 1))
                step(tt(pdT[:, :, T:NT], pdT[:, :, T:NT], proj[:, 0:PCH, T:NT], ALU.add))
                v.wait_ge(sem("pool_prompt_done"), 1)
                for c in range(PCH):
                    last = v.scalar_tensor_tensor(out=pdT[:, c, T:NT], in0=pdT[:, c, T:NT], scalar=rcnt[:, c, T - 1:T],
                                                  in1=proj[:, c, T:NT], op0=ALU.mult, op1=ALU.subtract)
                inc(last, "pool_diff")
                for c in range(PCH):
                    b = full(v, f"pool{c}")
                    freed(v.tensor_scalar(mixT[:, c, :], b[:, 0:NT], constT[:, R_PS + c:R_PS + c + 1], None, ALU.mult),
                          f"pool{c}")


            def convolve(_):
                v.wait_ge(sem("proj_out"), out_count(CV0 + CVN - 1))
                for c in range(CVN):
                    last = v.tensor_scalar(cv[:, c, :], proj[:, CV0 + c, :], cw(NCV, c), None, ALU.mult)
                step(last)
                for i in range(NCV):
                    back = NCV - i
                    for c in range(CVN):
                        v.scalar_tensor_tensor(out=cv[:, c, back:T], in0=proj[:, CV0 + c, 0:T - back], scalar=cw(i, c),
                                               in1=cv[:, c, back:T], op0=ALU.mult, op1=ALU.add)
                        last = v.scalar_tensor_tensor(out=cv[:, c, T:NT], in0=cext[:, c, i:NS * NCV:NCV], scalar=cw(i, c),
                                                      in1=cv[:, c, T:NT], op0=ALU.mult, op1=ALU.add)
                    if i < NCV - 1:
                        step(last)
                inc(last, "conv_done")


            def decays(_):
                b = full(v, "ba")
                v.wait_ge(sem("gcol_in"), 32)
                v.tensor_scalar(ab[:, 0, :], b[0:GH, 0:NT], -1.0, None, ALU.mult)
                freed(v.tensor_scalar(ab[:, 3, :], b[32:32 + GH, 0:NT], gcol[:, 1:2], None, ALU.add), "ba")
                v.wait_ge(bank_free[2], frees_at("ba"))
                step(v.tensor_scalar(ab[:, 1, :], ab[:, 3, :], 0.0, None, ALU.max))
                inc(v.scalar_tensor_tensor(out=ab[:, 4, :], in0=ab[:, 3, :], scalar=0.5, in1=ab[:, 1, :],
                                           op0=ALU.mult, op1=ALU.subtract), "ab_in")
                v.wait_ge(sem("ab_exp"), 1)
                step(v.tensor_scalar(ab[:, 0, :], ab[:, 0, :], 1.0, None, ALU.add))
                step(v.reciprocal(ab[:, 0, :], ab[:, 0, :]))
                step(tt(ab[:, 1, :], ab[:, 1, :], ab[:, 4, :], ALU.add))
                step(v.tensor_scalar(gcol[:, 3:4], gcol[:, 2:3], -1.0, None, ALU.mult))
                inc(v.tensor_scalar(ab[:, 1, :], ab[:, 1, :], gcol[:, 3:4], None, ALU.mult), "ab_g")


            def key_norm(_):
                for c in range(2 * GC):
                    b = full(v, f"dn{c}")
                    freed(v.scalar_tensor_tensor(out=cv[:, c, :], in0=cv[:, c, :],
                                                 scalar=float(DK) ** -0.5 if c < GC else 1.0, in1=b[:, 0:NT],
                                                 op0=ALU.mult, op1=ALU.mult), f"dn{c}")
                for c in range(2 * GC):
                    v.wait_ge(bank_free[filled[f"dn{c}"][0]], frees_at(f"dn{c}"))
                v.sem_inc(sem("qk_d"), 1)

            def dn_heads(_):
                b = full(v, "gn")
                freed(v.tensor_copy(gn[:, :, :, :].rearrange("p n w h -> p (n w h)"), b[:, 0:4 * GH]), "gn")
                v.wait_ge(bank_free[4], frees_at("gn"))
                v.sem_inc(sem("gn_out"), 1)
                for c in range(GC):
                    b = full(v, f"bbc{c}")
                    v.tensor_copy(bgs[:, 0, c, :], b[:, T:NT])
                    v.tensor_copy(bgs[:, 1, c, :], b[:, NT:NT + NS])
                    freed(tt(kbT[:, c, :], cv[:, GC + c, 0:T], b[:, 0:T], ALU.mult), f"bbc{c}")
                v.wait_ge(bank_free[6], frees_at("bbc1"))
                v.sem_inc(sem("kbT"), 1)
                for n in range(TT):
                    last = tt(P1[:, n, :, :], bc(triu[:, :].unsqueeze(1), [P, GH, P]),
                              bc(gn[:, n, 1, :].unsqueeze(2), [P, GH, P]), ALU.mult)
                inc(last, "ug")

            def dn_cumulate(_):
                b = full(v, "gcum")
                freed(v.tensor_copy(gs[:, 0:2, :].rearrange("p a h -> p (a h)"), b[:, 0:4 * GH]), "gcum")
                v.wait_ge(bank_free[7], frees_at("gcum"))
                inc(tt(gs[:, 3, :], gs[:, 1, :], gs[:, 0, :], ALU.subtract), "gs_in")

            def dn_spread(_):
                for n in range(TT):
                    b = full(v, f"gbc{n}")
                    if n:
                        v.wait_ge(bank_free[5], frees_at("gbc1") - 1)
                    freed(tt(DT[:, n, :, :], b[:, :].rearrange("p (h i) -> p h i", h=GH),
                             bc(gs[:, 0, n * GH:(n + 1) * GH].unsqueeze(2), [P, GH, P]), ALU.subtract), f"gbc{n}")
                v.wait_ge(bank_free[4], frees_at("gbc0"))
                v.wait_ge(bank_free[5], frees_at("gbc1"))
                inc(v.tensor_scalar(DT[:, :, :, :], DT[:, :, :, :], 0.0, None, ALU.min), "decay_in")

            def dn_rows(_):
                v.wait_ge(sem("gs_exp"), 1)
                for n in range(TT):
                    last = tt(gs[:, 6, n * GH:(n + 1) * GH], gs[:, 2, n * GH:(n + 1) * GH], gn[:, n, 0, :], ALU.mult)
                step(last)
                b = full(v, "dn_rows0")
                rows_v = b[:, :].rearrange("p (n d) -> p n d", d=DK)
                tt(kbg[:, :, :].rearrange("p n (h d) -> p (n h) d", d=DK), rows_v,
                   bc(gs[:, 6, :].unsqueeze(2), [P, TT * GH, DK]), ALU.mult)
                freed(tt(kd[:, :, :].rearrange("p n (h d) -> p (n h) d", d=DK), rows_v,
                         bc(gs[:, 3, :].unsqueeze(2), [P, TT * GH, DK]), ALU.mult), "dn_rows0")
                b = full(v, "dn_rows1")
                for n in range(TT):
                    last = tt(vb[:, n, :].rearrange("p (h d) -> p h d", d=DV),
                              b[:, n * GH * DV:(n + 1) * GH * DV].rearrange("p (h d) -> p h d", d=DV),
                              bc(gn[:, n, 0, :].unsqueeze(2), [P, GH, DV]), ALU.mult)
                freed(last, "dn_rows1")
                v.wait_ge(bank_free[7], frees_at("dn_rows1"))
                v.sem_inc(sem("dn_scaled"), 1)

            def dn_products(_):
                v.wait_ge(sem("decay_exp"), 1)
                for n in range(TT):
                    last = tt(DT[:, n, :, :], DT[:, n, :, :], bc(triu[:, :].unsqueeze(1), [P, GH, P]), ALU.mult)
                step(last)
                for h2 in range(2):
                    for w, dst in enumerate((MT, AT)):
                        b = full(v, f"kk{w}{h2}")
                        freed(tt(halves(dst, h2), b[:, :].rearrange("p (n c i) -> p n c i", n=TT, c=GC), halves(DT, h2),
                                 ALU.mult), f"kk{w}{h2}")
                v.wait_ge(bank_free[7], frees_at("kk11"))

                for n in range(TT):
                    step(level(0, n))
                    inc(tt(Tt[:, n, :, :], bc(ident[:, :].unsqueeze(1), [P, GH, P]), BT[:, n, :, :], ALU.subtract), "Tt")
                    v.wait_ge(sem("Tt"), n + 1)
                for n in range(TT):
                    inc(level(1, n), "BT")

            def dn_values(_):
                b = full(v, "u0")
                freed(v.tensor_copy(vn[:, 0, :], b[:, 0:GH * DV]), "u0")
                v.wait_ge(bank_free[6], frees_at("u0"))
                v.sem_inc(sem("vn"), 1)
                b = full(v, "u1")
                freed(v.tensor_copy(vn[:, 1, :], b[:, 0:GH * DV]), "u1")
                v.wait_ge(bank_free[7], frees_at("u1"))

            def dn_state(_):
                b = full(v, "state1")
                freed(v.tensor_copy(S1[:, :, :], b[:, 0:GC * DV].rearrange("p (c v) -> p c v", c=GC)), "state1")
                v.wait_ge(bank_free[5], frees_at("state1"))
                v.sem_inc(sem("S1"), 1)

            def dn_carry(_):
                for h2 in range(2):
                    b = full(v, f"kcS{h2}")
                    own = vn[:, 1, :].rearrange("p (c w d) -> p w c d", w=2, d=DV)[:, h2, :, :]
                    freed(tt(own, own, b[:, 0:GC * DV].rearrange("p (c d) -> p c d", c=GC), ALU.subtract), f"kcS{h2}")
                v.wait_ge(bank_free[7], frees_at("kcS1"))
                v.sem_inc(sem("vn"), 1)

            def dn_out(_):
                b = full(v, "state2")
                for h in range(GH):
                    c, r = h // 2, 64 * (h % 2)
                    last = v.scalar_tensor_tensor(out=S2[r:r + 64, c, :], in0=S1[r:r + 64, c, :],
                                                  scalar=gs[r:r + 64, 4, GH + h:GH + h + 1],
                                                  in1=b[r:r + 64, c * DV:(c + 1) * DV], op0=ALU.mult, op1=ALU.add)
                freed(last, "state2")
                v.wait_ge(bank_free[4], frees_at("state2"))
                v.sem_inc(sem("S2_done"), 1)
                b = full(v, "oT")
                freed(v.tensor_copy(pdT[:, :, 0:T], b[:, :].rearrange("p (c t) -> p c t", c=GC)), "oT")


            def step_old(_):
                b = full(v, "kS")
                kSv = b[:, 0:GC * NS].rearrange("p (c q) -> p c q", c=GC)
                freed(tt(sv[:, 0, :, :], kSv, bgs[:, 1, :, :], ALU.mult), "kS")
                v.wait_ge(bank_free[6], frees_at("kS"))
                step(tt(sv[:, 1, :, :], cv[:, 2 * GC:3 * GC, T:NT], sv[:, 0, :, :], ALU.subtract))
                step(tt(sv[:, 0, :, :], sv[:, 1, :, :], bgs[:, 0, :, :], ALU.mult))
                vd = P1[:, :, :, :].rearrange("p n h i -> p (n h i)").rearrange("p (q c w) -> p q c w", q=NS, c=GC)
                for c in range(GC):
                    last = tt(vd[:, :, c, :], bc(i64[:, :].unsqueeze(1), [P, NS, DV]),
                              bc(sv[:, 0, c, :].unsqueeze(2), [P, NS, DV]), ALU.mult)
                inc(last, "vdiag")
                for c in range(GC):
                    tt(Ss[:, :, c, :], Ss[:, :, c, :], bc(bgs[:, 1, c, :].unsqueeze(2), [P, NS, DV]), ALU.mult)

            def step_spread(_):
                for n in range(2):
                    b = full(v, f"vbc{n}")
                    hq = NS // 2
                    for c in range(GC):
                        last = tt(Sx[:, n * hq:(n + 1) * hq, c, :],
                                  b[:, :].rearrange("p (q c w) -> p q c w", q=hq, c=GC)[:, :, c, :],
                                  bc(cv[:, GC + c, T + n * hq:T + (n + 1) * hq].unsqueeze(2), [P, hq, DV]), ALU.mult)
                    freed(last, f"vbc{n}")
                v.wait_ge(bank_free[7], frees_at("vbc1"))
                inc(tt(x_nat[:, 0, :], x_nat[:, 0, :], x_nat[:, 1, :], ALU.add), "Snew")

            def step_new(_):
                b = full(v, "qS")
                freed(v.tensor_copy(pdT[:, :, T:NT], b[:, 0:GC * NS].rearrange("p (c q) -> p c q", c=GC)), "qS")
                v.wait_ge(bank_free[4], frees_at("qS"))
                v.sem_inc(sem("o_done"), 1)

            def out_norm(_):
                v.wait_ge(sem("rooto"), 2)
                step(v.reciprocal(rbc[:, 0:GC, :], rbc[:, 0:GC, :]))
                step(v.scalar_tensor_tensor(out=pdT[:, :, :].rearrange("p c t -> p (c t)"),
                                            in0=pdT[:, :, :].rearrange("p c t -> p (c t)"),
                                            scalar=constT[:, R_Q + 2:R_Q + 3],
                                            in1=rbc[:, 0:GC, :].rearrange("p c t -> p (c t)"), op0=ALU.mult, op1=ALU.mult))
                v.wait_ge(sem("z_silu"), 1)
                step(tt(mixT[:, PCH + AC:DC, :], pdT[:, :, :], proj[:, Z0:Z0 + GC, :], ALU.mult))


            def own_scores(_):
                step(tt(prod[0:NS, 0:AW], nat8[:, 0, :], nat8[:, 1, :], ALU.mult))
                step(v.tensor_reduce(own8[:, 0, 0:H], prod[0:NS, 0:AW].rearrange("p (h d) -> p h d", d=HD), AX, ALU.add))
                inc(tt(own8[:, 1, :].rearrange("p (q h) -> p q h", h=H), bc(ident[0:NS, 0:NS].unsqueeze(2), [NS, NS, H]),
                       bc(own8[:, 0, 0:H].unsqueeze(1), [NS, NS, H]), ALU.mult), "own_diag")
                b = full(v, "own")
                freed(v.tensor_copy(sm64[:, 2, :, :].rearrange("p q h -> p (q h)"), b[:, 0:NS * H]), "own")
                b = full(v, "gsum")
                freed(v.tensor_reduce(g4, b[:, :].rearrange("p (n t h) -> p n h t", t=PPB, h=H), AX, ALU.add), "gsum")
                v.wait_ge(bank_free[7], frees_at("gsum"))
                step(v.memset(cnt4[:, :, :, :], 0.0))
                for n in range(NB):
                    for m in range(NB):
                        if m != n:
                            step(tt(cmp1[:, :, :], gate4[:, :, m, :], gate4[:, :, n, :], ALU.is_ge if m < n else ALU.is_gt))
                            step(tt(cnt4[:, :, n, :], cnt4[:, :, n, :], cmp1[:, :, :], ALU.add))
                step(v.tensor_scalar(g4, c4, float(min(TOPK, NB + 1)), None, ALU.is_lt))
                step(v.tensor_scalar(c4, g4, FAR, -FAR, ALU.mult, ALU.add))
                b = full(v, "sT")
                freed(v.tensor_reduce(tokmax[:, :], b[:, :].rearrange("p (n t) -> p n t", n=4), AX, ALU.max), "sT")
                v.wait_ge(bank_free[4], frees_at("sT"))
                v.wait_ge(sem("tails_out"), 64)
                for n in range(4):
                    last = v.tensor_scalar(w_a[:, n * P:(n + 1) * P], ident[:, :], tokmax[:, n:n + 1], None, ALU.mult)
                inc(last, "max_diag")

            def spread_max(_):
                b = full(v, "pmax")

                freed(tt(paged(w_b), paged(b[:, :]), bc(c4.unsqueeze(2), [P, NS * NB, PPB, H]), ALU.add), "pmax")
                v.wait_ge(bank_free[5], frees_at("pmax"))
                step(v.tensor_reduce(sm64[:, 0, :, :], queried(w_b).rearrange("p q n h -> p q h n"), AX, ALU.max))
                step(tt(sm64[:, 1, :, :], sm64[:, 0, :, :], sm64[:, 2, :, :], ALU.max))
                tt(sm64[:, 3, :, :], sm64[:, 2, :, :], sm64[:, 1, :, :], ALU.subtract)
                step(tt(queried(w_b), queried(s_all[:, :]), bc(sm64[:, 1, :, :].unsqueeze(2), [P, NS, NPG, H]), ALU.subtract))
                inc(v.tensor_scalar(w_b, w_b, 0.0, None, ALU.min), "shifted")

            def denominators(_):
                v.wait_ge(sem("rooto"), 2)
                step(v.memset(prod[:, :], 0.0))
                v.wait_ge(sem("exp8"), 1)
                inc(tt(paged(w_b), paged(w_b), bc(g4.unsqueeze(2), [P, NS * NB, PPB, H]), ALU.mult), "exps")
                b = full(v, "den")
                freed(v.tensor_reduce(sm64[:, 4, :, :], queried(b[:, :]).rearrange("p q n h -> p q h n"), AX, ALU.add), "den")
                v.wait_ge(bank_free[6], frees_at("den"))
                step(tt(sm64[:, 4, :, :], sm64[:, 4, :, :], sm64[:, 3, :, :], ALU.add))
                step(v.reciprocal(sm64[:, 4, :, :], sm64[:, 4, :, :]))
                tt(sm64[:, 5, :, :], sm64[:, 3, :, :], sm64[:, 4, :, :], ALU.mult)
                inc(tt(pP.rearrange("p (q n) m -> p q n m", q=NS)[:, :, :, 0:H], queried(w_b),
                       bc(sm64[:, 4, :, :].unsqueeze(2), [P, NS, NPG, H]), ALU.mult), "p_ready")

            def page_values(q):
                b = full(v, f"pv{q}")
                if q == 0:
                    v.wait_ge(sem("krow_out"), 32)
                if q >= 2:
                    v.wait_ge(sem("folded"), q - 1)
                freed(tt(stg[:, q % 2, :].rearrange("p (h d) -> p h d", d=HD), b[:, :].rearrange("p (h d) -> p h d", d=HD),
                         bc(dm8[:, :].unsqueeze(2), [P, H, HD]), ALU.mult), f"pv{q}")
                v.wait_ge(bank_free[4 + q % 2], frees_at(f"pv{q}"))
                v.sem_inc(sem("pv_masked"), 1)

            def mix_low(_):
                v.wait_ge(sem("mix_hi"), 1)
                inc(tt(a_lo[:, :, 0:T], mixT[:, :, 0:T], a_hi[:, :, 0:T], ALU.subtract), "mix_lo")

            def page_end(_):
                b = full(v, "y8")
                freed(v.tensor_copy(w_a, b[:, :]), "y8")
                v.wait_ge(bank_free[6], frees_at("y8"))
                v.sem_inc(sem("y8_out"), 1)
                b = full(v, "yT8")
                for c in range(AC):
                    last = v.tensor_reduce(mixT[:, PCH + c, T:NT],
                                           b[:, c * P:(c + 1) * P].rearrange("p (g r) -> p r g", g=4)[:, 0:NS, :], AX, ALU.add)
                freed(last, "yT8")
                v.wait_ge(bank_free[7], frees_at("yT8"))
                own_v = w_b[:, 0:AC * NS].rearrange("p (c q) -> p c q", c=AC)
                for h2 in range(2):
                    r = slice(64 * h2, 64 * h2 + 64)
                    last = tt(own_v[r, :, :], proj[r, VC0:VC0 + AC, T:NT],
                              sm64[r, 5, :, :].rearrange("p q (c w) -> p w c q", w=2)[:, h2, :, :], ALU.mult)
                step(last)
                inc(tt(mixT[:, PCH:PCH + AC, T:NT], mixT[:, PCH:PCH + AC, T:NT], own_v, ALU.add), "mix")


            go = {
                "QSUM": lambda _: head_rec("rootq", 0, "q_rec"), "KSUM": lambda _: head_rec("rootk", 1, "k_rec"),
                "DSUM": lambda _: head_rec("rootd", 2, "d_rec"),
                "QNORM": lambda _: head_norm("qn", QC0, R_Q, "q_done"),
                "KNORM": lambda _: head_norm("kn", KC0, R_Q + 1, "k_done"),
                "QR": lambda _: rows8("q8", 0, "q_rows8"), "KR": lambda _: rows8("k8", 1, "k_rows8"),
                "VR": lambda _: rows8("v8", 2, "v_rows8"), "K": scores, "CEXT": cached_rows, "CONV": convolve, "AB": decays,
                "DNORM": key_norm, "GN": dn_heads, "GC": dn_cumulate, "GBC": dn_spread, "ROWS": dn_rows, "KK": dn_products,
                "M": outer, "S": att_first, "H": att_head, "HE": lambda _: att_take(H // 2 - 1), "POOL": pool_maps,
                "UA": dn_values, "UB": dn_state, "UC": dn_carry, "UD": dn_out, "XA": step_old, "XB": step_spread,
                "XC": step_new, "XD": out_norm, "OWN": own_scores, "DMAX": spread_max, "DEXP": denominators,
                "A": mod_reduce, "V": page_values, "VE": page_end,
                "MX": mix_low,
            }
            for st, n in ORDER:
                if st in go:
                    go[st](n)

            def residual(name, j, gate, done):
                b = full(v, name)
                m = gate * DC + j
                v.scalar_tensor_tensor(out=xT[:, j, 0:T], in0=b[:, 0:T], scalar=modT[:, m, 0:1], in1=xT[:, j, 0:T],
                                       op0=ALU.mult, op1=ALU.add)
                freed(tt(sv[:, 0, 0, :], b[:, T:NT], modT[:, m, 1:NC], ALU.mult), name)
                v.wait_ge(bank_free[filled[name][0]], frees_at(name))
                inc(tt(xT[:, j, T:NT], xT[:, j, T:NT], sv[:, 0, 0, :], ALU.add), done)
                v.wait_ge(sem(done), j + 1)

            def w_low(n):
                item = split[n]
                c = width(item)
                v.wait_ge(sem("w_high"), n + 1)
                if n >= PARTS:
                    v.wait_ge(*part_free[split[n - PARTS]])
                used_up(tt(w_lo[:, n % PARTS, 0:c], arrived(v, item)[:, 0:c], w_hi[:, n % PARTS, 0:c], ALU.subtract),
                        item, "w_split")

            v.wait_ge(sem("mix_hi"), 2)
            inc(tt(a_lo[:, :, T:NT], mixT[:, :, T:NT], a_hi[:, :, T:NT], ALU.subtract), "mix_lo")
            done = 0
            for n in range(PARTS):
                w_low(n)
            at = PARTS
            for j in range(DC):
                residual(f"out{j}", j, 2, "x1")
                if j % 2 and at < D // IW + 2:
                    w_low(at)
                    at += 1
            modulation(4, R_N2)
            norm_apply("root2", 3, "h2")
            v.wait_ge(sem("h2_hi"), 1)
            inc(tt(a_lo[:, :, :], hT[:, :, :], a_hi[:, :, :], ALU.subtract), "h2_lo")

            def hide(f):
                v.wait_ge(sem("silu"), f + 1)
                b = full(v, f"up{f}")
                own = hidden[:, f % 2, :]
                freed(tt(own, rbc[:, f % 4, :], b[:, 0:NT], ALU.mult), f"up{f}")
                v.wait_ge(bank_free[filled[f"up{f}"][0]], frees_at(f"up{f}"))
                step(v.tensor_copy(hid_hi[:, f, :], own))
                inc(tt(hid_lo[:, f, :], own, hid_hi[:, f, :], ALU.subtract), "hidden")

            n0 = D // IW
            for n in range(at, len(split) + 2):
                if n < len(split):
                    w_low(n)
                kind, i = split[n - 2]
                if kind == "up":
                    for f in (2 * i, 2 * i + 1):
                        hide(f)
                if kind == "down" and i[1] == len(DKT) - 1:
                    for j in (2 * i[0], 2 * i[0] + 1):
                        residual(f"down{j}", j, 5, "x2")
            v.wait_ge(sem("states_out"), 64)
            for r in range(TT + 1):
                m = P if r < TT else NS
                for hlf in range(2):
                    b = full(v, f"y{r}{hlf}")
                    freed(v.tensor_copy(ynat[0:m, r, 512 * hlf:512 * hlf + 512], b[0:m, :]), f"y{r}{hlf}")
                    v.wait_ge(bank_free[filled[f"y{r}{hlf}"][0]], frees_at(f"y{r}{hlf}"))
                v.sem_inc(sem("y_rows"), 1)

        @block.scalar
        def _(a):
            step = order(a, "act_step")

            def inc(ins, name):
                ins.then_inc(sem(name), 1)

            for r in range(TT):
                a.dma_start(x_nat[:, r, :], x_prompt[0, r * P:(r + 1) * P, :]).then_inc(sem("x_in"), 16)
            a.dma_start(x_nat[0:NS, TT, :], x_sample[:, 0, :]).then_inc(sem("x_in"), 16)
            a.dma_start(gcol[:, 0:1], a_log.rearrange("o h -> h o")).then_inc(sem("gcol_in"), 16)
            a.dma_start(gcol[:, 1:2], dt_bias.rearrange("o h -> h o")).then_inc(sem("gcol_in"), 16)
            a.dma_start(wba[:, :, :], w_in[0].rearrange("(k p) n -> p k n", p=P)[:, :, PJ * P:]).then_inc(sem("wba_in"), 16)
            for g in range(2 * PCH):
                a.dma_start(poolw[64 * (g % 2):64 * (g % 2) + 64, g // 2, :], pool_w[0, g]).then_inc(sem("poolw_in"), 16)
            a.dma_start(cst[:, :], state_conv[0].rearrange("q t c -> (q t) c")).then_inc(sem("cst_in"), 16)
            a.dma_start(pbuf, state_pool[0].rearrange("q t c -> q (t c)")).then_inc(sem("pbuf_in"), 16)

            a.wait_ge(sem("c_in"), 32)
            inc(a.activation(c_nat, c_nat, ACT.Silu), "c_silu")
            for c in range(1, DC, 2):
                b = full(a, f"xT{c}")
                freed(a.activation(xT[:, c, :], b[:, 0:NT], ACT.Copy), f"xT{c}")
            a.wait_ge(bank_free[7], frees_at("xT7"))
            a.wait_ge(bank_free[5], frees_at("xT5"))
            a.wait_ge(bank_free[4], frees_at("xT4"))
            a.wait_ge(bank_free[6], frees_at("xT6"))
            inc(a.activation(hT[:, :, :], xT[:, :, :], ACT.Square), "sq1")

            def ada_rows(j):
                b = full(a, f"ada{j}")
                if j:
                    full(a, f"adaT{j - 1}")
                freed(a.activation(adaS[:, :], b[:, :], ACT.Copy), f"ada{j}")
                a.wait_ge(bank_free[3], frees_at(f"ada{j}"))
                a.sem_inc(sem("ada_rows"), 1)

            for j in range(2 * D // IW // 2):
                ada_rows(j)
            a.wait_ge(sem("cT_made"), 1)

            def roots(name, banks, scale, done):
                for c in range(banks):
                    nm = f"{name}{c}" if banks > 1 else name
                    b = full(a, nm)
                    freed(a.activation(rbc[:, c, :], b[:, 0:NT], ACT.Sqrt, bias=eps[:, 0:1], scale=scale), nm)
                    a.wait_ge(bank_free[filled[nm][0]], frees_at(nm))
                    a.sem_inc(sem(done), 1)

            roots("ss1", 1, 1.0 / D, "root1")

            def proj_out(item):
                for n in range(2):
                    j = 2 * item + n
                    b = full(a, f"proj{j}")
                    freed(a.activation(proj[:, j, :], b[:, 0:NT], ACT.Copy), f"proj{j}")
                    a.wait_ge(bank_free[n], frees_at(f"proj{j}"))
                    a.sem_inc(sem("proj_out"), 1)

            def q_copy(q):
                b = full(a, f"qb{q}")
                if q >= 2:
                    a.wait_ge(sem("k_scored"), q - 1)
                freed(a.activation(qb[:, q % 2, :], b[:, :], ACT.Copy), f"qb{q}")
                a.wait_ge(bank_free[2], frees_at(f"qb{q}"))
                a.sem_inc(sem("qb"), 1)

            def take(name, dst, rows_, cols, done):
                b = full(a, name)
                freed(a.activation(dst, b[0:rows_, 0:cols], ACT.Copy), name)
                a.wait_ge(bank_free[filled[name][0]], frees_at(name))
                a.sem_inc(sem(done), 1)

            def att_exp(h):
                a.wait_ge(sem("masked"), h + 1)
                a.activation(sm[:, h % 2, 0:P], sm[:, h % 2, 0:P], ACT.Exp, bias=st4[:, h % 2, 2:3], scale=SCALE,
                             accum_out=st4[:, h % 2, 4:5])
                inc(a.activation(sm[:, h % 2, P:3 * P], sm[:, h % 2, P:3 * P], ACT.Exp, bias=st4[:, h % 2, 3:4],
                                 scale=SCALE, accum_out=st4[:, h % 2, 5:6]), "exped")

            def att_pT(h):
                if h == 2:
                    a.wait_ge(sem("att_even"), 1)
                elif h > 2:
                    if h % 2:
                        full(a, f"O{(h - 2) // 2}")
                    else:
                        a.wait_ge(sem("att_even"), h // 2)
                b = full(a, f"PT{h}")
                freed(a.activation(pT[:, h % 2, :], b[:, 0:3 * P], ACT.Copy), f"PT{h}")
                a.wait_ge(bank_free[h % 2], frees_at(f"PT{h}"))
                a.sem_inc(sem("probsT"), 1)

            def project(item):
                proj_out(item)
                if item == (QC0 + AC - 1) // 2:
                    inc(a.activation(mixT[:, 0:AC, :], proj[:, QC0:QC0 + AC, :], ACT.Square), "q_sq")
                if item == (KC0 + AC - 1) // 2:
                    inc(a.activation(mixT[:, AC:2 * AC, :], proj[:, KC0:KC0 + AC, :], ACT.Square), "k_sq")

            def head_root(name, row, scale, done):
                b = full(a, name)
                freed(a.activation(rbc[0:2 * AC, row, :], b[0:2 * AC, 0:NT], ACT.Sqrt, bias=eps[0:2 * AC, 0:1],
                                   scale=scale), name)
                a.wait_ge(bank_free[filled[name][0]], frees_at(name))
                a.sem_inc(sem(done), 1)

            def k_rows(_):
                for r in range(TT):
                    take(f"krow{r}", stg[:, r, :], P, AW, "k_rows")

            def v_rows(_):
                for r in range(TT):
                    take(f"vrow{r}", vnat[:, r, :], P, AW, "v_rows")

            def tails(_):
                a.wait_ge(sem("qdT"), 1)
                take("utail", utail[0:NBUF + NS, :], NBUF + NS, POOLW, "tails")
                for hlf in range(2):
                    take(f"ctail{hlf}", tail[0:NCV + NS, 384 * hlf:384 * hlf + 384], NCV + NS, 384, "tails")

            def conv_gates(_):
                a.wait_ge(sem("conv_done"), 1)
                a.activation(proj[:, Z0:Z0 + GC, :], proj[:, Z0:Z0 + GC, :], ACT.Silu).then_inc(sem("z_silu"), 1)
                step(a.activation(cv[:, :, :], cv[:, :, :], ACT.Silu))
                inc(a.activation(sq4, cv[:, 0:2 * GC, :], ACT.Square), "d_sq")

            def decays(_):
                a.wait_ge(sem("ab_in"), 1)
                a.activation(ab[:, 0, :], ab[:, 0, :], ACT.Exp)
                step(a.activation(ab[:, 4, :], ab[:, 4, :], ACT.Exp, scale=2.0))
                a.activation(gcol[:, 2:3], gcol[:, 0:1], ACT.Exp)
                inc(a.activation(ab[:, 4, :], ab[:, 4, :], ACT.Ln, bias=eps[0:GH, 1:2]), "ab_exp")
                a.wait_ge(sem("ab_g"), 1)
                inc(a.activation(ab[:, 2, :], ab[:, 1, :], ACT.Exp), "ab_done")

            def chunk_decays(_):
                a.wait_ge(sem("gs_in"), 1)
                a.activation(gs[:, 2, :], gs[:, 0, :], ACT.Exp)
                a.activation(gs[:, 3, :], gs[:, 3, :], ACT.Exp)
                inc(a.activation(gs[:, 4, :], gs[:, 1, :], ACT.Exp), "gs_exp")

            def decay_matrices(_):
                b = full(a, "gbc1")
                freed(a.activation(w_a, b[:, :], ACT.Exp), "gbc1")
                a.wait_ge(sem("decay_in"), 1)
                step(a.activation(DT[:, :, :, :], DT[:, :, :, :], ACT.Exp))
                a.sem_inc(sem("decay_exp"), 1)
                a.sem_inc(sem("ebc"), 1)

            def dn_first(_):
                for n in range(TT):
                    b = full(a, f"T0{n}")
                    freed(a.activation(Tn[:, n, :, :], b[:, :].rearrange("p (h i) -> p h i", h=GH), ACT.Copy), f"T0{n}")
                    a.wait_ge(bank_free[4 + n], frees_at(f"T0{n}"))
                    a.sem_inc(sem("Tn"), 1)

            def dn_inner(s):
                for n in range(TT):
                    b = full(a, f"P1{s}{n}")
                    freed(a.activation(P1[:, n, :, :], b[:, :].rearrange("p (h i) -> p h i", h=GH), ACT.Copy), f"P1{s}{n}")
                    a.wait_ge(bank_free[4 + n], frees_at(f"P1{s}{n}"))
                    a.sem_inc(sem("P1"), 1)

            def dn_values(_):
                b = full(a, "kc")
                freed(a.activation(kcT[:, :, :], b[:, 0:GC * P].rearrange("p (c i) -> p c i", c=GC), ACT.Copy), "kc")
                a.wait_ge(bank_free[4], frees_at("kc"))
                a.sem_inc(sem("kcT"), 1)

            def out_squares(_):
                a.wait_ge(sem("o_done"), 1)
                inc(a.activation(sq4[:, 0:GC, :], pdT[:, :, :], ACT.Square), "o_sq")

            def out_roots(_):
                a.wait_ge(sem("k_done"), 1)
                for c in range(GC):
                    b = full(a, f"oss{c}")
                    freed(a.activation(rbc[:, c, :], b[:, 0:NT], ACT.Sqrt, bias=eps[:, 0:1], scale=1.0 / DV), f"oss{c}")
                    a.wait_ge(bank_free[6 + c], frees_at(f"oss{c}"))
                    a.sem_inc(sem("rooto"), 1)

            def page_exps(_):
                a.wait_ge(sem("shifted"), 1)
                a.activation(sm64[:, 3, :, :], sm64[:, 3, :, :], ACT.Exp, scale=SCALE)
                inc(a.activation(w_b, w_b, ACT.Exp, scale=SCALE), "exp8")

            def mix_high(_):
                a.wait_ge(sem("p_ready"), 1)
                inc(a.activation(a_hi[:, :, 0:T], mixT[:, :, 0:T], ACT.Copy), "mix_hi")

            def att_head(h):
                if h + 1 < H:
                    att_exp(h + 1)
                att_pT(h)

            go = {
                "W": project, "QSUM": lambda _: head_root("qss", 0, 1.0 / HD, "rootq"),
                "KSUM": lambda _: head_root("kss", 1, 1.0 / HD, "rootk"), "DSUM": lambda _: head_root("dss", 2, 1.0, "rootd"),
                "QB": q_copy, "KROW": k_rows, "VROW": v_rows, "TAILS": tails, "CONV": conv_gates, "AB": decays,
                "GC": chunk_decays, "GBC": decay_matrices, "TI": dn_first, "L": dn_inner, "UA": dn_values,
                "XC": out_squares, "XD": out_roots, "S": lambda _: att_exp(0), "H": att_head, "A": ada_rows,
                "DMAX": page_exps, "MX": mix_high,
            }
            for st, n in ORDER:
                if st in go:
                    go[st](n)

            def w_high(n):
                item = split[n]
                c = width(item)
                if n >= PARTS:
                    a.wait_ge(*part_free[split[n - PARTS]])
                inc(a.activation(w_hi[:, n % PARTS, 0:c], arrived(a, item)[:, 0:c], ACT.Copy), "w_high")

            a.wait_ge(sem("mix"), 1)
            inc(a.activation(a_hi[:, :, T:NT], mixT[:, :, T:NT], ACT.Copy), "mix_hi")
            for n in range(D // IW + 2):
                w_high(n)
            a.wait_ge(sem("x1"), DC)
            inc(a.activation(hT[:, :, :], xT[:, :, :], ACT.Square), "sq2")
            roots("ss2", 1, 1.0 / D, "root2")
            a.wait_ge(sem("h2"), 1)
            inc(a.activation(a_hi[:, :, :], hT[:, :, :], ACT.Copy), "h2_hi")
            for n in range(D // IW + 2, len(split) + 2):
                if n < len(split):
                    w_high(n)
                kind, i = split[n - 2]
                if kind == "gate":
                    for f in (2 * i, 2 * i + 1):
                        b = full(a, f"gate{f}")
                        if f >= 4:
                            a.wait_ge(sem("hidden"), f - 3)
                        freed(a.activation(rbc[:, f % 4, :], b[:, 0:NT], ACT.Silu), f"gate{f}")
                        a.wait_ge(bank_free[filled[f"gate{f}"][0]], frees_at(f"gate{f}"))
                        a.sem_inc(sem("silu"), 1)

        @block.gpsimd
        def _(g):
            step = order(g, "pool_step")

            def zeros(ap):
                step(g.memset(ap, 0.0))

            def diagonal(ap, base, pattern):
                return g.affine_select(out=ap, in_=ap, compare_op=ALU.not_equal, fill=1.0, base=base, pattern=pattern,
                                       channel_multiplier=1)

            zeros(ident[:, :])
            step(diagonal(ident[:, :], 0, [[-1, P]]))
            g.sem_inc(sem("ident_made"), 1)
            step(g.memset(ones[:, :], 1.0))
            step(g.memset(blk[:, :], 0.0))
            step(g.memset(selc[:, :, :], 0.0))
            step(g.memset(dm8[:, :], 0.0))
            step(g.memset(i64[:, :], 0.0))
            step(g.memset(sel8[:, :, :], 0.0))
            step(g.memset(headsum[:, :, :], 0.0))
            step(g.memset(triu[:, :], 1.0))
            step(g.memset(cmask[:, :, :], 0.0))
            zeros(lvl[:, :, :])
            step(g.memset(blk[0:64, 0:64], 1.0))
            step(g.memset(blk[64:P, 64:P], 1.0))
            step(diagonal(i64[:, :], 0, [[-1, HD]]))
            for q in range(4):
                step(diagonal(dm8[:, :], -32 * q, [[-1, H]]))
            step(diagonal(i64[:, :], -64, [[-1, HD]]))
            step(g.affine_select(out=selc[:, :, :], in_=selc[:, :, :], compare_op=ALU.not_equal, fill=1.0, base=0,
                                 pattern=[[1, NS], [-1, 32]], channel_multiplier=0))
            step(g.affine_select(out=sel8[:, :, :].rearrange("p c (w d) -> p c w d", w=2),
                                 in_=sel8[:, :, :].rearrange("p c (w d) -> p c w d", w=2), compare_op=ALU.not_equal,
                                 fill=1.0, base=0, pattern=[[-2, AC], [-1, 2], [0, HD]], channel_multiplier=1))
            for c in range(AC):
                for h2 in range(2):
                    step(g.memset(headsum[64 * h2:64 * h2 + 64, c, 2 * c + h2:2 * c + h2 + 1], 1.0))
            step(g.affine_select(out=triu[:, :], in_=triu[:, :], compare_op=ALU.is_ge, fill=0.0, base=0,
                                 pattern=[[1, P]], channel_multiplier=-1))
            for n in (0, 2):
                step(g.affine_select(out=cmask[:, n, :], in_=cmask[:, n, :], compare_op=ALU.is_ge, fill=-FAR, base=0,
                                     pattern=[[-1, P]], channel_multiplier=1))
            for s in range(7):
                w = 1 << s
                part = lvl[:, s, :].rearrange("p (a b c) -> p a b c", b=2, c=w)[:, :, 1, :]
                step(g.memset(part, 1.0))
                step(g.affine_select(out=part, in_=part, compare_op=ALU.is_ge, fill=0.0, base=0,
                                     pattern=[[-2 * w, P // (2 * w)], [0, w]], channel_multiplier=1))
                step(g.affine_select(out=part, in_=part, compare_op=ALU.is_ge, fill=0.0, base=w - 1,
                                     pattern=[[2 * w, P // (2 * w)], [0, w]], channel_multiplier=-1))
            g.sem_inc(sem("masks_made"), 1)
            cnt_i = prod[:, 0:T].bitcast(I32)
            step(g.iota(cnt_i, pattern=[[1, T]], base=1, channel_multiplier=0))
            for c in range(PCH):
                step(g.tensor_copy(rcnt[:, c, :], cnt_i))
            g.sem_inc(sem("iota_made"), 1)

            outs = [0]

            def store(dst, src):
                outs[0] += 1
                g.dma_start(dst, src).then_inc(sem("stored"), 16)

            g.dma_start(pool_sample[0, :, 0:NBUF - 1, :], state_pool[0, :, 1:NBUF, :]).then_inc(sem("stored"), 16)
            g.dma_start(conv_sample[0, :, 0:NCV - 1, :], state_conv[0, :, 1:NCV, :]).then_inc(sem("stored"), 16)
            outs[0] += 2
            g.wait_ge(sem("ebc"), 1)
            g.wait_ge(sem("qk_d"), 1)
            ebc = w_a
            for h in range(GH):
                c, r = h // 2, slice(64 * (h % 2), 64 * (h % 2) + 64)
                step(g.tensor_tensor(qdT[r, c, :], cv[r, c, P:T], ebc[r, h * P:(h + 1) * P], ALU.mult))
            g.sem_inc(sem("qdT"), 1)
            g.wait_ge(sem("k_rows"), 2)
            for r in range(TT):
                g.dma_start(k_prompt[0, 0, r * P:(r + 1) * P].rearrange("t h d -> t (h d)"), stg[:, r, :])\
                 .then_inc(sem("krow_out"), 16)
            g.wait_ge(sem("v_rows"), 2)
            for r in range(TT):
                store(v_prompt[0, 0, r * P:(r + 1) * P].rearrange("t h d -> t (h d)"), vnat[:, r, :])
            g.wait_ge(sem("k_rows8"), 1)
            g.wait_ge(sem("v_rows8"), 1)
            store(k_sample[0, :, 0].rearrange("q h d -> q (h d)"), nat8[:, 1, :])
            store(v_sample[0, :, 0].rearrange("q h d -> q (h d)"), nat8[:, 2, :])
            g.wait_ge(sem("proj_out"), out_count(PCH - 1))
            g.wait_ge(sem("rcnt_made"), 1)
            g.wait_ge(sem("cT_made"), 1)

            def add_back(dst, src, d):
                step(g.tensor_copy(dst[:, 0:d], src[:, 0:d]))
                step(g.tensor_tensor(dst[:, d:T], src[:, d:T], src[:, 0:T - d], ALU.add))

            for c in range(PCH):
                src, at = proj[:, c, 0:T], 0
                w = 1
                while w < WINDOWS[2 * c + 1]:
                    dst = (pw1, pw2)[at % 2]
                    add_back(dst, src, w)
                    w *= 2
                    at += 1
                    src = dst
                    for gg in range(2):
                        if WINDOWS[2 * c + gg] == w:
                            r = slice(64 * gg, 64 * gg + 64)
                            step(g.tensor_tensor(pdT[r, c, 0:T], src[r, :], rcnt[r, c, :], ALU.mult))
                            step(g.tensor_tensor(pdT[r, c, 0:T], pdT[r, c, 0:T], proj[r, c, 0:T], ALU.subtract))
            g.sem_inc(sem("pool_prompt_done"), 1)
            g.wait_ge(sem("tails"), 3)
            for dst, src in ((pool_prompt[0, 0], utail[0:NBUF, :]), (pool_sample[0, :, NBUF - 1, :], utail[NBUF:NBUF + NS, :]),
                             (conv_prompt[0, 0], tail[0:NCV, :]), (conv_sample[0, :, NCV - 1, :], tail[NCV:NCV + NS, :])):
                g.dma_start(dst, src).then_inc(sem("tails_out"), 16)
            g.wait_ge(sem("S2_done"), 1)
            for c in range(GC):
                store(delta_prompt[0, 0].rearrange("(c w) k n -> c (w k) n", w=2)[c], S2[:, c, :])
            g.wait_ge(sem("Snew"), 1)
            for c in range(GC):
                for w in range(2):
                    g.dma_start(delta_sample[0, :, 2 * c + w].rearrange("q k n -> k q n"),
                                Ss[64 * w:64 * w + 64, :, c, :]).then_inc(sem("states_out"), 16)
            for r in range(TT + 1):
                g.wait_ge(sem("y_rows"), r + 1)
                if r < TT:
                    store(y_prompt[0, r * P:(r + 1) * P, :], ynat[:, r, :])
                else:
                    store(y_sample[:, 0, :], ynat[0:NS, TT, :])
            g.wait_ge(sem("stored"), 16 * outs[0])
            g.wait_ge(sem("krow_out"), 32)
            g.wait_ge(sem("tails_out"), 64)
            g.wait_ge(sem("states_out"), 64)

        @block.sync
        def _(sp):
            sp.dma_start(c_nat[0:1, :], c_prompt).then_inc(sem("c_in"), 16)
            sp.dma_start(c_nat[1:NC, :], c_sample).then_inc(sem("c_in"), 16)
            for r, src, m in ((R_ADAB, ada_b, 6 * DC), (R_N1, norm1_w, DC), (R_N2, norm2_w, DC), (R_PS, pool_scale, PCH)):
                sp.dma_start(rows[r:r + m, :], src.rearrange("o (m p) -> (o m) p", p=P)).then_inc(sem("rows_in"), 16)
            sp.dma_start(rows[R_CW:R_Q, :], conv_w[0].rearrange("i (c p) -> (i c) p", p=P)).then_inc(sem("rows_in"), 16)
            for n, src in enumerate((q_norm_w, k_norm_w, dn_norm_w)):
                for w in range(2):
                    sp.dma_start(rows[R_Q + n:R_Q + n + 1, 64 * w:64 * w + 64], src).then_inc(sem("rows_in"), 16)
            sp.dma_start(table[:, :], page_table.rearrange("q n -> (q n)").unsqueeze(0)).then_inc(sem("table_in"), 16)
            cols = {"ada": ada_w, "win": w_in, "wout": w_out, "gate": w_gate, "up": w_up}
            held = [None] * RING
            loaded = False
            for it in stream:
                kind, i = it
                s = place[it][0]
                if held[s] is not None:
                    sp.wait_ge(*released[held[s]])
                held[s] = it
                dst = ring[:, s, :]
                if kind in cols:
                    sp.dma_start(dst.rearrange("p (k n) -> p k n", k=DC),
                                 cols[kind][0].rearrange("(k p) n -> p k n", p=P)[:, :, i * IW:(i + 1) * IW])\
                      .then_inc(slot_full[s], 16)
                elif kind == "down":
                    k0, k1 = DKT[i[1]]
                    sp.dma_start(dst[:, 0:(k1 - k0) * IW].rearrange("p (k n) -> p k n", n=IW),
                                 w_down[0, k0 * P:k1 * P].rearrange("(k p) n -> p k n", p=P)[:, :, i[0] * IW:(i[0] + 1) * IW])\
                      .then_inc(slot_full[s], 16)
                else:
                    if not loaded:
                        sp.wait_ge(sem("table_in"), 16)
                        loaded = True
                    cache = cache_k if kind == "k" else cache_v
                    for k in range(PGI):
                        at = i[0] * NPG + i[1] * PGI + k
                        page = sp.value_load(table[0:1, at:at + 1], min_val=0, max_val=NPHYS - 1)
                        sp.dma_start(dst[:, k * AW:(k + 1) * AW],
                                     cache[0, bass.ds(page, 1)].rearrange("o t h d -> (o t) (h d)"))\
                          .then_inc(slot_full[s], 16)
                if it == ("win", 6):
                    sp.wait_ge(sem("sq1"), 1)
                    for c in range(GC):
                        for w in range(2):
                            sp.dma_start(Ss[64 * w:64 * w + 64, :, c, :],
                                         state_delta[0, :, 2 * c + w].rearrange("q k n -> k q n")).then_inc(sem("S_in"), 16)


_INS = ['x_prompt', 'x_sample', 'cache_k', 'cache_v', 'state_pool', 'state_conv', 'state_delta', 'page_table',
        'c_prompt', 'c_sample', 'norm1_w', 'ada_w', 'ada_b', 'w_in', 'pool_w', 'pool_scale', 'q_norm_w', 'k_norm_w',
        'conv_w', 'a_log', 'dt_bias', 'dn_norm_w', 'w_out', 'norm2_w', 'w_gate', 'w_up', 'w_down']


def kernel(**inputs):
    import numpy as _np
    import concourse.bacc as _bacc
    from concourse import mybir as _mybir
    from concourse.bass_utils import run_bass_kernel_spmd as _run

    xp, xs, ck = inputs["x_prompt"].shape, inputs["x_sample"].shape, inputs["cache_k"].shape
    sp, sc, sd = (inputs[n].shape for n in ("state_pool", "state_conv", "state_delta"))
    outs = [xp, xs, (1, xp[0], xp[1], *ck[3:]), (1, xp[0], xp[1], *ck[3:]), (1, xs[0], xs[1], *ck[3:]),
            (1, xs[0], xs[1], *ck[3:]), (1, xp[0], *sp[2:]), sp, (1, xp[0], *sc[2:]), sc, (1, xp[0], *sd[2:]), sd]
    nc = _bacc.Bacc("TRN2", target_bir_lowering=False, num_devices=1)
    arrays, args = {}, []
    for name in _INS:
        a = _np.ascontiguousarray(inputs[name])
        arrays[f"in_{name}_dram"] = a
        args.append(nc.dram_tensor(f"in_{name}_dram", a.shape, _mybir.dt.from_np(a.dtype), kind="ExternalInput").ap())
    for i, shape in enumerate(outs):
        args.append(nc.dram_tensor(f"out_{i}_dram", shape, _mybir.dt.float32, kind="ExternalOutput").ap())
    build(nc, *args)
    r = _run(nc, [arrays], core_ids=[0])
    return tuple(r.results[0][f"out_{i}_dram"] for i in range(len(outs)))
```
